# Optimizing a Trainium2 kernel written in Bass

```python
import math
import jax, jax.numpy as jnp
from jax import lax
import numpy as np

D_MODEL = 1024
BATCH = 1
SEQ = 256
DEPTH = 4

GRID_W = 64
ROPE_THETA = 10000.0
N_MIXERS = 3
EPS = 1e-6

SSM_EXPAND = 2
SSM_D_INNER = SSM_EXPAND * D_MODEL
SSM_HEAD_DIM = 64
SSM_HEADS = SSM_D_INNER // SSM_HEAD_DIM
SSM_GROUPS = 8
SSM_STATE = 128
SSM_CONV = 5
SSM_CHUNK = 128
SSM_CONV_DIM = SSM_D_INNER + 2 * SSM_GROUPS * SSM_STATE
SSM_IN_DIM = SSM_D_INNER + SSM_CONV_DIM + 2 * SSM_HEADS

ATT_HEAD_DIM = 128
ATT_Q_HEADS = D_MODEL // ATT_HEAD_DIM
ATT_KV_HEADS = 2
ATT_BLOCK = 128
ATT_IN_DIM = (ATT_Q_HEADS + 2 * ATT_KV_HEADS) * ATT_HEAD_DIM

RET_HEADS = 4
RET_QK_DIM = D_MODEL // RET_HEADS
RET_V_DIM = 2 * RET_QK_DIM
RET_CHUNK = 128
RET_IN_DIM = 2 * D_MODEL + 2 * (2 * D_MODEL)

D_FF = 4 * D_MODEL

N_A = (DEPTH + 2) // 3
N_B = (DEPTH + 1) // 3
N_C = DEPTH // 3

kernel_name = "hybrid_ssd_gqa_retention_encoder"

def rmsnorm(x, w):
    xf = x.astype(jnp.float32)
    y = xf * lax.rsqrt(jnp.mean(xf * xf, axis=-1, keepdims=True) + EPS)
    return (y * w.astype(jnp.float32)).astype(x.dtype)

def rmsnorm_plain(x):
    xf = x.astype(jnp.float32)
    return (xf * lax.rsqrt(jnp.mean(xf * xf, axis=-1, keepdims=True) + EPS)).astype(x.dtype)

def flip_seq(t):
    return jnp.flip(t, axis=1)

def axial_rope_tables(S, dim):
    rows = S // GRID_W
    row = jnp.repeat(jnp.arange(rows, dtype=jnp.float32), GRID_W)
    col = jnp.tile(jnp.arange(GRID_W, dtype=jnp.float32), rows)
    half = dim // 2
    nf = half // 2
    inv = ROPE_THETA ** (-(jnp.arange(nf, dtype=jnp.float32) * 2.0) / half)
    ang = jnp.stack([row[:, None] * inv, col[:, None] * inv], axis=1)
    return jnp.cos(ang), jnp.sin(ang)

def apply_axial_rope(x, cos, sin):
    b, S, H, dim = x.shape
    nf = dim // 4
    xr = x.astype(jnp.float32).reshape(b, S, H, 2, 2, nf)
    x1 = xr[..., 0, :]
    x2 = xr[..., 1, :]
    c = cos[:, None]
    s = sin[:, None]
    out = jnp.stack([x1 * c - x2 * s, x2 * c + x1 * s], axis=-2)
    return out.reshape(b, S, H, dim).astype(x.dtype)

def depthwise_conv_centred(x, w, bias):
    pad = w.shape[0] // 2
    y = lax.conv_general_dilated(
        x, w[:, None, :].astype(x.dtype), window_strides=(1,), padding=[(pad, pad)],
        dimension_numbers=("NWC", "WIO", "NWC"), feature_group_count=x.shape[-1])
    return y + bias.astype(x.dtype)

def ssd_scan(x, dt, A, Bm, Cm, strict):
    b, S, H, P = x.shape
    G, N = Bm.shape[2], Bm.shape[3]
    hpg = H // G
    L = SSM_CHUNK
    c = S // L
    xc = x.astype(jnp.float32).reshape(b, c, L, G, hpg, P)
    dtc = dt.reshape(b, c, L, G, hpg)
    Bc = Bm.astype(jnp.float32).reshape(b, c, L, G, N)
    Cc = Cm.astype(jnp.float32).reshape(b, c, L, G, N)
    acum = jnp.cumsum(dtc * A.reshape(G, hpg), axis=2)
    mask = jnp.tril(jnp.ones((L, L), dtype=bool), k=-1 if strict else 0)[:, :, None, None]
    seg = acum[:, :, :, None] - acum[:, :, None, :]
    decay = jnp.where(mask, jnp.exp(jnp.where(mask, seg, 0.0)), 0.0)
    cb = jnp.einsum("bclgn,bcsgn->bclsg", Cc, Bc)
    w = cb[..., None] * decay * dtc[:, :, None]
    y_diag = jnp.einsum("bclsgh,bcsghp->bclghp", w, xc)
    decay_to_end = jnp.exp(acum[:, :, -1:] - acum)
    states = jnp.einsum("bclgn,bclgh,bclghp->bcghpn", Bc, decay_to_end * dtc, xc)
    chunk_decay = jnp.exp(acum[:, :, -1])

    def step(h, inp):
        st, dec = inp
        return h * dec[..., None, None] + st, h

    h0 = jnp.zeros((b, G, hpg, P, N), jnp.float32)
    _, prev = lax.scan(step, h0, (jnp.swapaxes(states, 0, 1), jnp.swapaxes(chunk_decay, 0, 1)))
    prev = jnp.swapaxes(prev, 0, 1)
    y_off = jnp.einsum("bclgn,bcghpn,bclgh->bclghp", Cc, prev, jnp.exp(acum))
    return (y_diag + y_off).reshape(b, S, H, P).astype(x.dtype)

def mamba2_mixer(h, w_in, conv_w, conv_b, dt_bias, a_log, d_skip, norm_w, w_out):
    b, S, _ = h.shape
    proj = h @ w_in
    z = proj[..., :SSM_D_INNER]
    xbc = proj[..., SSM_D_INNER:SSM_D_INNER + SSM_CONV_DIM]
    dt_raw = proj[..., SSM_D_INNER + SSM_CONV_DIM:]
    xbc = jax.nn.silu(depthwise_conv_centred(xbc, conv_w, conv_b))
    gn = SSM_GROUPS * SSM_STATE
    xs = xbc[..., :SSM_D_INNER].reshape(b, S, SSM_HEADS, SSM_HEAD_DIM)
    Bm = xbc[..., SSM_D_INNER:SSM_D_INNER + gn].reshape(b, S, SSM_GROUPS, SSM_STATE)
    Cm = xbc[..., SSM_D_INNER + gn:].reshape(b, S, SSM_GROUPS, SSM_STATE)
    dt = jax.nn.softplus(dt_raw.astype(jnp.float32).reshape(b, S, 2, SSM_HEADS)
                         + dt_bias.astype(jnp.float32))
    A = -jnp.exp(a_log.astype(jnp.float32))
    y_f = ssd_scan(xs, dt[:, :, 0], A[0], Bm, Cm, strict=False)
    y_b = flip_seq(ssd_scan(flip_seq(xs), flip_seq(dt[:, :, 1]), A[1],
                            flip_seq(Bm), flip_seq(Cm), strict=True))
    y = y_f + y_b + xs * d_skip[:, None].astype(xs.dtype)
    y = y.reshape(b, S, SSM_D_INNER)
    y = rmsnorm(y * jax.nn.silu(z), norm_w)
    return y @ w_out

def gqa_axial_mixer(h, w_in, q_norm, k_norm, w_out, cos, sin):
    b, S, _ = h.shape
    nq = ATT_Q_HEADS * ATT_HEAD_DIM
    nk = ATT_KV_HEADS * ATT_HEAD_DIM
    proj = h @ w_in
    q = proj[..., :nq].reshape(b, S, ATT_Q_HEADS, ATT_HEAD_DIM)
    k = proj[..., nq:nq + nk].reshape(b, S, ATT_KV_HEADS, ATT_HEAD_DIM)
    v = proj[..., nq + nk:].reshape(b, S, ATT_KV_HEADS, ATT_HEAD_DIM)
    q = apply_axial_rope(rmsnorm(q, q_norm), cos, sin)
    k = apply_axial_rope(rmsnorm(k, k_norm), cos, sin)
    rep = ATT_Q_HEADS // ATT_KV_HEADS
    nblk = S // ATT_BLOCK
    qb = q.reshape(b, nblk, ATT_BLOCK, ATT_KV_HEADS, rep, ATT_HEAD_DIM).transpose(1, 0, 2, 3, 4, 5)
    scale = ATT_HEAD_DIM ** -0.5

    def block(q_blk):
        s = jnp.einsum("bqkrd,bskd->bkrqs", q_blk, k).astype(jnp.float32) * scale
        p = jax.nn.softmax(s, axis=-1)
        return jnp.einsum("bkrqs,bskd->bqkrd", p.astype(v.dtype), v)

    o = lax.map(block, qb)
    o = o.transpose(1, 0, 2, 3, 4, 5).reshape(b, S, nq)
    return o @ w_out

def retention_scan(q, k, v, log_gamma, strict):
    b, S, H, dk = q.shape
    dv = v.shape[-1]
    L = RET_CHUNK
    c = S // L
    qc = q.astype(jnp.float32).reshape(b, c, L, H, dk)
    kc = k.astype(jnp.float32).reshape(b, c, L, H, dk)
    vc = v.astype(jnp.float32).reshape(b, c, L, H, dv)
    pos = jnp.arange(L, dtype=jnp.float32)
    mask = jnp.tril(jnp.ones((L, L), dtype=bool), k=-1 if strict else 0)[..., None]
    diff = (pos[:, None] - pos[None, :])[..., None] * log_gamma
    dmat = jnp.where(mask, jnp.exp(jnp.where(mask, diff, 0.0)), 0.0)
    scores = jnp.einsum("bclhd,bcshd->bclsh", qc, kc) * dmat
    y_in = jnp.einsum("bclsh,bcshe->bclhe", scores, vc)
    k_dec = jnp.exp((L - 1 - pos)[:, None] * log_gamma)
    states = jnp.einsum("bclhd,lh,bclhe->bchde", kc, k_dec, vc)
    chunk_dec = jnp.exp(L * log_gamma)

    def step(r, st):
        return r * chunk_dec[:, None, None] + st, r

    r0 = jnp.zeros((b, H, dk, dv), jnp.float32)
    _, prev = lax.scan(step, r0, jnp.swapaxes(states, 0, 1))
    prev = jnp.swapaxes(prev, 0, 1)
    q_dec = jnp.exp((pos + 1)[:, None] * log_gamma)
    y_cross = jnp.einsum("bclhd,bchde,lh->bclhe", qc, prev, q_dec)
    return (y_in + y_cross).reshape(b, S, H, dv).astype(v.dtype)

def retention_mixer(h, w_in, log2_decay, w_out, cos, sin):
    b, S, _ = h.shape
    proj = h @ w_in
    q = proj[..., :D_MODEL].reshape(b, S, RET_HEADS, RET_QK_DIM)
    k = proj[..., D_MODEL:2 * D_MODEL].reshape(b, S, RET_HEADS, RET_QK_DIM)
    v = proj[..., 2 * D_MODEL:4 * D_MODEL].reshape(b, S, RET_HEADS, RET_V_DIM)
    g = proj[..., 4 * D_MODEL:]
    q = apply_axial_rope(q, cos, sin)
    k = apply_axial_rope(k, cos, sin) * (RET_QK_DIM ** -0.5)
    log_gamma = jnp.log1p(-jnp.exp2(log2_decay.astype(jnp.float32)))
    y_f = retention_scan(q, k, v, log_gamma[0], strict=False)
    y_b = flip_seq(retention_scan(flip_seq(q), flip_seq(k), flip_seq(v), log_gamma[1], strict=True))
    y = rmsnorm_plain(y_f + y_b).reshape(b, S, 2 * D_MODEL)
    return (jax.nn.silu(g) * y) @ w_out

def sqrelu_mlp(h, w1, w2):
    a = jax.nn.relu(h @ w1)
    return (a * a) @ w2

def setup_inputs(seed: int = 0) -> dict:
    key = jax.random.key(seed)
    ks = iter(jax.random.split(key, 32))
    f32 = jnp.float32

    def nrm(shape, scale):
        return jax.random.normal(next(ks), shape, f32) * scale

    def gain(shape):
        return 1.0 + 0.05 * jax.random.normal(next(ks), shape, f32)

    x = jax.random.normal(next(ks), (BATCH, SEQ, D_MODEL), f32)
    norm_mix_pre = gain((DEPTH, D_MODEL))
    norm_mix_post = gain((DEPTH, D_MODEL))
    norm_ffn_pre = gain((DEPTH, D_MODEL))
    norm_ffn_post = gain((DEPTH, D_MODEL))
    mlp_w_in = nrm((DEPTH, D_MODEL, D_FF), D_MODEL ** -0.5)
    mlp_w_out = nrm((DEPTH, D_FF, D_MODEL), D_FF ** -0.5)
    ssm_w_in = nrm((N_A, D_MODEL, SSM_IN_DIM), D_MODEL ** -0.5)
    ssm_conv_w = nrm((N_A, SSM_CONV, SSM_CONV_DIM), SSM_CONV ** -0.5)
    ssm_conv_b = nrm((N_A, SSM_CONV_DIM), 0.02)
    dt0 = jnp.exp(jax.random.uniform(next(ks), (N_A, 2, SSM_HEADS), f32,
                                     math.log(1e-3), math.log(1e-1)))
    ssm_dt_bias = dt0 + jnp.log(-jnp.expm1(-dt0))
    ssm_a_log = jnp.log(jax.random.uniform(next(ks), (N_A, 2, SSM_HEADS), f32, 1.0, 16.0))
    ssm_d = gain((N_A, SSM_HEADS))
    ssm_norm = gain((N_A, SSM_D_INNER))
    ssm_w_out = nrm((N_A, SSM_D_INNER, D_MODEL), SSM_D_INNER ** -0.5)
    att_w_in = nrm((N_B, D_MODEL, ATT_IN_DIM), D_MODEL ** -0.5)
    att_q_norm = gain((N_B, ATT_HEAD_DIM))
    att_k_norm = gain((N_B, ATT_HEAD_DIM))
    att_w_out = nrm((N_B, ATT_Q_HEADS * ATT_HEAD_DIM, D_MODEL), (ATT_Q_HEADS * ATT_HEAD_DIM) ** -0.5)
    ret_w_in = nrm((N_C, D_MODEL, RET_IN_DIM), D_MODEL ** -0.5)
    ret_log2_decay = (-5.0 - jnp.arange(RET_HEADS, dtype=f32))[None, None, :] \
        + 0.1 * jax.random.normal(next(ks), (N_C, 2, RET_HEADS), f32)
    ret_w_out = nrm((N_C, 2 * D_MODEL, D_MODEL), (2 * D_MODEL) ** -0.5)
    return {
        "x": x,
        "norm_mix_pre": norm_mix_pre, "norm_mix_post": norm_mix_post,
        "norm_ffn_pre": norm_ffn_pre, "norm_ffn_post": norm_ffn_post,
        "mlp_w_in": mlp_w_in, "mlp_w_out": mlp_w_out,
        "ssm_w_in": ssm_w_in, "ssm_conv_w": ssm_conv_w, "ssm_conv_b": ssm_conv_b,
        "ssm_dt_bias": ssm_dt_bias, "ssm_a_log": ssm_a_log, "ssm_d": ssm_d,
        "ssm_norm": ssm_norm, "ssm_w_out": ssm_w_out,
        "att_w_in": att_w_in, "att_q_norm": att_q_norm, "att_k_norm": att_k_norm,
        "att_w_out": att_w_out,
        "ret_w_in": ret_w_in, "ret_log2_decay": ret_log2_decay, "ret_w_out": ret_w_out,
    }

def reference(x, norm_mix_pre, norm_mix_post, norm_ffn_pre, norm_ffn_post, mlp_w_in, mlp_w_out,
              ssm_w_in, ssm_conv_w, ssm_conv_b, ssm_dt_bias, ssm_a_log, ssm_d, ssm_norm, ssm_w_out,
              att_w_in, att_q_norm, att_k_norm, att_w_out,
              ret_w_in, ret_log2_decay, ret_w_out):
    S = x.shape[1]
    cos_att, sin_att = axial_rope_tables(S, ATT_HEAD_DIM)
    cos_ret, sin_ret = axial_rope_tables(S, RET_QK_DIM)
    for i in range(DEPTH):
        kind = i % N_MIXERS
        j = i // N_MIXERS
        hn = rmsnorm(x, norm_mix_pre[i])
        if kind == 0:
            m = mamba2_mixer(hn, ssm_w_in[j], ssm_conv_w[j], ssm_conv_b[j], ssm_dt_bias[j],
                             ssm_a_log[j], ssm_d[j], ssm_norm[j], ssm_w_out[j])
        elif kind == 1:
            m = gqa_axial_mixer(hn, att_w_in[j], att_q_norm[j], att_k_norm[j], att_w_out[j],
                                cos_att, sin_att)
        else:
            m = retention_mixer(hn, ret_w_in[j], ret_log2_decay[j], ret_w_out[j], cos_ret, sin_ret)
        x = x + rmsnorm(m, norm_mix_post[i]).astype(x.dtype)
        hn = rmsnorm(x, norm_ffn_pre[i])
        x = x + rmsnorm(sqrelu_mlp(hn, mlp_w_in[i], mlp_w_out[i]), norm_ffn_post[i]).astype(x.dtype)
    return x


_drawn_inputs = setup_inputs


def setup_inputs(seed=0):
    import zlib

    import numpy as np

    out = dict(_drawn_inputs(seed))
    spreads = {}
    factors = {'att_q_norm': 4.348, 'att_k_norm': 4.369}
    for name, (base, spread) in spreads.items():
        noise = np.random.default_rng([zlib.crc32(name.encode()), seed]).standard_normal(out[name].shape)
        drawn = base * np.exp(spread * noise) if base else spread * noise
        out[name] = __import__('jax').numpy.asarray(drawn.astype(out[name].dtype))
    for name, factor in factors.items():
        out[name] = (out[name] * factor).astype(out[name].dtype)
    return out
```

```python
from contextlib import ExitStack

import numpy as np

import concourse.bass as bass
from concourse import mybir

ALU = mybir.AluOpType
ACT = mybir.ActivationFunctionType
AX = mybir.AxisListType
F32 = mybir.dt.float32
F32R = mybir.dt.float32r
I32 = mybir.dt.int32

P = 128
D_MODEL, SEQ, DEPTH = 1024, 256, 4
TT = SEQ // P
KD = D_MODEL // P
EPS = 1e-6
D_FF = 4 * D_MODEL
SSM_INNER, SSM_HEADS, SSM_HDIM, SSM_GROUPS, SSM_STATE, SSM_CONV = 2048, 32, 64, 8, 128, 5
HPG = SSM_HEADS // SSM_GROUPS
CONV_DIM = SSM_INNER + 2 * SSM_GROUPS * SSM_STATE
CT_N = CONV_DIM // P
PAD = SSM_CONV // 2
AQ, AKV, AD = 8, 2, 128
RH, RQK, RV = 4, 256, 512
GRID_W, ROPE_THETA = 64, 10000.0
SSM_LAYERS = [l for l in range(DEPTH) if l % 3 == 0]

UNIT = 2048
HALF = UNIT // 2
XBC_UNITS = CONV_DIM // 256
Z_UNITS = 2 * SSM_INNER // 512
SSM_OUT_UNITS = SSM_INNER // 256
ATT_GROUPS = (AQ + 2 * AKV) * AD // 512
ATT_OUT_UNITS = AQ * AD // 256
RET_GROUPS = 6 * D_MODEL // 512
RET_OUT_UNITS = 2 * D_MODEL // 256
MLP_STEPS = D_FF // 256
MLP_UNITS = 2 * MLP_STEPS
MIX_UNITS = {0: XBC_UNITS + Z_UNITS + SSM_OUT_UNITS, 1: 2 * ATT_GROUPS + ATT_OUT_UNITS,
             2: 2 * RET_GROUPS + RET_OUT_UNITS}
FIRST_UNIT = []
_n = 0
for _l in range(DEPTH):
    FIRST_UNIT += [_n, _n + MIX_UNITS[_l % 3]]
    _n += MIX_UNITS[_l % 3] + MLP_UNITS
N_UNITS = _n

C_ID, C_LE, C_GT, C_GE, C_LT = (P * i for i in range(5))
N_CONST = 5 * P
T_COSA, T_SINA = 0, 256
N_TABA = 512
T_COSR, T_SINR, T_AHEAD, T_BEHIND = 0, 512, 1024, 1536
N_TABR = 2048


def rope_tables(dim):
    rows = SEQ // GRID_W
    row = np.repeat(np.arange(rows, dtype=np.float32), GRID_W)
    col = np.tile(np.arange(GRID_W, dtype=np.float32), rows)
    half = dim // 2
    nf = half // 2
    inv = np.float32(ROPE_THETA) ** (-(np.arange(nf, dtype=np.float32) * np.float32(2)) / np.float32(half))
    ang = np.stack([row[:, None] * inv, col[:, None] * inv], axis=1).astype(np.float32)
    c, s = np.cos(ang), np.sin(ang)
    cos = np.stack([c, c], axis=2).reshape(TT, P, dim)
    sin = np.stack([-s, s], axis=2).reshape(TT, P, dim)
    return [a.transpose(1, 0, 2).reshape(P, TT * dim).astype(np.float32) for a in (cos, sin)]


def shape_constants():
    a = np.arange(P)
    k, t = a[:, None], a[None, :]
    base = np.concatenate([k == t, k <= t, k > t, k >= t, k < t], axis=1).astype(np.float32)
    tab_a = np.concatenate(rope_tables(AD), axis=1)
    s = (np.arange(TT)[None, :, None] * P + a[:, None, None])
    diff = (np.arange(SEQ)[None, None, :] - s).astype(np.float32)
    tab_r = np.concatenate(rope_tables(RQK) + [np.maximum(diff, 0).reshape(P, -1),
                                               np.maximum(-diff, 0).reshape(P, -1)], axis=1)
    return base, tab_a, tab_r.astype(np.float32)


def build(nc, w, consts, tab_a, tab_r, out):
    ctx = ExitStack()
    with ctx:
        def sb(name, shape, dt=F32):
            return ctx.enter_context(nc.sbuf_tensor(name, [P] + list(shape), dt))

        def sem(name):
            return ctx.enter_context(nc.semaphore(name))

        raw = sb("raw", [2, UNIT])
        whi = sb("whi", [4, HALF], F32R)
        wlo = sb("wlo", [4, HALF], F32R)
        feat = sb("feat", [32, SEQ], F32R)
        x = sb("x", [TT, D_MODEL])
        h = sb("h", [TT, D_MODEL])
        big = sb("big", [12288])
        tmp = sb("tmp", [9472])
        gain = sb("gain", [2, D_MODEL])
        cst = sb("cst", [N_CONST])
        cols = sb("cols", [2, 208])
        par = sb("par", [2, 160])
        negA = sb("negA", [2, 64])
        wdt_hi = sb("wdt_hi", [2, 512], F32R)
        wdt_lo = sb("wdt_lo", [2, 512], F32R)
        sq = sb("sq", [64])
        rs = sb("rs", [128])
        dts = sb("dts", [2, P])
        fac = sb("fac", [4, 32])
        srcf = sb("srcf", [2, 32])
        lg = sb("lg", [64])
        ps = [ctx.enter_context(nc.psum_tensor(f"ps{i}", [P, 512], F32)) for i in range(8)]

        ident = cst[:, C_ID:C_ID + P]
        upto, after, fromon, before = (cst[:, c:c + P] for c in (C_LE, C_GT, C_GE, C_LT))
        HT_HI, HT_LO = 16, 24
        Y_LO = {0: 16, 1: 8, 2: 16}

        raw_in = [sem("raw_in0"), sem("raw_in1")]
        hi_done, lo_done, w_used = sem("hi_done"), sem("lo_done"), sem("w_used")
        x_in = [sem("x_in0"), sem("x_in1")]
        const_in, rows_in, par_in = sem("const_in"), sem("rows_in"), sem("par_in")
        gain_in = [sem("gain_in0"), sem("gain_in1")]
        tab_in = sem("tab_in")
        out_done = sem("out_done")
        set_t, set_e, set_a, set_w = sem("set_t"), sem("set_e"), sem("set_a"), sem("set_w")
        x_sq, h_done, h_t, h_hi, h_lo = sem("x_sq"), sem("h_done"), sem("h_t"), sem("h_hi"), sem("h_lo")
        acc0, m_sq, x_done = sem("acc0"), sem("m_sq"), sem("x_done")
        chain = sem("chain")
        pchain = sem("pchain")
        S = {}
        for l in range(DEPTH):
            names = {0: "pad_ok dt_mm dt_abs dt_u dt_ok pre_mm pre_e conv_in conv0 conv1 conv_y x_t x_tok z_ok cb_mm cb_ok "
                        "mf_ok seg_mm seg_e w_ok xs_ok xd_ok y_mm y_v y_g y_sq y_t y_hi y_lo",
                     1: "qkv_in tab_ok qn_r r0 r1 qk_t qk_in s_mm s_max s_e p_ok p_t p_in o_mm o_hi o_lo",
                     2: "lg_e d_pre d_e qk_raw r0 r1 qk_t qk_in v_in g_in s_mm s_w y_mm y_sq y_g y_t y_hi y_lo"}[l % 3]
            for nm in (names + " relu sqr a_hi a_lo").split():
                S[l, nm] = sem(f"l{l}_{nm}")

        def view(buf, at, *shape):
            n = int(np.prod(shape))
            v = buf[:, at:at + n]
            if len(shape) == 2:
                return v.rearrange("p (a b) -> p a b", b=shape[1])
            if len(shape) == 3:
                return v.rearrange("p (a b c) -> p a b c", b=shape[1], c=shape[2])
            return v

        dtw = h[:, 0, 0:7 * P].rearrange("p (a b) -> p a b", b=P)
        xtok = view(big, 0, TT, SSM_INNER)
        BT, CT = view(big, 4096, SSM_GROUPS, SEQ), view(big, 6144, SSM_GROUPS, SEQ)
        sz = view(big, 8192, TT, SSM_INNER)
        CW = SEQ + 2 * PAD
        cpad = [view(tmp, 2 * CW * i, 2, CW) for i in range(2)]
        cacc = [view(tmp, 4 * CW + 512 * i, 2, SEQ) for i in range(2)]
        xc = [view(tmp, 4 * CW + 1024 + 512 * i, 2, SEQ) for i in range(4)]
        prod = view(tmp, 4 * CW + 3072, SSM_CONV, SEQ)
        MF = [view(tmp, 1024 * fb, TT, 512) for fb in range(2)]
        XS = [view(tmp, 2048 + 512 * i, TT, 256) for i in range(3)]
        EX = view(tmp, 3584, TT, 512)
        WM = [view(tmp, 4608 + 1024 * fb, TT, 512) for fb in range(2)]
        CBM = view(tmp, 6656, 3, TT, P)
        YT = [view(tmp, 7424 + 512 * i, TT, 256) for i in range(3)]
        XD = view(tmp, 8960, TT, 256)
        qkv = view(big, 0, TT, 1536)
        qkT = view(big, 3072, 10, SEQ)
        prob = [view(big, 5632 + 512 * i, TT, SEQ) for i in range(2)]
        probT = [view(big, 6656 + 512 * i, TT, SEQ) for i in range(2)]
        tabA = view(tmp, 0, N_TABA)
        gq = view(tmp, 512, 256)
        tw = view(tmp, 768, 4, TT, AD)
        ra = [view(tmp, 1792 + 1280 * j, 1280) for j in range(2)]
        rb = [view(tmp, 4352 + 1280 * j, 1280) for j in range(2)]
        rT = view(big, 0, 16, SEQ)
        vr = view(big, 4096, TT, 4 * RV)
        sg = view(big, 8192, TT, 4 * RV)
        tabR = view(tmp, 0, N_TABR)
        dec = view(tmp, 2048, RH, TT, SEQ)
        rraw = view(tmp, 4096, TT, 512)
        rA, rB = view(tmp, 5120, TT, 512), view(tmp, 6144, TT, 512)
        wt = [view(tmp, 7168 + 512 * i, TT, SEQ) for i in range(2)]
        drow = view(tmp, 8192, TT, 256)
        rl = [view(tmp, 512 * i, 512) for i in range(2)]
        aa = view(tmp, 1024, 512)

        def rope_att(eng, ops, link, j, done):
            v = qkv[:, j, 0:1280].rearrange("p (h d) -> p h d", d=AD)
            r = rs[:, 20 + 10 * j:30 + 10 * j].unsqueeze(2).to_broadcast([P, 10, AD])
            link(ops.tensor_tensor(v, v, r, ALU.mult))
            for b, (h0, hn) in enumerate(((0, AQ), (AQ, AKV))):
                hv = v[:, h0:h0 + hn, :]
                ops.tensor_tensor(ra[j].rearrange("p (h d) -> p h d", d=AD)[:, h0:h0 + hn, :], hv,
                                  tw[:, 2 * b, j, :].unsqueeze(1).to_broadcast([P, hn, AD]), ALU.mult)
                src = hv.rearrange("p h (a r d) -> p h a r d", a=2, r=2)
                dst = rb[j].rearrange("p (h d) -> p h d", d=AD)[:, h0:h0 + hn, :].rearrange("p h (a r d) -> p h a r d", a=2, r=2)
                sn = tw[:, 2 * b + 1, j, :].rearrange("p (a r d) -> p a r d", a=2, r=2)
                for a in range(2):
                    for r_ in range(2):
                        ins = ops.tensor_tensor(dst[:, :, a, r_, :], src[:, :, a, 1 - r_, :],
                                                sn[:, a, r_, :].unsqueeze(1).to_broadcast([P, hn, AD // 4]), ALU.mult)
            link(ins)
            ops.tensor_tensor(qkv[:, j, 0:1280], ra[j], rb[j], ALU.add).then_inc(done, 1)

        def low_y(V, dve, l, i, g, kk):
            dve.wait_ge(S[l, "y_hi"], 2 * g + kk + 1)
            if kk == 0:
                dve.wait_ge(S[l, "y_hi"], 2 * g + 2)
            V.scalar_tensor_tensor(out=feat[:, 16 + 2 * g + kk, :], in0=ps[7][:, 256 * kk:256 * kk + 256],
                                   scalar=cols[:, i, 192 + 2 * g + kk:193 + 2 * g + kk],
                                   in1=feat[:, 2 * g + kk, :].bitcast(F32), op0=ALU.mult,
                                   op1=ALU.subtract).then_inc(S[l, "y_lo"], 1)

        block = ctx.enter_context(nc.Block())

        @block.sync
        def _(sp):
            def load(q, par_, src, static):
                if not static or q >= 1:
                    sp.wait_ge(lo_done, 4 * q + 2 * par_ - 2)
                dst = raw[:, par_, :]
                if len(src.shape) == 3:
                    dst = dst.rearrange("p (k n) -> p k n", k=src.shape[1])
                sp.dma_start(dst, src).then_inc(raw_in[par_], 16)

            def group_src(wm, c0, hf):
                return wm.rearrange("(k p) n -> p k n", p=P)[:, 4 * hf:4 * hf + 4, c0:c0 + 512]

            def rows_src(wm, u):
                return wm[256 * u:256 * u + 256, :].rearrange("(k p) n -> p k n", p=P)

            for j in range(TT):
                sp.dma_start(x[:, j, :], w["x"][0, j * P:(j + 1) * P, :]).then_inc(x_in[j], 16)
            sp.dma_start(cst[:, :], consts).then_inc(const_in, 16)
            for l in range(DEPTH):
                n = FIRST_UNIT[2 * l]
                kind, i = l % 3, l // 3
                srcs = []
                if kind == 0:
                    wi = w["ssm_w_in"][i]
                    for u in range(XBC_UNITS):
                        c0 = SSM_INNER + 256 * u
                        srcs.append(wi.rearrange("(k p) n -> p k n", p=P)[:, :, c0:c0 + 256])
                    srcs += [group_src(wi, 512 * (u // 2), u % 2) for u in range(Z_UNITS)]
                    srcs += [rows_src(w["ssm_w_out"][i], u) for u in range(SSM_OUT_UNITS)]
                elif kind == 1:
                    srcs += [group_src(w["att_w_in"][i], 512 * (u // 2), u % 2) for u in range(2 * ATT_GROUPS)]
                    srcs += [rows_src(w["att_w_out"][i], u) for u in range(ATT_OUT_UNITS)]
                else:
                    for q in range(RET_GROUPS):
                        c0 = 512 * q if q < 4 else 512 * (4 + (q - 4) // 2 + 4 * (q % 2))
                        srcs += [group_src(w["ret_w_in"][i], c0, hf) for hf in range(2)]
                    srcs += [rows_src(w["ret_w_out"][i], u) for u in range(RET_OUT_UNITS)]
                for u, src in enumerate(srcs):
                    load((n + u) // 2, (n + u) % 2, src, True)
                q0 = FIRST_UNIT[2 * l + 1] // 2
                w1 = w["mlp_w_in"][l].rearrange("(k p) f -> p k f", p=P)
                w2 = w["mlp_w_out"][l].rearrange("(s k p) n -> p s k n", p=P, k=2)
                load(q0, 0, w1[:, :, 0:256], True)
                load(q0, 1, w1[:, :, 256:512], True)
                with sp.Fori(0, MLP_STEPS // 2 - 1) as it:
                    for b in range(2):
                        load(q0 + 1 + it * 2 + b, 0, w2[:, bass.ds(it * 2 + b, 1), :, :].squeeze(1), False)
                        load(q0 + 1 + it * 2 + b, 1, w1[:, :, bass.ds(it * 512 + 512 + 256 * b, 256)], False)
                load(q0 + MLP_STEPS - 1, 0, w2[:, MLP_STEPS - 2, :, :], True)
                load(q0 + MLP_STEPS - 1, 1, w2[:, MLP_STEPS - 1, :, :], True)
            for j in range(TT):
                sp.wait_ge(x_done, TT * (2 * DEPTH - 1) + j + 1)
                sp.dma_start(out[0, j * P:(j + 1) * P, :], x[:, j, :]).then_inc(out_done, 16)
            sp.wait_ge(out_done, 32)

        @block.gpsimd
        def _(pool):
            steps = [0]

            def link(ins):
                steps[0] += 1
                ins.then_inc(pchain, 1)
                pool.wait_ge(pchain, steps[0])

            gain_rows = []
            for l in range(DEPTH):
                gain_rows += [w["norm_mix_pre"][l], w["norm_mix_post"][l], w["norm_ffn_pre"][l], w["norm_ffn_post"][l]]
            sent = [0]

            def send_gain():
                u = sent[0]
                if u >= len(gain_rows):
                    return
                sent[0] += 1
                if u >= 2:
                    pool.wait_ge(h_done if u % 2 == 0 else x_done, 2 * ((u - 2) // 2) + 2)
                pool.dma_start(gain[:, u % 2, :], gain_rows[u].partition_broadcast(P)).then_inc(gain_in[u % 2], 16)

            send_gain()
            send_gain()
            for i in range(len(SSM_LAYERS)):
                cw = w["ssm_conv_w"][i].rearrange("t (c p) -> (t c) p", p=P)
                r0, r1 = view(tmp, 256 * i, P), view(tmp, 256 * i + 128, P)
                pool.dma_start(r0[0:96, :], cw[0:96, :]).then_inc(rows_in, 16)
                pool.dma_start(r1[0:64, :], cw[96:160, :]).then_inc(rows_in, 16)
                pool.dma_start(r1[64:96, :], w["ssm_conv_b"][i].rearrange("(c p) -> c p", p=P)).then_inc(rows_in, 16)
                pool.dma_start(r1[96:112, :], w["ssm_norm"][i].rearrange("(c p) -> c p", p=P)).then_inc(rows_in, 16)
                pool.dma_start(par[:, i, 0:64], w["ssm_dt_bias"][i].rearrange("a h -> (a h)").partition_broadcast(P)).then_inc(par_in, 16)
                pool.dma_start(par[:, i, 64:128], w["ssm_a_log"][i].rearrange("a h -> (a h)").partition_broadcast(P)).then_inc(par_in, 16)
                pool.dma_start(par[:, i, 128:160], w["ssm_d"][i].partition_broadcast(P)).then_inc(par_in, 16)
                pool.dma_start(view(tmp, 512 + 512 * i, KD, 64),
                               w["ssm_w_in"][i][:, SSM_INNER + CONV_DIM:].rearrange("(k p) n -> p k n", p=P)).then_inc(par_in, 16)

            def rope_ret(l, q):
                pool.wait_ge(S[l, "qk_raw"], 2 * q + 2)
                if q >= 1:
                    pool.wait_ge(S[l, "qk_t"], 2 * q)
                src = rraw[:, 1, :].rearrange("p (h d) -> p h d", h=2)
                cosb = tabR[:, T_COSR + 256:T_COSR + 512].unsqueeze(1).to_broadcast([P, 2, 256])
                nc.gpsimd.tensor_tensor(rA[:, 1, :].rearrange("p (h d) -> p h d", h=2), src, cosb, ALU.mult)
                s5 = rraw[:, 1, :].rearrange("p (h r d) -> p h r d", h=4, r=2)
                o5 = rB[:, 1, :].rearrange("p (h r d) -> p h r d", h=4, r=2)
                sn = tabR[:, T_SINR + 256:T_SINR + 512].rearrange("p (a r d) -> p a r d", a=2, r=2)
                for hd in range(2):
                    for r in range(2):
                        ins = nc.gpsimd.tensor_tensor(o5[:, 2 * hd:2 * hd + 2, r, :], s5[:, 2 * hd:2 * hd + 2, 1 - r, :],
                                                      sn[:, :, r, :], ALU.mult)
                link(ins)
                nc.gpsimd.tensor_tensor(rA[:, 1, :], rA[:, 1, :], rB[:, 1, :], ALU.add).then_inc(S[l, "r1"], 1)

            for l in range(DEPTH):
                kind, i = l % 3, l // 3
                s = 2 * l
                send_gain()
                if kind == 0:
                    pool.wait_ge(h_done, 2 * s + 2)
                    for b in range(2):
                        nc.gpsimd.memset(cpad[b][:, :, 0:PAD], 0.0)
                        nc.gpsimd.memset(cpad[b][:, :, PAD + SEQ:CW], 0.0).then_inc(S[l, "pad_ok"], 1)
                    pool.wait_ge(S[l, "pad_ok"], 2)
                    for u in range(XBC_UNITS):
                        ct = 2 * u + 1
                        if u >= 1:
                            pool.wait_ge(S[l, "conv1"], u)
                        pool.wait_ge(S[l, "conv_in"], u + 1)
                        if u >= 2:
                            pool.wait_ge(S[l, "conv_y"], 2 * (u - 1))
                        src = cpad[u % 2][:, 1, 0:SEQ]
                        windows = bass.AP(tensor=src.tensor, offset=src.offset, ap=[src.ap[0], [1, SSM_CONV], [1, SEQ]])
                        taps = cols[:, i, ct:5 * CT_N:CT_N].unsqueeze(2).to_broadcast([P, SSM_CONV, SEQ])
                        link(nc.gpsimd.tensor_tensor(prod, windows, taps, ALU.mult))
                        link(nc.gpsimd.tensor_tensor(prod[:, 0:2, :], prod[:, 0:2, :], prod[:, 2:4, :], ALU.add))
                        link(nc.gpsimd.tensor_tensor(prod[:, 0, :], prod[:, 0, :], prod[:, 4, :], ALU.add))
                        nc.gpsimd.tensor_tensor(cacc[u % 2][:, 1, :], prod[:, 0, :], prod[:, 1, :],
                                                ALU.add).then_inc(S[l, "conv1"], 1)
                    pool.wait_ge(S[l, "dt_ok"], 2)
                    pool.wait_ge(S[l, "pre_e"], 1)
                    nc.gpsimd.tensor_tensor(srcf[:, 0, :], fac[:, 2, :], dts[:, 0, 0:32], ALU.mult)
                    link(nc.gpsimd.tensor_tensor(srcf[:, 1, :], fac[:, 3, :], dts[:, 0, 96:128], ALU.mult))
                    dA = dts[:, 1, :].rearrange("p (j d h) -> p j d h", j=2, d=2)
                    dt = dts[:, 0, :].rearrange("p (j d h) -> p j d h", j=2, d=2)
                    pool.wait_ge(S[l, "x_tok"], 8)
                    pool.wait_ge(S[l, "conv_y"], 2 * XBC_UNITS)
                    def exponents(g):
                        if g >= 1:
                            pool.wait_ge(S[l, "seg_mm"], 2 * g)
                        for j in range(TT):
                            for fb, mask in ((0, upto), (1, fromon)):
                                nc.gpsimd.tensor_tensor(MF[fb][:, j, :].rearrange("p (h t) -> p h t", h=HPG),
                                                        mask.unsqueeze(1).to_broadcast([P, HPG, P]),
                                                        dA[:, j, fb, HPG * g:HPG * g + HPG].unsqueeze(2).to_broadcast([P, HPG, P]),
                                                        ALU.mult).then_inc(S[l, "mf_ok"], 1)

                    def sources(g):
                        hs = slice(HPG * g, HPG * g + HPG)
                        if g >= 1:
                            pool.wait_ge(S[l, "y_mm"], g)
                        for j in range(TT):
                            xh = xtok[:, j, 256 * g:256 * g + 256].rearrange("p (h d) -> p h d", h=HPG)
                            for b, f in enumerate((dt[:, j, 0, hs], dt[:, j, 1, hs], srcf[:, j, hs])):
                                nc.gpsimd.tensor_tensor(XS[b][:, j, :].rearrange("p (h d) -> p h d", h=HPG), xh,
                                                        f.unsqueeze(2).to_broadcast([P, HPG, SSM_HDIM]),
                                                        ALU.mult).then_inc(S[l, "xs_ok"], 1)

                    exponents(0)
                    sources(0)
                    for g in range(SSM_GROUPS):
                        if g >= 1:
                            pool.wait_ge(S[l, "y_g"], g)
                        dsk = par[:, i, 128 + HPG * g:128 + HPG * g + HPG].unsqueeze(2).to_broadcast([P, HPG, SSM_HDIM])
                        for j in range(TT):
                            ins = nc.gpsimd.tensor_tensor(XD[:, j, :].rearrange("p (h d) -> p h d", h=HPG),
                                                          xtok[:, j, 256 * g:256 * g + 256].rearrange("p (h d) -> p h d", h=HPG),
                                                          dsk, ALU.mult)
                        link(ins)
                        if g + 1 < SSM_GROUPS:
                            exponents(g + 1)
                        pool.wait_ge(S[l, "y_v"], g + 1)
                        if g >= 1:
                            pool.wait_ge(S[l, "y_t"], g)
                            pool.wait_ge(S[l, "y_sq"], 2 * g)
                        link(nc.gpsimd.tensor_tensor(XD, YT[1], XD, ALU.add))
                        nc.gpsimd.tensor_tensor(YT[2], XD, sz[:, :, 256 * g:256 * g + 256], ALU.mult).then_inc(S[l, "y_g"], 1)
                        if g + 1 < SSM_GROUPS:
                            sources(g + 1)
                elif kind == 1:
                    pool.wait_ge(h_done, 2 * s + 2)
                    pool.dma_start(tabA, tab_a).then_inc(tab_in, 16)
                    pool.dma_start(gq[:, 0:128], w["att_q_norm"][i].partition_broadcast(P)).then_inc(tab_in, 16)
                    pool.dma_start(gq[:, 128:256], w["att_k_norm"][i].partition_broadcast(P)).then_inc(tab_in, 16)
                    pool.wait_ge(S[l, "tab_ok"], 1)
                    pool.wait_ge(S[l, "qn_r"], 1)
                    rope_att(pool, nc.gpsimd, link, 1, S[l, "r1"])
                else:
                    pool.wait_ge(h_done, 2 * s + 2)
                    pool.dma_start(tabR, tab_r).then_inc(tab_in, 16)
                    pool.dma_start(lg[:, 0:8], w["ret_log2_decay"][i].rearrange("a h -> (a h)").partition_broadcast(P)).then_inc(tab_in, 16)
                    pool.wait_ge(tab_in, 80)
                    for q in range(4):
                        rope_ret(l, q)
                send_gain()
                send_gain()
                send_gain()

        @block.scalar
        def _(act):
            def split(q, par_, static=True):
                act.wait_ge(raw_in[par_], 16 * (q + 1))
                for hf in range(2):
                    if not static or q >= 1:
                        act.wait_ge(w_used, 4 * q + 2 * par_ + hf - 3)
                    nc.scalar.activation(whi[:, 2 * par_ + hf, :], raw[:, par_, hf * HALF:(hf + 1) * HALF],
                                         ACT.Copy).then_inc(hi_done, 1)

            def splitn(n):
                if n < N_UNITS:
                    split(n // 2, n % 2)

            def prep(s):
                for j in range(TT):
                    if s == 0:
                        act.wait_ge(x_in[j], 16)
                    else:
                        act.wait_ge(x_done, 2 * s - 2 + j + 1)
                    nc.scalar.activation(h[:, j, :], x[:, j, :], ACT.Square, accum_out=sq[:, j:j + 1]).then_inc(x_sq, 1)
                for j in range(TT):
                    for c in range(2):
                        act.wait_ge(h_t, 4 * s + 2 * j + c + 1)
                        nc.scalar.activation(feat[:, HT_HI + 4 * c:HT_HI + 4 * c + 4, j * P:(j + 1) * P],
                                             ps[4 + 2 * j + c][:, :].rearrange("p (k t) -> p k t", k=4),
                                             ACT.Copy).then_inc(h_hi, 1)

            def post(s):
                for j in range(TT):
                    if j == 0:
                        act.wait_ge(acc0, s + 1)
                    else:
                        act.wait_ge(w_used, 2 * (FIRST_UNIT + [N_UNITS])[s + 1])
                    for c in range(2):
                        nc.scalar.activation(h[:, j, 512 * c:512 * c + 512], ps[2 * j + c][:, :], ACT.Square,
                                             accum_out=sq[:, 4 + 2 * j + c:5 + 2 * j + c]).then_inc(m_sq, 1)

            act.wait_ge(par_in, 16 * 8)
            for i in range(2):
                nc.scalar.activation(negA[:, i, :], par[:, i, 64:128], ACT.Exp).then_inc(set_a, 1)
                nc.scalar.activation(wdt_hi[:, i, :], view(tmp, 512 + 512 * i, 512), ACT.Copy).then_inc(set_w, 1)
            act.wait_ge(set_t, 1)
            for i in range(2):
                nc.scalar.activation(cols[:, i, 0:96], ps[0][:, 256 * i:256 * i + 96], ACT.Copy).then_inc(set_e, 1)
                nc.scalar.activation(cols[:, i, 96:208], ps[0][:, 256 * i + 128:256 * i + 240], ACT.Copy).then_inc(set_e, 1)
            splitn(0)
            splitn(1)
            for l in range(DEPTH):
                kind, s, n0 = l % 3, 2 * l, FIRST_UNIT[2 * l]
                i = l // 3
                prep(s)
                if kind == 0:
                    def conv_finish(u):
                        for cc in range(2):
                            ct = 2 * u + cc
                            act.wait_ge(S[l, "conv0" if cc == 0 else "conv1"], u + 1)
                            if ct < 16:
                                if u >= 4:
                                    act.wait_ge(S[l, "x_t"], u - 3)
                                dst = xc[u % 4][:, cc, :]
                            else:
                                dst = (BT if ct < 24 else CT)[:, ct % 8, :]
                            nc.scalar.activation(dst, cacc[u % 2][:, cc, :], ACT.Silu,
                                                 bias=cols[:, i, 160 + ct:161 + ct]).then_inc(S[l, "conv_y"], 1)

                    def x_evac(u):
                        act.wait_ge(S[l, "x_t"], u + 1)
                        nc.scalar.activation(xtok[:, :, 256 * u:256 * u + 256],
                                             ps[6 + u % 2][:, :].rearrange("p (j c) -> p j c", j=2),
                                             ACT.Copy).then_inc(S[l, "x_tok"], 1)

                    act.wait_ge(S[l, "dt_abs"], 1)
                    nc.scalar.activation(dtw[:, 1, :], dtw[:, 1, :], ACT.Exp, scale=-1.0).then_inc(S[l, "dt_u"], 1)
                    act.wait_ge(S[l, "pre_mm"], 1)
                    nc.scalar.activation(fac[:, :, :].rearrange("p a h -> p (a h)"), ps[3][:, 0:128], ACT.Exp).then_inc(S[l, "pre_e"], 1)
                    for u in range(XBC_UNITS):
                        act.wait_ge(w_used, 2 * (n0 + u) + 2)
                        if u >= 2:
                            act.wait_ge(S[l, "conv0"], u - 1)
                            act.wait_ge(S[l, "conv1"], u - 1)
                        nc.scalar.activation(cpad[u % 2][:, :, PAD:PAD + SEQ],
                                             ps[4 + u % 2][:, :].rearrange("p (c t) -> p c t", c=2),
                                             ACT.Copy).then_inc(S[l, "conv_in"], 1)
                        splitn(n0 + u + 2)
                        if u >= 1:
                            conv_finish(u - 1)
                        if 3 <= u < 11:
                            x_evac(u - 3)
                    conv_finish(XBC_UNITS - 1)
                    for u in range(Z_UNITS):
                        if u % 2:
                            act.wait_ge(w_used, 2 * (n0 + XBC_UNITS + u) + 2)
                            for j in range(TT):
                                nc.scalar.activation(sz[:, j, 256 * (u - 1):256 * (u + 1)],
                                                     ps[2 * (u // 2 % 2) + j][:, :], ACT.Silu).then_inc(S[l, "z_ok"], 1)
                        splitn(n0 + XBC_UNITS + u + 2)

                    def exps(g):
                        for j in range(TT):
                            act.wait_ge(S[l, "seg_mm"], 2 * g + j + 1)
                            if g >= 1:
                                act.wait_ge(S[l, "w_ok"], 4 * (g - 1) + 2 * j + 2)
                            nc.scalar.activation(EX[:, j, :], ps[5 + j][:, :], ACT.Exp).then_inc(S[l, "seg_e"], 1)

                    exps(0)
                    for g in range(SSM_GROUPS):
                        if g + 1 < SSM_GROUPS:
                            exps(g + 1)
                        act.wait_ge(S[l, "y_g"], g + 1)
                        for j in range(TT):
                            nc.scalar.activation(h[:, j, 0:256], YT[2][:, j, :], ACT.Square,
                                                 accum_out=sq[:, 16 + 8 * j + g:17 + 8 * j + g]).then_inc(S[l, "y_sq"], 1)
                            act.wait_ge(S[l, "y_sq"], 2 * g + j + 1)
                        act.wait_ge(S[l, "y_t"], g + 1)
                        for kk in range(2):
                            nc.scalar.activation(feat[:, 2 * g + kk, :], ps[7][:, 256 * kk:256 * kk + 256], ACT.Identity,
                                                 scale=cols[:, i, 192 + 2 * g + kk:193 + 2 * g + kk]).then_inc(S[l, "y_hi"], 1)
                    for u in range(SSM_OUT_UNITS):
                        splitn(n0 + XBC_UNITS + Z_UNITS + u + 2)
                elif kind == 1:
                    for u in range(2 * ATT_GROUPS):
                        if u % 2:
                            act.wait_ge(w_used, 2 * (n0 + u) + 2)
                            for j in range(TT):
                                nc.scalar.activation(qkv[:, j, 256 * (u - 1):256 * (u + 1)], ps[(u - 1) + j][:, :],
                                                     ACT.Copy).then_inc(S[l, "qkv_in"], 1)
                        splitn(n0 + u + 2)
                    for c in range(5):
                        act.wait_ge(S[l, "qk_t"], c + 1)
                        nc.scalar.activation(qkT[:, 2 * c:2 * c + 2, :], ps[6 + c % 2][:, :].rearrange("p (a t) -> p a t", a=2),
                                             ACT.Copy).then_inc(S[l, "qk_in"], 1)

                    def exp_head(hd):
                        act.wait_ge(S[l, "s_max"], hd + 1)
                        if hd >= 2:
                            act.wait_ge(S[l, "p_t"], hd - 1)
                        for j in range(TT):
                            nc.scalar.activation(prob[hd % 2][:, j, :], ps[hd % 2][:, j * SEQ:(j + 1) * SEQ], ACT.Exp,
                                                 bias=sq[:, 48 + 2 * (hd % 2) + j:49 + 2 * (hd % 2) + j], scale=float(AD) ** -0.5,
                                                 accum_out=sq[:, 52 + 2 * (hd % 2) + j:53 + 2 * (hd % 2) + j]).then_inc(S[l, "s_e"], 1)

                    exp_head(0)
                    for hd in range(AQ):
                        if hd + 1 < AQ:
                            exp_head(hd + 1)
                        act.wait_ge(S[l, "p_t"], hd + 1)
                        if hd >= 2:
                            act.wait_ge(S[l, "o_mm"], hd - 1)
                        nc.scalar.activation(probT[hd % 2], ps[2 + hd % 2][:, :].rearrange("p (a t) -> p a t", a=2),
                                             ACT.Copy).then_inc(S[l, "p_in"], 1)
                        act.wait_ge(S[l, "o_mm"], hd + 1)
                        nc.scalar.activation(feat[:, hd, :], ps[4 + hd % 2][:, 0:SEQ], ACT.Copy).then_inc(S[l, "o_hi"], 1)
                    for u in range(ATT_OUT_UNITS):
                        splitn(n0 + 2 * ATT_GROUPS + u + 2)
                else:
                    act.wait_ge(tab_in, 80)
                    nc.scalar.activation(lg[:, 8:16], lg[:, 0:8], ACT.Exp, scale=float(np.log(2.0))).then_inc(S[l, "lg_e"], 1)
                    act.wait_ge(S[l, "lg_e"], 2)
                    nc.scalar.activation(lg[:, 24:32], lg[:, 16:24], ACT.Ln).then_inc(S[l, "lg_e"], 1)
                    for hd in range(RH):
                        act.wait_ge(S[l, "d_pre"], hd + 1)
                        nc.scalar.activation(dec[:, hd, :, :], dec[:, hd, :, :], ACT.Exp).then_inc(S[l, "d_e"], 1)

                    def ysq(hd):
                        act.wait_ge(S[l, "y_mm"], hd + 1)
                        for j in range(TT):
                            nc.scalar.activation(rA[:, j, :], ps[4 + j][:, :], ACT.Square,
                                                 accum_out=sq[:, 32 + j:33 + j]).then_inc(S[l, "y_sq"], 1)

                    for q in range(RET_GROUPS):
                        splitn(n0 + 2 * q + 2)
                        act.wait_ge(w_used, 2 * (n0 + 2 * q + 1) + 2)
                        for j in range(TT):
                            src = ps[2 * (q % 2) + j][:, :]
                            if q < 4:
                                if q >= 1:
                                    act.wait_ge(S[l, "r0" if j == 0 else "r1"], q)
                                nc.scalar.activation(rraw[:, j, :], src, ACT.Copy).then_inc(S[l, "qk_raw"], 1)
                            elif q % 2 == 0:
                                hd = (q - 4) // 2
                                nc.scalar.activation(vr[:, j, RV * hd:RV * hd + RV], src, ACT.Copy).then_inc(S[l, "v_in"], 1)
                            else:
                                hd = (q - 4) // 2
                                nc.scalar.activation(sg[:, j, RV * hd:RV * hd + RV], src, ACT.Silu).then_inc(S[l, "g_in"], 1)
                        splitn(n0 + 2 * q + 3)
                        if q < 4:
                            for b in range(2):
                                act.wait_ge(S[l, "qk_t"], 2 * q + b + 1)
                                nc.scalar.activation(rT[:, 4 * q + 2 * b:4 * q + 2 * b + 2, :],
                                                     ps[4 + b][:, :].rearrange("p (a t) -> p a t", a=2),
                                                     ACT.Copy).then_inc(S[l, "qk_in"], 1)
                        elif q % 2:
                            ysq((q - 4) // 2)
                    for u in range(RET_OUT_UNITS):
                        act.wait_ge(S[l, "y_t"], u + 1)
                        nc.scalar.activation(feat[:, 2 * u:2 * u + 2, :], ps[4 + u % 4][:, :].rearrange("p (a t) -> p a t", a=2),
                                             ACT.Copy).then_inc(S[l, "y_hi"], 1)
                        if u >= 1:
                            splitn(n0 + 2 * RET_GROUPS + u + 1)
                    splitn(n0 + 2 * RET_GROUPS + RET_OUT_UNITS + 1)
                post(s)

                s += 1
                n0 = FIRST_UNIT[s]
                q0 = n0 // 2
                prep(s)

                def relu(st, b, q, par_, static):
                    act.wait_ge(w_used, 4 * q + 2 * par_ + 2)
                    if not static or st >= 2:
                        act.wait_ge(S[l, "a_lo"], st - 1)
                    nc.scalar.activation(rl[b], ps[4 + b][:, :], ACT.Relu).then_inc(S[l, "relu"], 1)
                    act.wait_ge(S[l, "relu"], st + 1)
                    nc.scalar.activation(feat[:, 4 * b:4 * b + 2, :], rl[b].rearrange("p (a t) -> p a t", a=2),
                                         ACT.Square).then_inc(S[l, "a_hi"], 1)

                relu(0, 0, q0, 0, True)
                splitn(n0 + 2)
                relu(1, 1, q0, 1, True)
                splitn(n0 + 3)
                with act.Fori(0, MLP_STEPS // 2 - 1) as it:
                    for b in range(2):
                        q = q0 + 1 + it * 2 + b
                        split(q + 1, 0, False)
                        relu(it * 2 + 2 + b, b, q, 1, False)
                        split(q + 1, 1, False)
                splitn(n0 + MLP_UNITS)
                splitn(n0 + MLP_UNITS + 1)
                post(s)

        @block.vector
        def _(dve):
            steps = [0]
            V = nc.vector

            def link(ins):
                steps[0] += 1
                ins.then_inc(chain, 1)
                dve.wait_ge(chain, steps[0])

            def split(q, par_):
                for hf in range(2):
                    dve.wait_ge(hi_done, 4 * q + 2 * par_ + hf + 1)
                    V.tensor_tensor(wlo[:, 2 * par_ + hf, :], raw[:, par_, hf * HALF:(hf + 1) * HALF],
                                    whi[:, 2 * par_ + hf, :].bitcast(F32), ALU.subtract).then_inc(lo_done, 1)

            def splitn(n):
                if n < N_UNITS:
                    split(n // 2, n % 2)

            def rsqrt(dst, v, scratch, done=None):
                link(V.tensor_scalar(dst.bitcast(I32), v.bitcast(I32), -0.5, 1597463007.0, ALU.mult, ALU.add))
                for it in range(3):
                    link(V.tensor_tensor(scratch, v, dst, ALU.mult))
                    link(V.tensor_tensor(scratch, scratch, dst, ALU.mult))
                    link(V.tensor_scalar(scratch, scratch, -0.5, 1.5, ALU.mult, ALU.add))
                    ins = V.tensor_tensor(dst, dst, scratch, ALU.mult)
                    if it == 2 and done is not None:
                        ins.then_inc(done, 1)
                        dve.wait_ge(done, 1)
                    else:
                        link(ins)

            def prep(s):
                u = 2 * s
                for j in range(TT):
                    dve.wait_ge(x_sq, 2 * s + j + 1)
                    link(V.tensor_scalar(rs[:, 0:1], sq[:, j:j + 1], 1.0 / D_MODEL, EPS, ALU.mult, ALU.add))
                    rsqrt(rs[:, 1:2], rs[:, 0:1], rs[:, 2:3])
                    if j == 0:
                        dve.wait_ge(gain_in[u % 2], 16 * (u // 2 + 1))
                    V.scalar_tensor_tensor(out=h[:, j, :], in0=x[:, j, :], scalar=rs[:, 1:2], in1=gain[:, u % 2, :],
                                           op0=ALU.mult, op1=ALU.mult).then_inc(h_done, 1)
                    dve.wait_ge(h_done, 2 * s + j + 1)
                for j in range(TT):
                    for c in range(2):
                        dve.wait_ge(h_hi, 4 * s + 2 * j + c + 1)
                        tk = slice(j * P, (j + 1) * P)
                        V.tensor_tensor(feat[:, HT_LO + 4 * c:HT_LO + 4 * c + 4, tk],
                                        ps[4 + 2 * j + c][:, :].rearrange("p (k t) -> p k t", k=4),
                                        feat[:, HT_HI + 4 * c:HT_HI + 4 * c + 4, tk].bitcast(F32),
                                        ALU.subtract).then_inc(h_lo, 1)

            def post(s, inner_rs=None):
                u = 2 * s + 1
                for j in range(TT):
                    dve.wait_ge(m_sq, 4 * s + 2 * j + 2)
                    a, b = sq[:, 4 + 2 * j:5 + 2 * j], sq[:, 5 + 2 * j:6 + 2 * j]
                    link(V.tensor_tensor(rs[:, 4:5], a, b, ALU.add))
                    if inner_rs is not None:
                        r = inner_rs[:, j:j + 1]
                        link(V.scalar_tensor_tensor(out=rs[:, 4:5], in0=rs[:, 4:5], scalar=r, in1=r, op0=ALU.mult, op1=ALU.mult))
                    link(V.tensor_scalar(rs[:, 5:6], rs[:, 4:5], 1.0 / D_MODEL, EPS, ALU.mult, ALU.add))
                    rsqrt(rs[:, 6:7], rs[:, 5:6], rs[:, 7:8])
                    if inner_rs is not None:
                        link(V.tensor_tensor(rs[:, 6:7], rs[:, 6:7], inner_rs[:, j:j + 1], ALU.mult))
                    if j == 0:
                        dve.wait_ge(gain_in[u % 2], 16 * (u // 2 + 1))
                    for c in range(2):
                        ins = V.scalar_tensor_tensor(out=h[:, j, 512 * c:512 * c + 512], in0=ps[2 * j + c][:, :], scalar=rs[:, 6:7],
                                                     in1=gain[:, u % 2, 512 * c:512 * c + 512], op0=ALU.mult, op1=ALU.mult)
                    link(ins)
                    V.tensor_tensor(x[:, j, :], x[:, j, :], h[:, j, :], ALU.add).then_inc(x_done, 1)

            for i in range(2):
                dve.wait_ge(set_a, i + 1)
                link(V.tensor_scalar(negA[:, i, :], negA[:, i, :], -1.0, None, ALU.mult))
                dve.wait_ge(set_w, i + 1)
                link(V.tensor_tensor(wdt_lo[:, i, :], view(tmp, 512 + 512 * i, 512), wdt_hi[:, i, :].bitcast(F32), ALU.subtract))
            splitn(0)
            splitn(1)
            for l in range(DEPTH):
                kind, s, n0 = l % 3, 2 * l, FIRST_UNIT[2 * l]
                i = l // 3
                if kind == 0:
                    dve.wait_ge(set_e, 4)
                prep(s)
                if kind == 0:
                    v, av, r = (dtw[:, k, :] for k in range(3))
                    dve.wait_ge(S[l, "dt_mm"], 1)
                    link(V.tensor_tensor(v.rearrange("p (j d) -> p j d", j=2), ps[2][:, 0:128].rearrange("p (j d) -> p j d", j=2),
                                         par[:, i, 0:64].unsqueeze(1).to_broadcast([P, 2, 64]), ALU.add))
                    V.scalar_tensor_tensor(out=av, in0=v, scalar=-1.0, in1=v, op0=ALU.mult, op1=ALU.max).then_inc(S[l, "dt_abs"], 1)
                    V.tensor_scalar(r, v, 0.0, None, ALU.max)
                    dve.wait_ge(S[l, "dt_u"], 1)
                    den, z, z2, p_ = (dtw[:, k, :] for k in range(3, 7))
                    link(V.tensor_scalar(den, av, 2.0, None, ALU.add))
                    link(V.reciprocal(den, den))
                    link(V.tensor_tensor(z, av, den, ALU.mult))
                    link(V.tensor_tensor(z2, z, z, ALU.mult))
                    link(V.tensor_scalar(p_, z2, 1.0 / 15, None, ALU.mult))
                    for k in (13, 11, 9, 7, 5, 3):
                        link(V.scalar_tensor_tensor(out=p_, in0=p_, scalar=1.0 / k, in1=z2, op0=ALU.add, op1=ALU.mult))
                    link(V.scalar_tensor_tensor(out=p_, in0=p_, scalar=1.0, in1=z, op0=ALU.add, op1=ALU.mult))
                    V.scalar_tensor_tensor(out=dts[:, 0, :], in0=p_, scalar=2.0, in1=r, op0=ALU.mult, op1=ALU.add).then_inc(S[l, "dt_ok"], 1)
                    dve.wait_ge(S[l, "dt_ok"], 1)
                    V.tensor_tensor(dts[:, 1, :].rearrange("p (j d) -> p j d", j=2), dts[:, 0, :].rearrange("p (j d) -> p j d", j=2),
                                    negA[:, i, :].unsqueeze(1).to_broadcast([P, 2, 64]), ALU.mult).then_inc(S[l, "dt_ok"], 1)
                    for u in range(XBC_UNITS):
                        ct = 2 * u
                        dve.wait_ge(S[l, "conv_in"], u + 1)
                        if u >= 2:
                            dve.wait_ge(S[l, "conv_y"], 2 * (u - 1))
                        if u == 0:
                            dve.wait_ge(S[l, "pad_ok"], 2)
                        o = cacc[u % 2][:, 0, :]
                        for t in range(SSM_CONV):
                            tap = cols[:, i, CT_N * t + ct:CT_N * t + ct + 1]
                            src = cpad[u % 2][:, 0, t:t + SEQ]
                            if t == 0:
                                ins = V.tensor_scalar(o, src, tap, None, ALU.mult)
                            else:
                                ins = V.scalar_tensor_tensor(out=o, in0=src, scalar=tap, in1=o, op0=ALU.mult, op1=ALU.add)
                            if t < SSM_CONV - 1:
                                link(ins)
                        ins.then_inc(S[l, "conv0"], 1)
                        splitn(n0 + u + 2)
                    for u in range(Z_UNITS):
                        splitn(n0 + XBC_UNITS + u + 2)

                    def masked(g):
                        dve.wait_ge(S[l, "cb_mm"], g + 1)
                        if g == 0:
                            dve.wait_ge(S[l, "conv_y"], 2 * XBC_UNITS)
                            dve.wait_ge(S[l, "x_tok"], 8)
                        else:
                            dve.wait_ge(S[l, "y_mm"], g)
                        cb = ps[4][:, :].rearrange("p (a j t) -> p a j t", a=2, j=2)
                        for b, m in enumerate((upto, after)):
                            V.tensor_tensor(CBM[:, b, :, :], cb[:, 0, :, :], m.unsqueeze(1).to_broadcast([P, 2, P]),
                                            ALU.mult).then_inc(S[l, "cb_ok"], 1)
                        V.tensor_copy(CBM[:, 2, :, :], cb[:, 1, :, :]).then_inc(S[l, "cb_ok"], 1)

                    for g in range(SSM_GROUPS):
                        masked(g)
                        dve.wait_ge(S[l, "cb_ok"], 3 * g + 3)
                        for j in range(TT):
                            dve.wait_ge(S[l, "seg_e"], 2 * g + j + 1)
                            for fb in range(2):
                                V.tensor_tensor(WM[fb][:, j, :].rearrange("p (h t) -> p h t", h=HPG),
                                                EX[:, j, :].rearrange("p (h t) -> p h t", h=HPG),
                                                CBM[:, fb, j, :].unsqueeze(1).to_broadcast([P, HPG, P]),
                                                ALU.mult).then_inc(S[l, "w_ok"], 1)
                        if g >= 1:
                            for kk in range(2):
                                low_y(V, dve, l, i, g - 1, kk)
                        dve.wait_ge(S[l, "y_mm"], g + 1)
                        if g >= 1:
                            dve.wait_ge(S[l, "y_g"], g)
                        for j in range(TT):
                            ins = V.tensor_tensor(YT[0][:, j, :].rearrange("p (h d) -> p h d", h=HPG),
                                                  ps[g % 2][:, 256 * j:256 * j + 256].rearrange("p (h d) -> p h d", h=HPG),
                                                  fac[:, j, HPG * g:HPG * g + HPG].unsqueeze(2).to_broadcast([P, HPG, SSM_HDIM]),
                                                  ALU.mult)
                        link(ins)
                        V.tensor_tensor(YT[1], ps[2 + g % 2][:, :].rearrange("p (j c) -> p j c", j=2), YT[0],
                                        ALU.add).then_inc(S[l, "y_v"], 1)
                    for kk in range(2):
                        low_y(V, dve, l, i, SSM_GROUPS - 1, kk)
                    dve.wait_ge(S[l, "y_sq"], 2 * SSM_GROUPS)
                    link(V.tensor_reduce(rs[:, 10:12], sq[:, 16:32].rearrange("p (j g) -> p j g", j=2), AX.X, ALU.add))
                    link(V.tensor_scalar(rs[:, 12:14], rs[:, 10:12], 1.0 / SSM_INNER, EPS, ALU.mult, ALU.add))
                    rsqrt(rs[:, 16:18], rs[:, 12:14], rs[:, 14:16])
                    for u in range(SSM_OUT_UNITS):
                        splitn(n0 + XBC_UNITS + Z_UNITS + u + 2)
                    post(s, rs[:, 16:18])
                elif kind == 1:
                    dve.wait_ge(tab_in, 48)
                    for b in range(2):
                        V.tensor_tensor(tw[:, 2 * b, :, :], tabA[:, 0:256].rearrange("p (j d) -> p j d", j=2),
                                        gq[:, 128 * b:128 * b + 128].unsqueeze(1).to_broadcast([P, 2, AD]), ALU.mult)
                    for b in range(2):
                        for a in range(2):
                            for r_ in range(2):
                                o = 64 * a + 32 * r_
                                og = 128 * b + 64 * a + 32 * (1 - r_)
                                ins = V.tensor_tensor(tw[:, 2 * b + 1, :, o:o + 32],
                                                      tabA[:, 256:512].rearrange("p (j d) -> p j d", j=2)[:, :, o:o + 32],
                                                      gq[:, og:og + 32].unsqueeze(1).to_broadcast([P, 2, 32]), ALU.mult)
                    ins.then_inc(S[l, "tab_ok"], 1)
                    for u in range(2 * ATT_GROUPS):
                        splitn(n0 + u + 2)
                    dve.wait_ge(S[l, "qkv_in"], 6)
                    for j in range(TT):
                        V.tensor_tensor(ra[j], qkv[:, j, 0:1280], qkv[:, j, 0:1280], ALU.mult).then_inc(S[l, "tab_ok"], 1)
                    for j in range(TT):
                        dve.wait_ge(S[l, "tab_ok"], 2 + j)
                        ins = V.tensor_reduce(rs[:, 40 + 10 * j:50 + 10 * j], ra[j].rearrange("p (h d) -> p h d", d=AD), AX.X, ALU.add)
                    link(ins)
                    link(V.tensor_scalar(rs[:, 60:80], rs[:, 40:60], 1.0 / AD, EPS, ALU.mult, ALU.add))
                    rsqrt(rs[:, 20:40], rs[:, 60:80], rs[:, 80:100], S[l, "qn_r"])
                    rope_att(dve, V, link, 0, S[l, "r0"])

                    def smax(hd):
                        dve.wait_ge(S[l, "s_mm"], hd + 1)
                        m = sq[:, 56 + 2 * (hd % 2):58 + 2 * (hd % 2)]
                        link(V.tensor_reduce(m, ps[hd % 2][:, :].rearrange("p (j s) -> p j s", j=2), AX.X, ALU.max))
                        V.tensor_scalar(sq[:, 48 + 2 * (hd % 2):50 + 2 * (hd % 2)], m, -float(AD) ** -0.5, None,
                                        ALU.mult).then_inc(S[l, "s_max"], 1)

                    smax(0)
                    for hd in range(AQ):
                        if hd + 1 < AQ:
                            smax(hd + 1)
                        dve.wait_ge(S[l, "s_e"], 2 * hd + 2)
                        link(V.reciprocal(rs[:, 100:102], sq[:, 52 + 2 * (hd % 2):54 + 2 * (hd % 2)]))
                        for j in range(TT):
                            V.tensor_scalar(prob[hd % 2][:, j, :], prob[hd % 2][:, j, :], rs[:, 100 + j:101 + j], None,
                                            ALU.mult).then_inc(S[l, "p_ok"], 1)
                        dve.wait_ge(S[l, "o_hi"], hd + 1)
                        V.tensor_tensor(feat[:, 8 + hd, :], ps[4 + hd % 2][:, 0:SEQ], feat[:, hd, :].bitcast(F32),
                                        ALU.subtract).then_inc(S[l, "o_lo"], 1)
                        dve.wait_ge(S[l, "p_ok"], 2 * hd + 2)
                    for u in range(ATT_OUT_UNITS):
                        splitn(n0 + 2 * ATT_GROUPS + u + 2)
                    post(s)
                else:
                    dve.wait_ge(S[l, "lg_e"], 1)
                    V.tensor_scalar(lg[:, 16:24], lg[:, 8:16], -1.0, 1.0, ALU.mult, ALU.add).then_inc(S[l, "lg_e"], 1)
                    dve.wait_ge(S[l, "lg_e"], 3)
                    link(V.tensor_scalar(lg[:, 32:40], lg[:, 16:24], 1.0, None, ALU.is_equal))
                    V.tensor_tensor(lg[:, 40:48], lg[:, 24:32], lg[:, 32:40], ALU.add)
                    link(V.scalar_tensor_tensor(out=lg[:, 48:56], in0=lg[:, 16:24], scalar=-1.0, in1=lg[:, 32:40], op0=ALU.add, op1=ALU.add))
                    link(V.reciprocal(lg[:, 48:56], lg[:, 48:56]))
                    link(V.scalar_tensor_tensor(out=lg[:, 48:56], in0=lg[:, 48:56], scalar=-1.0, in1=lg[:, 8:16], op0=ALU.mult, op1=ALU.mult))
                    link(V.tensor_tensor(lg[:, 56:64], lg[:, 48:56], lg[:, 40:48], ALU.mult))
                    for hd in range(RH):
                        link(V.tensor_scalar(drow, tabR[:, T_AHEAD:T_AHEAD + 512].rearrange("p (j t) -> p j t", j=2),
                                             lg[:, 56 + hd:57 + hd], None, ALU.mult))
                        V.scalar_tensor_tensor(out=dec[:, hd, :, :], in0=tabR[:, T_BEHIND:T_BEHIND + 512].rearrange("p (j t) -> p j t", j=2),
                                               scalar=lg[:, 60 + hd:61 + hd], in1=drow, op0=ALU.mult,
                                               op1=ALU.add).then_inc(S[l, "d_pre"], 1)
                        dve.wait_ge(S[l, "d_pre"], hd + 1)

                    def scored(hd):
                        dve.wait_ge(S[l, "s_mm"], hd + 1)
                        dve.wait_ge(S[l, "d_e"], hd + 1)
                        if hd >= 2:
                            dve.wait_ge(S[l, "y_mm"], hd - 1)
                        V.scalar_tensor_tensor(out=wt[hd % 2], in0=ps[6 + hd % 2][:, :].rearrange("p (j t) -> p j t", j=2),
                                               scalar=float(RQK) ** -0.5, in1=dec[:, hd, :, :], op0=ALU.mult,
                                               op1=ALU.mult).then_inc(S[l, "s_w"], 1)

                    for q in range(RET_GROUPS):
                        splitn(n0 + 2 * q + 2)
                        if q < 4:
                            dve.wait_ge(S[l, "qk_raw"], 2 * q + 1)
                            if q >= 1:
                                dve.wait_ge(S[l, "qk_t"], 2 * q)
                            V.tensor_tensor(rA[:, 0, :].rearrange("p (h d) -> p h d", h=2), rraw[:, 0, :].rearrange("p (h d) -> p h d", h=2),
                                            tabR[:, T_COSR:T_COSR + 256].unsqueeze(1).to_broadcast([P, 2, 256]), ALU.mult)
                            s5 = rraw[:, 0, :].rearrange("p (h r d) -> p h r d", h=4, r=2)
                            o5 = rB[:, 0, :].rearrange("p (h r d) -> p h r d", h=4, r=2)
                            sn = tabR[:, T_SINR:T_SINR + 256].rearrange("p (a r d) -> p a r d", a=2, r=2)
                            for hd in range(2):
                                for r_ in range(2):
                                    ins = V.tensor_tensor(o5[:, 2 * hd:2 * hd + 2, r_, :], s5[:, 2 * hd:2 * hd + 2, 1 - r_, :],
                                                          sn[:, :, r_, :], ALU.mult)
                            link(ins)
                            V.tensor_tensor(rA[:, 0, :], rA[:, 0, :], rB[:, 0, :], ALU.add).then_inc(S[l, "r0"], 1)
                        elif q % 2 == 0:
                            scored((q - 4) // 2)
                        splitn(n0 + 2 * q + 3)
                        if q >= 4 and q % 2:
                            hd = (q - 4) // 2
                            dve.wait_ge(S[l, "y_sq"], 2 * hd + 2)
                            link(V.tensor_scalar(rs[:, 104:106], sq[:, 32:34], 1.0 / RV, EPS, ALU.mult, ALU.add))
                            rsqrt(rs[:, 106:108], rs[:, 104:106], rs[:, 108:110])
                            for j in range(TT):
                                V.scalar_tensor_tensor(out=vr[:, j, RV * hd:RV * hd + RV], in0=ps[4 + j][:, :], scalar=rs[:, 106 + j:107 + j],
                                                       in1=sg[:, j, RV * hd:RV * hd + RV], op0=ALU.mult, op1=ALU.mult).then_inc(S[l, "y_g"], 1)
                            dve.wait_ge(S[l, "y_g"], 2 * hd + 2)
                    for u in range(RET_OUT_UNITS):
                        dve.wait_ge(S[l, "y_hi"], u + 1)
                        V.tensor_tensor(feat[:, 16 + 2 * u:18 + 2 * u, :], ps[4 + u % 4][:, :].rearrange("p (a t) -> p a t", a=2),
                                        feat[:, 2 * u:2 * u + 2, :].bitcast(F32), ALU.subtract).then_inc(S[l, "y_lo"], 1)
                        if u >= 1:
                            splitn(n0 + 2 * RET_GROUPS + u + 1)
                    splitn(n0 + 2 * RET_GROUPS + RET_OUT_UNITS + 1)
                    post(s)

                s += 1
                n0 = FIRST_UNIT[s]
                q0 = n0 // 2
                prep(s)

                def square(st, b, static):
                    dve.wait_ge(S[l, "relu"], st + 1)
                    if not static or st >= 1:
                        dve.wait_ge(S[l, "a_lo"], st)
                    V.tensor_tensor(aa, rl[b], rl[b], ALU.mult).then_inc(S[l, "sqr"], 1)
                    dve.wait_ge(S[l, "sqr"], st + 1)
                    dve.wait_ge(S[l, "a_hi"], st + 1)
                    V.tensor_tensor(feat[:, 4 * b + 2:4 * b + 4, :], aa.rearrange("p (a t) -> p a t", a=2),
                                    feat[:, 4 * b:4 * b + 2, :].bitcast(F32), ALU.subtract).then_inc(S[l, "a_lo"], 1)

                square(0, 0, True)
                splitn(n0 + 2)
                square(1, 1, True)
                splitn(n0 + 3)
                with dve.Fori(0, MLP_STEPS // 2 - 1) as it:
                    for b in range(2):
                        q = q0 + 1 + it * 2 + b
                        split(q + 1, 0)
                        square(it * 2 + 2 + b, b, False)
                        split(q + 1, 1)
                splitn(n0 + MLP_UNITS)
                splitn(n0 + MLP_UNITS + 1)
                post(s)

        @block.tensor
        def _(pe):
            mm = nc.tensor.matmul
            TP = nc.tensor.transpose

            def token_major(q, par_, lhs_hi, lhs_lo, banks, first, k0, nk, width, order=None, static=True, on_first_tile=None):
                cn = width // 512
                for hf in range(2):
                    slot = 2 * par_ + hf
                    pe.wait_ge(lo_done, 4 * q + 2 * par_ + hf + 1)
                    for j in range(TT):
                        for k in range(nk):
                            kk = k0 + hf * nk + k
                            tk = slice(j * P, (j + 1) * P)
                            st = first and hf == 0 and k == 0
                            for c in range(cn):
                                cs = slice(k * width + 512 * c, k * width + 512 * c + 512)
                                o = ps[banks[j * cn + c]][:, :]
                                mm(o, lhs_hi(kk)[:, tk], whi[:, slot, cs], start=st, stop=False, skip_group_check=True)
                                ins = mm(o, lhs_hi(kk)[:, tk], wlo[:, slot, cs], start=False, stop=False, skip_group_check=True)
                            for c in range(cn):
                                cs = slice(k * width + 512 * c, k * width + 512 * c + 512)
                                ins = mm(ps[banks[j * cn + c]][:, :], lhs_lo(kk)[:, tk], whi[:, slot, cs],
                                         start=False, stop=True, skip_group_check=True)
                        if on_first_tile is not None and hf == 1 and j == 0:
                            ins.then_inc(on_first_tile, 1)
                    ins.then_inc(w_used, 1)

            def feature_major(q, par_, bank):
                for hf in range(2):
                    slot = 2 * par_ + hf
                    pe.wait_ge(lo_done, 4 * q + 2 * par_ + hf + 1)
                    for f in range(2):
                        o = ps[bank][:, f * SEQ:(f + 1) * SEQ]
                        for k in range(4):
                            ws = slice(k * 256 + f * P, k * 256 + f * P + P)
                            kk = 4 * hf + k
                            mm(o, whi[:, slot, ws], feat[:, HT_HI + kk, :], start=(hf == 0 and f == 0 and k == 0), stop=False, skip_group_check=True)
                            mm(o, whi[:, slot, ws], feat[:, HT_LO + kk, :], start=False, stop=False, skip_group_check=True)
                            ins = mm(o, wlo[:, slot, ws], feat[:, HT_HI + kk, :], start=False, stop=True, skip_group_check=True)
                    ins.then_inc(w_used, 1)

            ht = (lambda k: feat[:, HT_HI + k, :]), (lambda k: feat[:, HT_LO + k, :])

            def prep(s):
                for j in range(TT):
                    pe.wait_ge(h_done, 2 * s + j + 1)
                    for c in range(2):
                        for k in range(4):
                            ins = TP(ps[4 + 2 * j + c][:, k * P:(k + 1) * P], h[:, j, (4 * c + k) * P:(4 * c + k + 1) * P], ident)
                        ins.then_inc(h_t, 1)

            def project(s, n, units, lhs_hi, lhs_lo, ready, per):
                for u in range(units):
                    pe.wait_ge(ready, per * (u + 1))
                    token_major((n + u) // 2, (n + u) % 2, lhs_hi, lhs_lo, (0, 1, 2, 3), u == 0, 2 * u, 1, D_MODEL,
                                on_first_tile=acc0 if u == units - 1 else None)

            pe.wait_ge(const_in, 16)
            pe.wait_ge(rows_in, 16 * 8)
            for i in range(2):
                TP(ps[0][:, 256 * i:256 * i + 96], view(tmp, 256 * i, P)[0:96, :], ident[0:96, 0:96])
                ins = TP(ps[0][:, 256 * i + 128:256 * i + 240], view(tmp, 256 * i + 128, P)[0:112, :], ident[0:112, 0:112])
            ins.then_inc(set_t, 1)

            for l in range(DEPTH):
                kind, s, n0 = l % 3, 2 * l, FIRST_UNIT[2 * l]
                i = l // 3
                prep(s)
                pe.wait_ge(h_lo, 4 * s + 4)
                if kind == 0:
                    pe.wait_ge(lo_done, 1)
                    for j in range(TT):
                        o = ps[2][:, 64 * j:64 * j + 64]
                        tk = slice(j * P, (j + 1) * P)
                        for k in range(KD):
                            ks = slice(64 * k, 64 * k + 64)
                            mm(o, feat[:, HT_HI + k, tk], wdt_hi[:, i, ks], start=(k == 0), stop=False)
                            mm(o, feat[:, HT_HI + k, tk], wdt_lo[:, i, ks], start=False, stop=False)
                            ins = mm(o, feat[:, HT_LO + k, tk], wdt_hi[:, i, ks], start=False, stop=(k == KD - 1))
                    ins.then_inc(S[l, "dt_mm"], 1)

                    def x_transposes(u):
                        pe.wait_ge(S[l, "conv_y"], 2 * u + 2)
                        if u >= 2:
                            pe.wait_ge(S[l, "x_tok"], u - 1)
                        for j in range(TT):
                            for cc in range(2):
                                ins = TP(ps[6 + u % 2][:, 256 * j + P * cc:256 * j + P * cc + P], xc[u % 4][:, cc, j * P:(j + 1) * P], ident)
                        ins.then_inc(S[l, "x_t"], 1)

                    for u in range(XBC_UNITS):
                        if u >= 2:
                            pe.wait_ge(S[l, "conv_in"], u - 1)
                        feature_major((n0 + u) // 2, (n0 + u) % 2, 4 + u % 2)
                        if u == 0:
                            dAv = dts[:, 1, :].rearrange("p (j d h) -> p j d h", j=2, d=2)
                            pe.wait_ge(S[l, "dt_ok"], 2)
                            for b, (m, j, fb) in enumerate(((fromon, 0, 1), (upto, 1, 0), (after, 0, 0), (before, 1, 1))):
                                ins = mm(ps[3][:, 32 * b:32 * b + 32], m, dAv[:, j, fb, :], start=True, stop=True)
                            ins.then_inc(S[l, "pre_mm"], 1)
                        if 2 <= u < 10:
                            x_transposes(u - 2)
                    pe.wait_ge(S[l, "pre_e"], 1)
                    for u in range(Z_UNITS):
                        n = n0 + XBC_UNITS + u
                        if u >= 4:
                            pe.wait_ge(S[l, "z_ok"], 2 * (u // 2 - 1))
                        token_major(n // 2, n % 2, *ht, (2 * (u // 2 % 2), 2 * (u // 2 % 2) + 1), u % 2 == 0, 4 * (u % 2), 2, 512)

                    def seg(g):
                        if g == 0:
                            pe.wait_ge(S[l, "conv_y"], 2 * XBC_UNITS)
                        else:
                            pe.wait_ge(S[l, "cb_ok"], 3 * g)
                        for a in range(2):
                            for j in range(TT):
                                src = j if a == 0 else 1 - j
                                ins = mm(ps[4][:, 256 * a + P * j:256 * a + P * j + P], BT[:, g, src * P:(src + 1) * P],
                                         CT[:, g, j * P:(j + 1) * P], start=True, stop=True)
                        ins.then_inc(S[l, "cb_mm"], 1)
                        for j in range(TT):
                            pe.wait_ge(S[l, "mf_ok"], 4 * g + 2 * j + 2)
                            if g >= 1:
                                pe.wait_ge(S[l, "seg_e"], 2 * (g - 1) + j + 1)
                            mm(ps[5 + j][:, :], after, MF[0][:, j, :], start=True, stop=False)
                            mm(ps[5 + j][:, :], before, MF[1][:, j, :], start=False, stop=True).then_inc(S[l, "seg_mm"], 1)

                    def y_transposes(g):
                        pe.wait_ge(S[l, "y_g"], g + 1)
                        if g >= 1:
                            pe.wait_ge(S[l, "y_lo"], 2 * g)
                        for kk in range(2):
                            for j in range(TT):
                                ins = TP(ps[7][:, 256 * kk + P * j:256 * kk + P * j + P], YT[2][:, j, P * kk:P * kk + P], ident)
                        ins.then_inc(S[l, "y_t"], 1)

                    pe.wait_ge(S[l, "z_ok"], 8)
                    seg(0)
                    for g in range(SSM_GROUPS):
                        if g + 1 < SSM_GROUPS:
                            seg(g + 1)
                        pe.wait_ge(S[l, "w_ok"], 4 * g + 4)
                        pe.wait_ge(S[l, "xs_ok"], 6 * g + 6)
                        if g >= 2:
                            pe.wait_ge(S[l, "y_v"], g - 1)
                        for j in range(TT):
                            for hd in range(HPG):
                                o = ps[2 + g % 2][:, 256 * j + SSM_HDIM * hd:256 * j + SSM_HDIM * (hd + 1)]
                                for fb in range(2):
                                    mm(o, WM[fb][:, j, P * hd:P * hd + P], XS[fb][:, j, SSM_HDIM * hd:SSM_HDIM * (hd + 1)],
                                       start=(fb == 0), stop=(fb == 1))
                        for j in range(TT):
                            ins = mm(ps[g % 2][:, 256 * j:256 * j + 256], CBM[:, 2, j, :], XS[2][:, 1 - j, :], start=True, stop=True)
                        ins.then_inc(S[l, "y_mm"], 1)
                        if g >= 1:
                            y_transposes(g - 1)
                    y_transposes(SSM_GROUPS - 1)
                    pe.wait_ge(S[l, "y_v"], SSM_GROUPS)
                    project(s, n0 + XBC_UNITS + Z_UNITS, SSM_OUT_UNITS, lambda k: feat[:, k, :], lambda k: feat[:, 16 + k, :],
                            S[l, "y_lo"], 2)
                elif kind == 1:
                    for u in range(2 * ATT_GROUPS):
                        token_major((n0 + u) // 2, (n0 + u) % 2, *ht, (2 * (u // 2), 2 * (u // 2) + 1), u % 2 == 0, 4 * (u % 2), 2, 512)
                    pe.wait_ge(S[l, "r0"], 1)
                    pe.wait_ge(S[l, "r1"], 1)
                    for c in range(5):
                        if c >= 2:
                            pe.wait_ge(S[l, "qk_in"], c - 1)
                        for b in range(2):
                            for j in range(TT):
                                ins = TP(ps[6 + c % 2][:, 256 * b + P * j:256 * b + P * j + P], qkv[:, j, P * (2 * c + b):P * (2 * c + b + 1)], ident)
                        ins.then_inc(S[l, "qk_t"], 1)

                    def scores(hd):
                        if hd >= 2:
                            pe.wait_ge(S[l, "s_e"], 2 * (hd - 1))
                        for j in range(TT):
                            ins = mm(ps[hd % 2][:, j * SEQ:(j + 1) * SEQ], qkT[:, hd, j * P:(j + 1) * P], qkT[:, AQ + hd // 4, :],
                                     start=True, stop=True)
                        ins.then_inc(S[l, "s_mm"], 1)

                    pe.wait_ge(S[l, "qk_in"], 5)
                    scores(0)
                    for hd in range(AQ):
                        if hd + 1 < AQ:
                            scores(hd + 1)
                        pe.wait_ge(S[l, "p_ok"], 2 * hd + 2)
                        if hd >= 2:
                            pe.wait_ge(S[l, "p_in"], hd - 1)
                        for b in range(2):
                            for j in range(TT):
                                ins = TP(ps[2 + hd % 2][:, 256 * b + P * j:256 * b + P * j + P], prob[hd % 2][:, j, P * b:P * b + P], ident)
                        ins.then_inc(S[l, "p_t"], 1)
                        pe.wait_ge(S[l, "p_in"], hd + 1)
                        if hd >= 2:
                            pe.wait_ge(S[l, "o_lo"], hd - 1)
                        vo = AQ * AD + AKV * AD + AD * (hd // 4)
                        for b in range(2):
                            ins = mm(ps[4 + hd % 2][:, 0:SEQ], qkv[:, b, vo:vo + AD], probT[hd % 2][:, b, :], start=(b == 0), stop=(b == 1))
                        ins.then_inc(S[l, "o_mm"], 1)
                    project(s, n0 + 2 * ATT_GROUPS, ATT_OUT_UNITS, lambda k: feat[:, k, :], lambda k: feat[:, 8 + k, :], S[l, "o_lo"], 2)
                else:
                    def rope_transposes(q):
                        pe.wait_ge(S[l, "r0"], q + 1)
                        pe.wait_ge(S[l, "r1"], q + 1)
                        for b in range(2):
                            if q >= 1:
                                pe.wait_ge(S[l, "qk_in"], 2 * q - 1 + b)
                            for a in range(2):
                                for j in range(TT):
                                    c = P * (2 * b + a)
                                    ins = TP(ps[4 + b][:, 256 * a + P * j:256 * a + P * j + P], rA[:, j, c:c + P], ident)
                            ins.then_inc(S[l, "qk_t"], 1)

                    def scores(hd):
                        if hd >= 2:
                            pe.wait_ge(S[l, "s_w"], hd - 1)
                        for b in range(TT):
                            for k in range(2):
                                ins = mm(ps[6 + hd % 2][:, b * SEQ:(b + 1) * SEQ], rT[:, 8 + 2 * hd + k, b * P:(b + 1) * P], rT[:, 2 * hd + k, :],
                                         start=(k == 0), stop=(k == 1))
                        ins.then_inc(S[l, "s_mm"], 1)

                    def y_head(hd):
                        pe.wait_ge(S[l, "s_w"], hd + 1)
                        pe.wait_ge(S[l, "v_in"], 2 * hd + 2)
                        if hd == 0:
                            pe.wait_ge(S[l, "qk_in"], 8)
                        else:
                            pe.wait_ge(S[l, "y_g"], 2 * hd)
                        for j in range(TT):
                            for b in range(TT):
                                ins = mm(ps[4 + j][:, :], wt[hd % 2][:, b, j * P:(j + 1) * P], vr[:, b, RV * hd:RV * hd + RV],
                                         start=(b == 0), stop=(b == 1))
                        ins.then_inc(S[l, "y_mm"], 1)

                    for q in range(RET_GROUPS):
                        for hf in range(2):
                            n = n0 + 2 * q + hf
                            if q >= 2 and hf == 0:
                                if q < 6:
                                    pe.wait_ge(S[l, "qk_raw"], 2 * (q - 1))
                                elif q % 2 == 0:
                                    pe.wait_ge(S[l, "v_in"], 2 * ((q - 6) // 2 + 1))
                                else:
                                    pe.wait_ge(S[l, "g_in"], 2 * ((q - 6) // 2 + 1))
                            token_major(n // 2, n % 2, *ht, (2 * (q % 2), 2 * (q % 2) + 1), hf == 0, 4 * hf, 2, 512)
                            if hf == 0 and 1 <= q <= 4:
                                rope_transposes(q - 1)
                            if hf == 0 and q >= 5 and q % 2:
                                y_head((q - 5) // 2)
                            if hf == 1 and q >= 4 and q % 2 == 0:
                                if q == 4:
                                    pe.wait_ge(S[l, "qk_in"], 8)
                                scores((q - 4) // 2)

                    def y_transposes(u):
                        pe.wait_ge(S[l, "y_g"], 2 * (u // 2) + 2)
                        if u < 2:
                            pe.wait_ge(S[l, "y_g"], 8)
                        if u >= 4:
                            pe.wait_ge(S[l, "y_lo"], u - 3)
                        for a in range(2):
                            for j in range(TT):
                                c = P * (2 * u + a)
                                ins = TP(ps[4 + u % 4][:, 256 * a + P * j:256 * a + P * j + P], vr[:, j, c:c + P], ident)
                        ins.then_inc(S[l, "y_t"], 1)

                    for u in range(3):
                        y_transposes(u)
                    pe.wait_ge(S[l, "g_in"], 8)
                    for u in range(RET_OUT_UNITS):
                        pe.wait_ge(S[l, "y_lo"], u + 1)
                        n = n0 + 2 * RET_GROUPS + u
                        token_major(n // 2, n % 2, lambda k: feat[:, k, :], lambda k: feat[:, 16 + k, :], (0, 1, 2, 3), u == 0, 2 * u, 1,
                                    D_MODEL, on_first_tile=acc0 if u == RET_OUT_UNITS - 1 else None)
                        if u + 3 < RET_OUT_UNITS:
                            y_transposes(u + 3)

                s += 1
                n0 = FIRST_UNIT[s]
                q0 = n0 // 2
                prep(s)
                pe.wait_ge(h_lo, 4 * s + 4)

                def up(st, b, q, par_, static):
                    if not static or st >= 2:
                        pe.wait_ge(S[l, "relu"], st - 1)
                    feature_major(q, par_, 4 + b)

                def down(st, b, q, par_, first, last=False):
                    pe.wait_ge(S[l, "a_lo"], st + 1)
                    token_major(q, par_, lambda k: feat[:, 4 * b + k, :], lambda k: feat[:, 4 * b + 2 + k, :], (0, 1, 2, 3), first, 0, 1,
                                D_MODEL, on_first_tile=acc0 if last else None)

                up(0, 0, q0, 0, True)
                up(1, 1, q0, 1, True)
                down(0, 0, q0 + 1, 0, True)
                up(2, 0, q0 + 1, 1, True)
                with pe.Fori(0, MLP_STEPS // 2 - 2) as it:
                    for b in range(2):
                        t = it * 2 + 1 + b
                        down(t, 1 - b, q0 + 1 + t, 0, False)
                        up(t + 2, 1 - b, q0 + 1 + t, 1, False)
                down(MLP_STEPS - 3, 1, q0 + MLP_STEPS - 2, 0, False)
                up(MLP_STEPS - 1, 1, q0 + MLP_STEPS - 2, 1, True)
                down(MLP_STEPS - 2, 0, q0 + MLP_STEPS - 1, 0, False)
                down(MLP_STEPS - 1, 1, q0 + MLP_STEPS - 1, 1, False, last=True)


_INS = ["x", "norm_mix_pre", "norm_mix_post", "norm_ffn_pre", "norm_ffn_post", "mlp_w_in", "mlp_w_out",
        "ssm_w_in", "ssm_conv_w", "ssm_conv_b", "ssm_dt_bias", "ssm_a_log", "ssm_d", "ssm_norm", "ssm_w_out",
        "att_w_in", "att_q_norm", "att_k_norm", "att_w_out", "ret_w_in", "ret_log2_decay", "ret_w_out"]


def kernel(**inputs):
    import concourse.bacc as _bacc
    from concourse.bass_utils import run_bass_kernel_spmd as _run

    nc = _bacc.Bacc("TRN2", target_bir_lowering=False, num_devices=1)
    arrays, aps = {}, {}
    for name in _INS:
        a = np.ascontiguousarray(inputs[name])
        arrays[f"in_{name}"] = a
        aps[name] = nc.dram_tensor(f"in_{name}", a.shape, F32, kind="ExternalInput").ap()
    extra = []
    for name, a in zip(("consts", "tab_a", "tab_r"), shape_constants()):
        arrays[f"in_{name}"] = a
        extra.append(nc.dram_tensor(f"in_{name}", a.shape, F32, kind="ExternalInput").ap())
    out = nc.dram_tensor("out_x", (1, SEQ, D_MODEL), F32, kind="ExternalOutput").ap()
    build(nc, aps, *extra, out)
    r = _run(nc, [arrays], core_ids=[0])
    return r.results[0]["out_x"]
```

```python
from contextlib import ExitStack

import numpy as np

import concourse.bass as bass
from concourse import mybir

ALU = mybir.AluOpType
ACT = mybir.ActivationFunctionType
AX = mybir.AxisListType
F32 = mybir.dt.float32
F32R = mybir.dt.float32r
I32 = mybir.dt.int32

P = 128
D_MODEL, SEQ, DEPTH = 1024, 256, 4
TT = SEQ // P
KD = D_MODEL // P
EPS = 1e-6
D_FF = 4 * D_MODEL
SSM_INNER, SSM_HEADS, SSM_HDIM, SSM_GROUPS, SSM_STATE, SSM_CONV = 2048, 32, 64, 8, 128, 5
HPG = SSM_HEADS // SSM_GROUPS
CONV_DIM = SSM_INNER + 2 * SSM_GROUPS * SSM_STATE
CT_N = CONV_DIM // P
PAD = SSM_CONV // 2
AQ, AKV, AD = 8, 2, 128
RH, RQK, RV = 4, 256, 512
GRID_W, ROPE_THETA = 64, 10000.0
SSM_LAYERS = [l for l in range(DEPTH) if l % 3 == 0]

UNIT = 2048
HALF = UNIT // 2
XBC_UNITS = CONV_DIM // 256
Z_UNITS = 2 * SSM_INNER // 512
SSM_OUT_UNITS = SSM_INNER // 256
ATT_GROUPS = (AQ + 2 * AKV) * AD // 512
ATT_OUT_UNITS = AQ * AD // 256
RET_GROUPS = 6 * D_MODEL // 512
RET_OUT_UNITS = 2 * D_MODEL // 256
MLP_STEPS = D_FF // 256
MLP_UNITS = 2 * MLP_STEPS
MIX_UNITS = {0: XBC_UNITS + Z_UNITS + SSM_OUT_UNITS, 1: 2 * ATT_GROUPS + ATT_OUT_UNITS,
             2: 2 * RET_GROUPS + RET_OUT_UNITS}
FIRST_UNIT = []
_n = 0
for _l in range(DEPTH):
    FIRST_UNIT += [_n, _n + MIX_UNITS[_l % 3]]
    _n += MIX_UNITS[_l % 3] + MLP_UNITS
N_UNITS = _n

C_ID, C_LE, C_GT, C_GE, C_LT = (P * i for i in range(5))
N_CONST = 5 * P
T_COSA, T_SINA = 0, 256
N_TABA = 512
T_COSR, T_SINR, T_AHEAD, T_BEHIND = 0, 512, 1024, 1536
N_TABR = 2048


def rope_tables(dim):
    rows = SEQ // GRID_W
    row = np.repeat(np.arange(rows, dtype=np.float32), GRID_W)
    col = np.tile(np.arange(GRID_W, dtype=np.float32), rows)
    half = dim // 2
    nf = half // 2
    inv = np.float32(ROPE_THETA) ** (-(np.arange(nf, dtype=np.float32) * np.float32(2)) / np.float32(half))
    ang = np.stack([row[:, None] * inv, col[:, None] * inv], axis=1).astype(np.float32)
    c, s = np.cos(ang), np.sin(ang)
    cos = np.stack([c, c], axis=2).reshape(TT, P, dim)
    sin = np.stack([-s, s], axis=2).reshape(TT, P, dim)
    return [a.transpose(1, 0, 2).reshape(P, TT * dim).astype(np.float32) for a in (cos, sin)]


def shape_constants():
    a = np.arange(P)
    k, t = a[:, None], a[None, :]
    base = np.concatenate([k == t, k <= t, k > t, k >= t, k < t], axis=1).astype(np.float32)
    tab_a = np.concatenate(rope_tables(AD), axis=1)
    s = (np.arange(TT)[None, :, None] * P + a[:, None, None])
    diff = (np.arange(SEQ)[None, None, :] - s).astype(np.float32)
    tab_r = np.concatenate(rope_tables(RQK) + [np.maximum(diff, 0).reshape(P, -1),
                                               np.maximum(-diff, 0).reshape(P, -1)], axis=1)
    return base, tab_a, tab_r.astype(np.float32)


def build(nc, w, consts, tab_a, tab_r, out):
    ctx = ExitStack()
    with ctx:
        def sb(name, shape, dt=F32):
            return ctx.enter_context(nc.sbuf_tensor(name, [P] + list(shape), dt))

        def sem(name):
            return ctx.enter_context(nc.semaphore(name))

        raw = sb("raw", [2, UNIT])
        whi = sb("whi", [4, HALF], F32R)
        wlo = sb("wlo", [4, HALF], F32R)
        feat = sb("feat", [32, SEQ], F32R)
        x = sb("x", [TT, D_MODEL])
        h = sb("h", [TT, D_MODEL])
        big = sb("big", [12288])
        tmp = sb("tmp", [9472])
        gain = sb("gain", [2, D_MODEL])
        cst = sb("cst", [N_CONST])
        cols = sb("cols", [2, 208])
        par = sb("par", [2, 160])
        negA = sb("negA", [2, 64])
        wdt_hi = sb("wdt_hi", [2, 512], F32R)
        wdt_lo = sb("wdt_lo", [2, 512], F32R)
        sq = sb("sq", [64])
        rs = sb("rs", [128])
        dts = sb("dts", [2, P])
        fac = sb("fac", [4, 32])
        srcf = sb("srcf", [2, 32])
        lg = sb("lg", [64])
        pacc = ctx.enter_context(nc.psum_tensor("pacc", [P, 4 * 512], F32))
        ps = [pacc[:, 512 * i:512 * i + 512] for i in range(4)]
        ps += [ctx.enter_context(nc.psum_tensor(f"ps{i}", [P, 512], F32)) for i in range(4, 8)]
        ecol = sb("ecol", [8])

        ident = cst[:, C_ID:C_ID + P]
        upto, after, fromon, before = (cst[:, c:c + P] for c in (C_LE, C_GT, C_GE, C_LT))
        HT_HI, HT_LO = 16, 24
        Y_LO = {0: 16, 1: 8, 2: 16}

        raw_in = [sem("raw_in0"), sem("raw_in1")]
        hi_done, lo_done, w_used = sem("hi_done"), sem("lo_done"), sem("w_used")
        x_in = [sem("x_in0"), sem("x_in1")]
        const_in, rows_in, par_in = sem("const_in"), sem("rows_in"), sem("par_in")
        gain_in = [sem("gain_in0"), sem("gain_in1")]
        tab_in = sem("tab_in")
        out_done = sem("out_done")
        set_t, set_e, set_a, set_w = sem("set_t"), sem("set_e"), sem("set_a"), sem("set_w")
        x_sq, h_done, h_t, h_hi, h_lo = sem("x_sq"), sem("h_done"), sem("h_t"), sem("h_hi"), sem("h_lo")
        acc0, m_sq, x_done = sem("acc0"), sem("m_sq"), sem("x_done")
        x_root, m_root, x_own, eps_set = sem("x_root"), sem("m_root"), sem("x_own"), sem("eps_set")
        chain = sem("chain")
        pchain = sem("pchain")
        S = {}
        for l in range(DEPTH):
            names = {0: "pad_ok dt_mm dt_abs dt_u dt_ok pre_mm pre_e conv_in conv0 conv1 conv_y x_t x_tok z_ok cb_mm cb_ok "
                        "mff_ok mfb_ok cd_ok seg_mm seg_e w_ok xs_ok xd_ok y_mm y_v y_g y_sq y_t y_hi y_lo",
                     1: "qkv_in tab_ok qn_r r0 r1 qk_t qk_in s_mm s_max s_e p_ok p_t p_in o_mm o_hi o_lo",
                     2: "lg_e d_pre d_e qk_raw r0 r1 qk_t qk_in v_in g_in s_mm s_w y_mm y_sq y_g y_t y_hi y_lo"}[l % 3]
            for nm in (names + " relu sqr a_hi a_lo").split():
                S[l, nm] = sem(f"l{l}_{nm}")

        def view(buf, at, *shape):
            n = int(np.prod(shape))
            v = buf[:, at:at + n]
            if len(shape) == 2:
                return v.rearrange("p (a b) -> p a b", b=shape[1])
            if len(shape) == 3:
                return v.rearrange("p (a b c) -> p a b c", b=shape[1], c=shape[2])
            return v

        junk = sb("junk", [D_MODEL], mybir.dt.bfloat16)
        dtw = h[:, 0, 0:7 * P].rearrange("p (a b) -> p a b", b=P)
        dt_feat = h[:, 1, 0:SEQ]
        xtok = view(big, 0, TT, SSM_INNER)
        BT, CT = view(big, 4096, SSM_GROUPS, SEQ), view(big, 6144, SSM_GROUPS, SEQ)
        sz = view(big, 8192, TT, SSM_INNER)
        CW = SEQ + 2 * PAD
        cpad = [view(tmp, 2 * CW * i, 2, CW) for i in range(2)]
        cacc = [view(tmp, 4 * CW + 512 * i, 2, SEQ) for i in range(2)]
        xc = [view(tmp, 4 * CW + 1024 + 512 * i, 2, SEQ) for i in range(4)]
        prod = view(tmp, 4 * CW + 3072, SSM_CONV, SEQ)
        MF = [view(tmp, 1024 * fb, TT, 512) for fb in range(2)]
        EX = view(tmp, 2048, TT, 512)
        CD = view(tmp, 3072, TT, 512)
        WM = [view(tmp, 4096, TT, 512), h[:, 0, :].rearrange("p (a b) -> p a b", b=512)]
        CBM = view(tmp, 5120, 2, TT, P)
        CBX = [view(tmp, 5632, TT, P), view(tmp, 8448, TT, P)]
        YT = [view(tmp, 5888 + 512 * i, TT, 256) for i in range(3)]
        XD = view(tmp, 7424, TT, 256)
        XS = [view(tmp, 7936, TT, 256), h[:, 1, 0:512].rearrange("p (a b) -> p a b", b=256)]
        qkv = view(big, 0, TT, 1536)
        qkT = view(big, 3072, 10, SEQ)
        prob = [view(big, 5632 + 512 * i, TT, SEQ) for i in range(2)]
        probT = [view(big, 6656 + 512 * i, TT, SEQ) for i in range(2)]
        tabA = view(tmp, 0, N_TABA)
        gq = view(tmp, 512, 256)
        tw = view(tmp, 768, 4, TT, AD)
        ra = [view(tmp, 1792 + 1280 * j, 1280) for j in range(2)]
        rb = [view(tmp, 4352 + 1280 * j, 1280) for j in range(2)]
        rT = view(big, 0, 16, SEQ)
        vr = view(big, 4096, TT, 4 * RV)
        sg = view(big, 8192, TT, 4 * RV)
        tabR = view(tmp, 0, N_TABR)
        dec = view(tmp, 2048, RH, TT, SEQ)
        rraw = view(tmp, 4096, TT, 512)
        rA, rB = view(tmp, 5120, TT, 512), view(tmp, 6144, TT, 512)
        wt = [view(tmp, 7168 + 512 * i, TT, SEQ) for i in range(2)]
        drow = view(tmp, 8192, TT, 256)
        rl = [view(tmp, 512 * i, 512) for i in range(2)]
        aa = view(tmp, 1024, 512)

        def rope_att(eng, ops, link, j, done):
            v = qkv[:, j, 0:1280].rearrange("p (h d) -> p h d", d=AD)
            r = rs[:, 20 + 10 * j:30 + 10 * j].unsqueeze(2).to_broadcast([P, 10, AD])
            link(ops.tensor_tensor(v, v, r, ALU.mult))
            for b, (h0, hn) in enumerate(((0, AQ), (AQ, AKV))):
                hv = v[:, h0:h0 + hn, :]
                ops.tensor_tensor(ra[j].rearrange("p (h d) -> p h d", d=AD)[:, h0:h0 + hn, :], hv,
                                  tw[:, 2 * b, j, :].unsqueeze(1).to_broadcast([P, hn, AD]), ALU.mult)
                src = hv.rearrange("p h (a r d) -> p h a r d", a=2, r=2)
                dst = rb[j].rearrange("p (h d) -> p h d", d=AD)[:, h0:h0 + hn, :].rearrange("p h (a r d) -> p h a r d", a=2, r=2)
                sn = tw[:, 2 * b + 1, j, :].rearrange("p (a r d) -> p a r d", a=2, r=2)
                for a in range(2):
                    for r_ in range(2):
                        ins = ops.tensor_tensor(dst[:, :, a, r_, :], src[:, :, a, 1 - r_, :],
                                                sn[:, a, r_, :].unsqueeze(1).to_broadcast([P, hn, AD // 4]), ALU.mult)
            link(ins)
            ops.tensor_tensor(qkv[:, j, 0:1280], ra[j], rb[j], ALU.add).then_inc(done, 1)

        def low_y(V, dve, l, i, g, kk):
            dve.wait_ge(S[l, "y_hi"], 2 * g + kk + 1)
            if kk == 0:
                dve.wait_ge(S[l, "y_hi"], 2 * g + 2)
            V.scalar_tensor_tensor(out=feat[:, 16 + 2 * g + kk, :], in0=ps[7][:, 256 * kk:256 * kk + 256],
                                   scalar=cols[:, i, 192 + 2 * g + kk:193 + 2 * g + kk],
                                   in1=feat[:, 2 * g + kk, :].bitcast(F32), op0=ALU.mult,
                                   op1=ALU.subtract).then_inc(S[l, "y_lo"], 1)

        block = ctx.enter_context(nc.Block())

        @block.sync
        def _(sp):
            def load(q, par_, src, static):
                if not static or q >= 1:
                    sp.wait_ge(lo_done, 4 * q + 2 * par_ - 2)
                dst = raw[:, par_, :]
                if len(src.shape) == 3:
                    dst = dst.rearrange("p (k n) -> p k n", k=src.shape[1])
                sp.dma_start(dst, src).then_inc(raw_in[par_], 16)

            def group_src(wm, c0, hf):
                return wm.rearrange("(k p) n -> p k n", p=P)[:, 4 * hf:4 * hf + 4, c0:c0 + 512]

            def rows_src(wm, u):
                return wm[256 * u:256 * u + 256, :].rearrange("(k p) n -> p k n", p=P)

            for j in range(TT):
                sp.dma_start(x[:, j, :], w["x"][0, j * P:(j + 1) * P, :]).then_inc(x_in[j], 16)
            sp.dma_start(cst[:, :], consts).then_inc(const_in, 16)
            for l in range(DEPTH):
                n = FIRST_UNIT[2 * l]
                kind, i = l % 3, l // 3
                srcs = []
                if kind == 0:
                    wi = w["ssm_w_in"][i]
                    for u in range(XBC_UNITS):
                        c0 = SSM_INNER + 256 * u
                        srcs.append(wi.rearrange("(k p) n -> p k n", p=P)[:, :, c0:c0 + 256])
                    srcs += [group_src(wi, 512 * (u // 2), u % 2) for u in range(Z_UNITS)]
                    srcs += [rows_src(w["ssm_w_out"][i], u) for u in range(SSM_OUT_UNITS)]
                elif kind == 1:
                    srcs += [group_src(w["att_w_in"][i], 512 * (u // 2), u % 2) for u in range(2 * ATT_GROUPS)]
                    srcs += [rows_src(w["att_w_out"][i], u) for u in range(ATT_OUT_UNITS)]
                else:
                    for q in range(RET_GROUPS):
                        c0 = 512 * q if q < 4 else 512 * (4 + (q - 4) // 2 + 4 * (q % 2))
                        srcs += [group_src(w["ret_w_in"][i], c0, hf) for hf in range(2)]
                    srcs += [rows_src(w["ret_w_out"][i], u) for u in range(RET_OUT_UNITS)]
                for u, src in enumerate(srcs):
                    load((n + u) // 2, (n + u) % 2, src, True)
                q0 = FIRST_UNIT[2 * l + 1] // 2
                w1 = w["mlp_w_in"][l].rearrange("(k p) f -> p k f", p=P)
                w2 = w["mlp_w_out"][l].rearrange("(s k p) n -> p s k n", p=P, k=2)
                load(q0, 0, w1[:, :, 0:256], True)
                load(q0, 1, w1[:, :, 256:512], True)
                with sp.Fori(0, MLP_STEPS // 2 - 1) as it:
                    for b in range(2):
                        load(q0 + 1 + it * 2 + b, 0, w2[:, bass.ds(it * 2 + b, 1), :, :].squeeze(1), False)
                        load(q0 + 1 + it * 2 + b, 1, w1[:, :, bass.ds(it * 512 + 512 + 256 * b, 256)], False)
                load(q0 + MLP_STEPS - 1, 0, w2[:, MLP_STEPS - 2, :, :], True)
                load(q0 + MLP_STEPS - 1, 1, w2[:, MLP_STEPS - 1, :, :], True)
            for j in range(TT):
                sp.wait_ge(x_done, TT * (2 * DEPTH - 1) + j + 1)
                sp.dma_start(out[0, j * P:(j + 1) * P, :], x[:, j, :]).then_inc(out_done, 16)
            sp.wait_ge(out_done, 32)

        @block.gpsimd
        def _(pool):
            steps = [0]

            def link(ins):
                steps[0] += 1
                ins.then_inc(pchain, 1)
                pool.wait_ge(pchain, steps[0])

            gain_rows = []
            for l in range(DEPTH):
                gain_rows += [w["norm_mix_pre"][l], w["norm_mix_post"][l], w["norm_ffn_pre"][l], w["norm_ffn_post"][l]]
            sent = [0]

            def send_gain():
                u = sent[0]
                if u >= len(gain_rows):
                    return
                sent[0] += 1
                if u >= 2:
                    pool.wait_ge(h_done if u % 2 == 0 else x_done, 2 * ((u - 2) // 2) + 2)
                pool.dma_start(gain[:, u % 2, :], gain_rows[u].partition_broadcast(P)).then_inc(gain_in[u % 2], 16)

            nc.gpsimd.memset(ecol[:, 0:1], EPS).then_inc(eps_set, 1)
            send_gain()
            send_gain()
            for i in range(len(SSM_LAYERS)):
                cw = w["ssm_conv_w"][i].rearrange("t (c p) -> (t c) p", p=P)
                r0, r1 = view(tmp, 256 * i, P), view(tmp, 256 * i + 128, P)
                pool.dma_start(r0[0:96, :], cw[0:96, :]).then_inc(rows_in, 16)
                pool.dma_start(r1[0:64, :], cw[96:160, :]).then_inc(rows_in, 16)
                pool.dma_start(r1[64:96, :], w["ssm_conv_b"][i].rearrange("(c p) -> c p", p=P)).then_inc(rows_in, 16)
                pool.dma_start(r1[96:112, :], w["ssm_norm"][i].rearrange("(c p) -> c p", p=P)).then_inc(rows_in, 16)
                pool.dma_start(par[:, i, 0:64], w["ssm_dt_bias"][i].rearrange("a h -> (a h)").partition_broadcast(P)).then_inc(par_in, 16)
                pool.dma_start(par[:, i, 64:128], w["ssm_a_log"][i].rearrange("a h -> (a h)").partition_broadcast(P)).then_inc(par_in, 16)
                pool.dma_start(par[:, i, 128:160], w["ssm_d"][i].partition_broadcast(P)).then_inc(par_in, 16)
                pool.dma_start(view(tmp, 512 + 512 * i, KD, 64),
                               w["ssm_w_in"][i][:, SSM_INNER + CONV_DIM:].rearrange("(k p) n -> p k n", p=P)).then_inc(par_in, 16)

            def rope_ret(l, q):
                pool.wait_ge(S[l, "qk_raw"], 2 * q + 2)
                if q >= 1:
                    pool.wait_ge(S[l, "qk_t"], 2 * q)
                src = rraw[:, 1, :].rearrange("p (h d) -> p h d", h=2)
                cosb = tabR[:, T_COSR + 256:T_COSR + 512].unsqueeze(1).to_broadcast([P, 2, 256])
                nc.gpsimd.tensor_tensor(rA[:, 1, :].rearrange("p (h d) -> p h d", h=2), src, cosb, ALU.mult)
                s5 = rraw[:, 1, :].rearrange("p (h r d) -> p h r d", h=4, r=2)
                o5 = rB[:, 1, :].rearrange("p (h r d) -> p h r d", h=4, r=2)
                sn = tabR[:, T_SINR + 256:T_SINR + 512].rearrange("p (a r d) -> p a r d", a=2, r=2)
                for hd in range(2):
                    for r in range(2):
                        ins = nc.gpsimd.tensor_tensor(o5[:, 2 * hd:2 * hd + 2, r, :], s5[:, 2 * hd:2 * hd + 2, 1 - r, :],
                                                      sn[:, :, r, :], ALU.mult)
                link(ins)
                nc.gpsimd.tensor_tensor(rA[:, 1, :], rA[:, 1, :], rB[:, 1, :], ALU.add).then_inc(S[l, "r1"], 1)

            for l in range(DEPTH):
                kind, i = l % 3, l // 3
                s = 2 * l
                send_gain()
                if kind == 0:
                    pool.wait_ge(h_done, 2 * s + 2)
                    for b in range(2):
                        nc.gpsimd.memset(cpad[b][:, :, 0:PAD], 0.0)
                        nc.gpsimd.memset(cpad[b][:, :, PAD + SEQ:CW], 0.0).then_inc(S[l, "pad_ok"], 1)
                    pool.wait_ge(S[l, "pad_ok"], 2)
                    for u in range(XBC_UNITS):
                        ct = 2 * u + 1
                        if u >= 1:
                            pool.wait_ge(S[l, "conv1"], u)
                        pool.wait_ge(S[l, "conv_in"], u + 1)
                        if u >= 2:
                            pool.wait_ge(S[l, "conv_y"], 2 * (u - 1))
                        src = cpad[u % 2][:, 1, 0:SEQ]
                        windows = bass.AP(tensor=src.tensor, offset=src.offset, ap=[src.ap[0], [1, SSM_CONV], [1, SEQ]])
                        taps = cols[:, i, ct:5 * CT_N:CT_N].unsqueeze(2).to_broadcast([P, SSM_CONV, SEQ])
                        link(nc.gpsimd.tensor_tensor(prod, windows, taps, ALU.mult))
                        link(nc.gpsimd.tensor_tensor(prod[:, 0:2, :], prod[:, 0:2, :], prod[:, 2:4, :], ALU.add))
                        link(nc.gpsimd.tensor_tensor(prod[:, 0, :], prod[:, 0, :], prod[:, 4, :], ALU.add))
                        nc.gpsimd.tensor_tensor(cacc[u % 2][:, 1, :], prod[:, 0, :], prod[:, 1, :],
                                                ALU.add).then_inc(S[l, "conv1"], 1)
                    pool.wait_ge(S[l, "dt_ok"], 2)
                    dA = dts[:, 1, :].rearrange("p (j d h) -> p j d h", j=2, d=2)
                    pool.wait_ge(S[l, "x_tok"], 8)
                    pool.wait_ge(S[l, "conv_y"], 2 * XBC_UNITS)
                    def exponents(g):
                        if g >= 1:
                            pool.wait_ge(S[l, "seg_mm"], 2 * g)
                        for j in range(TT):
                            nc.gpsimd.tensor_tensor(MF[1][:, j, :].rearrange("p (h t) -> p h t", h=HPG),
                                                    fromon.unsqueeze(1).to_broadcast([P, HPG, P]),
                                                    dA[:, j, 1, HPG * g:HPG * g + HPG].unsqueeze(2).to_broadcast([P, HPG, P]),
                                                    ALU.mult).then_inc(S[l, "mfb_ok"], 1)

                    def sources(g):
                        if g >= 2:
                            pool.wait_ge(S[l, "y_mm"], g - 1)
                        for j in range(TT):
                            ins = nc.gpsimd.tensor_tensor(XS[g % 2][:, j, :].rearrange("p (h d) -> p h d", h=HPG),
                                                          xtok[:, j, 256 * g:256 * g + 256].rearrange("p (h d) -> p h d", h=HPG),
                                                          srcf[:, j, HPG * g:HPG * g + HPG].unsqueeze(2).to_broadcast([P, HPG, SSM_HDIM]),
                                                          ALU.mult)
                        ins.then_inc(S[l, "xs_ok"], 1)

                    exponents(0)
                    pool.wait_ge(S[l, "pre_e"], 1)
                    nc.gpsimd.tensor_tensor(srcf[:, 0, :], fac[:, 2, :], dts[:, 0, 0:32], ALU.mult)
                    link(nc.gpsimd.tensor_tensor(srcf[:, 1, :], fac[:, 3, :], dts[:, 0, 96:128], ALU.mult))
                    def skipped(g):
                        if g >= 1:
                            pool.wait_ge(S[l, "y_g"], g)
                        dsk = par[:, i, 128 + HPG * g:128 + HPG * g + HPG].unsqueeze(2).to_broadcast([P, HPG, SSM_HDIM])
                        for j in range(TT):
                            ins = nc.gpsimd.tensor_tensor(XD[:, j, :].rearrange("p (h d) -> p h d", h=HPG),
                                                          xtok[:, j, 256 * g:256 * g + 256].rearrange("p (h d) -> p h d", h=HPG),
                                                          dsk, ALU.mult)
                        link(ins)

                    def gated(g):
                        pool.wait_ge(S[l, "y_v"], g + 1)
                        if g >= 1:
                            pool.wait_ge(S[l, "y_t"], g)
                            pool.wait_ge(S[l, "y_sq"], 2 * g)
                        link(nc.gpsimd.tensor_tensor(XD, YT[1], XD, ALU.add))
                        nc.gpsimd.tensor_tensor(YT[2], XD, sz[:, :, 256 * g:256 * g + 256], ALU.mult).then_inc(S[l, "y_g"], 1)

                    sources(0)
                    exponents(1)
                    for g in range(SSM_GROUPS):
                        if g >= 1:
                            gated(g - 1)
                        if g + 2 < SSM_GROUPS:
                            exponents(g + 2)
                        skipped(g)
                        if g + 1 < SSM_GROUPS:
                            sources(g + 1)
                    gated(SSM_GROUPS - 1)
                elif kind == 1:
                    pool.wait_ge(h_done, 2 * s + 2)
                    pool.dma_start(tabA, tab_a).then_inc(tab_in, 16)
                    pool.dma_start(gq[:, 0:128], w["att_q_norm"][i].partition_broadcast(P)).then_inc(tab_in, 16)
                    pool.dma_start(gq[:, 128:256], w["att_k_norm"][i].partition_broadcast(P)).then_inc(tab_in, 16)
                    pool.wait_ge(S[l, "tab_ok"], 1)
                    pool.wait_ge(S[l, "qn_r"], 1)
                    rope_att(pool, nc.gpsimd, link, 1, S[l, "r1"])
                else:
                    pool.wait_ge(h_done, 2 * s + 2)
                    pool.dma_start(tabR, tab_r).then_inc(tab_in, 16)
                    pool.dma_start(lg[:, 0:8], w["ret_log2_decay"][i].rearrange("a h -> (a h)").partition_broadcast(P)).then_inc(tab_in, 16)
                    pool.wait_ge(tab_in, 80)
                    for q in range(4):
                        rope_ret(l, q)
                send_gain()
                send_gain()
                send_gain()

        @block.scalar
        def _(act):
            def split(q, par_, static=True):
                act.wait_ge(raw_in[par_], 16 * (q + 1))
                for hf in range(2):
                    if not static or q >= 1:
                        act.wait_ge(w_used, 4 * q + 2 * par_ + hf - 3)
                    nc.scalar.activation(whi[:, 2 * par_ + hf, :], raw[:, par_, hf * HALF:(hf + 1) * HALF],
                                         ACT.Copy).then_inc(hi_done, 1)

            def splitn(n):
                if n < N_UNITS:
                    split(n // 2, n % 2)

            def squares(s, j):
                if s == 0:
                    act.wait_ge(x_in[j], 16)
                    act.wait_ge(eps_set, 1)
                else:
                    act.wait_ge(x_done, 2 * s - 2 + j + 1)
                nc.scalar.activation(junk[:, :], x[:, j, :], ACT.Square, accum_out=sq[:, j:j + 1]).then_inc(x_sq, 1)
                act.wait_ge(x_sq, 2 * s + j + 1)
                if s % 2 == 0:
                    nc.scalar.activation(sq[:, 2 + j:3 + j], sq[:, j:j + 1], ACT.Sqrt, bias=ecol[:, 0:1],
                                         scale=1.0 / D_MODEL).then_inc(x_root, 1)

            def leading(s, j):
                for c in range(2):
                    act.wait_ge(h_t, 4 * s + 2 * j + c + 1)
                    nc.scalar.activation(feat[:, HT_HI + 4 * c:HT_HI + 4 * c + 4, j * P:(j + 1) * P],
                                         ps[4 + 2 * j + c][:, :].rearrange("p (k t) -> p k t", k=4),
                                         ACT.Copy).then_inc(h_hi, 1)

            def post(s, j):
                if j == 0:
                    act.wait_ge(acc0, s + 1)
                else:
                    act.wait_ge(w_used, 2 * (FIRST_UNIT + [N_UNITS])[s + 1])
                nc.scalar.activation(junk[:, :], pacc[:, 1024 * j:1024 * j + 1024], ACT.Square,
                                     accum_out=sq[:, 4 + j:5 + j]).then_inc(m_sq, 1)
                act.wait_ge(m_sq, 2 * s + j + 1)
                if s % 2 or s // 2 % 3 == 0:
                    act.wait_ge(x_own, sum(1 for q in range(s + 1) if q % 2 or q // 2 % 3 == 0))
                    bias = ecol[:, 2 + j:3 + j]
                else:
                    bias = ecol[:, 0:1]
                nc.scalar.activation(sq[:, 6 + j:7 + j], sq[:, 4 + j:5 + j], ACT.Sqrt, bias=bias,
                                     scale=1.0 / D_MODEL).then_inc(m_root, 1)

            def turn(s):
                post(s, 0)
                if s + 1 < 2 * DEPTH:
                    splitn(FIRST_UNIT[s + 1])
                post(s, 1)
                if s + 1 < 2 * DEPTH:
                    if s % 2:
                        squares(s + 1, 0)
                        squares(s + 1, 1)
                    leading(s + 1, 0)
                    splitn(FIRST_UNIT[s + 1] + 1)
                    leading(s + 1, 1)
                    if s % 2 == 0:
                        squares(s + 1, 0)
                        squares(s + 1, 1)

            act.wait_ge(par_in, 16 * 8)
            for i in range(2):
                nc.scalar.activation(negA[:, i, :], par[:, i, 64:128], ACT.Exp).then_inc(set_a, 1)
                nc.scalar.activation(wdt_hi[:, i, :], view(tmp, 512 + 512 * i, 512), ACT.Copy).then_inc(set_w, 1)
            act.wait_ge(set_t, 1)
            for i in range(2):
                nc.scalar.activation(cols[:, i, 0:96], ps[0][:, 256 * i:256 * i + 96], ACT.Copy).then_inc(set_e, 1)
                nc.scalar.activation(cols[:, i, 96:208], ps[0][:, 256 * i + 128:256 * i + 240], ACT.Copy).then_inc(set_e, 1)
            splitn(0)
            splitn(1)
            for l in range(DEPTH):
                kind, s, n0 = l % 3, 2 * l, FIRST_UNIT[2 * l]
                i = l // 3
                if l == 0:
                    squares(0, 0)
                    squares(0, 1)
                    leading(0, 0)
                    leading(0, 1)
                if kind == 0:
                    def conv_finish(u):
                        for cc in range(2):
                            ct = 2 * u + cc
                            act.wait_ge(S[l, "conv0" if cc == 0 else "conv1"], u + 1)
                            if ct < 16:
                                if u >= 4:
                                    act.wait_ge(S[l, "x_t"], u - 3)
                                dst = xc[u % 4][:, cc, :]
                            else:
                                dst = (BT if ct < 24 else CT)[:, ct % 8, :]
                            nc.scalar.activation(dst, cacc[u % 2][:, cc, :], ACT.Silu,
                                                 bias=cols[:, i, 160 + ct:161 + ct]).then_inc(S[l, "conv_y"], 1)

                    def y_leading(g):
                        act.wait_ge(S[l, "y_t"], g + 1)
                        for kk in range(2):
                            nc.scalar.activation(feat[:, 2 * g + kk, :], ps[7][:, 256 * kk:256 * kk + 256], ACT.Identity,
                                                 scale=cols[:, i, 192 + 2 * g + kk:193 + 2 * g + kk]).then_inc(S[l, "y_hi"], 1)

                    def x_evac(u):
                        act.wait_ge(S[l, "x_t"], u + 1)
                        nc.scalar.activation(xtok[:, :, 256 * u:256 * u + 256],
                                             ps[6 + u % 2][:, :].rearrange("p (j c) -> p j c", j=2),
                                             ACT.Copy).then_inc(S[l, "x_tok"], 1)

                    for u in range(XBC_UNITS):
                        if u == 1:
                            act.wait_ge(S[l, "dt_mm"], 1)
                            nc.scalar.activation(dt_feat[0:64, :], ps[3][0:64, 0:SEQ], ACT.Copy).then_inc(S[l, "dt_mm"], 1)
                        act.wait_ge(w_used, 2 * (n0 + u) + 2)
                        if u >= 2:
                            act.wait_ge(S[l, "conv0"], u - 1)
                            act.wait_ge(S[l, "conv1"], u - 1)
                        nc.scalar.activation(cpad[u % 2][:, :, PAD:PAD + SEQ],
                                             ps[4 + u % 2][:, :].rearrange("p (c t) -> p c t", c=2),
                                             ACT.Copy).then_inc(S[l, "conv_in"], 1)
                        if u == 3:
                            act.wait_ge(S[l, "dt_abs"], 1)
                            nc.scalar.activation(dtw[:, 1, :], dtw[:, 1, :], ACT.Exp, scale=-1.0).then_inc(S[l, "dt_u"], 1)
                        splitn(n0 + u + 2)
                        if u >= 1:
                            conv_finish(u - 1)
                        if 3 <= u < 11:
                            x_evac(u - 3)
                    conv_finish(XBC_UNITS - 1)
                    for u in range(Z_UNITS):
                        if u % 2:
                            act.wait_ge(w_used, 2 * (n0 + XBC_UNITS + u) + 2)
                            for j in range(TT):
                                nc.scalar.activation(sz[:, j, 256 * (u - 1):256 * (u + 1)],
                                                     ps[2 * (u // 2 % 2) + j][:, :], ACT.Silu).then_inc(S[l, "z_ok"], 1)
                        splitn(n0 + XBC_UNITS + u + 2)

                    act.wait_ge(S[l, "pre_mm"], 1)
                    nc.scalar.activation(fac[:, :, :].rearrange("p a h -> p (a h)"), ps[7][:, 0:128], ACT.Exp).then_inc(S[l, "pre_e"], 1)

                    def exps(g):
                        for j in range(TT):
                            act.wait_ge(S[l, "seg_mm"], 2 * g + j + 1)
                            if g >= 1:
                                act.wait_ge(S[l, "w_ok"], 2 * (g - 1) + j + 1)
                            nc.scalar.activation(EX[:, j, :], ps[5 + j][:, :], ACT.Exp).then_inc(S[l, "seg_e"], 1)

                    def forward(g):
                        act.wait_ge(S[l, "cb_ok"], 3 * g + 1)
                        for j in range(TT):
                            if g >= 1:
                                act.wait_ge(S[l, "w_ok"], 2 * (g - 1) + j + 1)
                            for hd in range(HPG):
                                c = 64 * j + HPG * g + hd
                                ins = nc.scalar.activation(CD[:, j, P * hd:P * hd + P], CBM[:, 0, j, :], ACT.Identity, scale=dts[:, 0, c:c + 1])
                            ins.then_inc(S[l, "cd_ok"], 1)

                    def y_squares(g):
                        act.wait_ge(S[l, "y_g"], g + 1)
                        for j in range(TT):
                            nc.scalar.activation(junk[:, 256 * j:256 * j + 256], YT[2][:, j, :], ACT.Square,
                                                 accum_out=sq[:, 16 + 8 * j + g:17 + 8 * j + g]).then_inc(S[l, "y_sq"], 1)
                        act.wait_ge(S[l, "y_sq"], 2 * g + 2)

                    exps(0)
                    forward(0)
                    for g in range(SSM_GROUPS):
                        if g + 1 < SSM_GROUPS:
                            forward(g + 1)
                            exps(g + 1)
                        if g >= 1:
                            y_squares(g - 1)
                            y_leading(g - 1)
                    y_squares(SSM_GROUPS - 1)
                    y_leading(SSM_GROUPS - 1)
                    for u in range(SSM_OUT_UNITS - 2):
                        splitn(n0 + XBC_UNITS + Z_UNITS + u + 2)
                elif kind == 1:
                    for u in range(2 * ATT_GROUPS):
                        if u % 2:
                            act.wait_ge(w_used, 2 * (n0 + u) + 2)
                            for j in range(TT):
                                nc.scalar.activation(qkv[:, j, 256 * (u - 1):256 * (u + 1)], ps[(u - 1) + j][:, :],
                                                     ACT.Copy).then_inc(S[l, "qkv_in"], 1)
                        splitn(n0 + u + 2)
                    for c in range(5):
                        act.wait_ge(S[l, "qk_t"], c + 1)
                        nc.scalar.activation(qkT[:, 2 * c:2 * c + 2, :], ps[6 + c % 2][:, :].rearrange("p (a t) -> p a t", a=2),
                                             ACT.Copy).then_inc(S[l, "qk_in"], 1)

                    def exp_head(hd):
                        act.wait_ge(S[l, "s_max"], hd + 1)
                        if hd >= 2:
                            act.wait_ge(S[l, "p_t"], hd - 1)
                        for j in range(TT):
                            nc.scalar.activation(prob[hd % 2][:, j, :], ps[hd % 2][:, j * SEQ:(j + 1) * SEQ], ACT.Exp,
                                                 bias=sq[:, 48 + 2 * (hd % 2) + j:49 + 2 * (hd % 2) + j], scale=float(AD) ** -0.5,
                                                 accum_out=sq[:, 52 + 2 * (hd % 2) + j:53 + 2 * (hd % 2) + j]).then_inc(S[l, "s_e"], 1)

                    exp_head(0)
                    for hd in range(AQ):
                        if hd + 1 < AQ:
                            exp_head(hd + 1)
                        act.wait_ge(S[l, "p_t"], hd + 1)
                        if hd >= 2:
                            act.wait_ge(S[l, "o_mm"], hd - 1)
                        nc.scalar.activation(probT[hd % 2], ps[2 + hd % 2][:, :].rearrange("p (a t) -> p a t", a=2),
                                             ACT.Copy).then_inc(S[l, "p_in"], 1)
                        act.wait_ge(S[l, "o_mm"], hd + 1)
                        nc.scalar.activation(feat[:, hd, :], ps[4 + hd % 2][:, 0:SEQ], ACT.Copy).then_inc(S[l, "o_hi"], 1)
                    for u in range(ATT_OUT_UNITS - 2):
                        splitn(n0 + 2 * ATT_GROUPS + u + 2)
                else:
                    act.wait_ge(tab_in, 80)
                    nc.scalar.activation(lg[:, 8:16], lg[:, 0:8], ACT.Exp, scale=float(np.log(2.0))).then_inc(S[l, "lg_e"], 1)
                    act.wait_ge(S[l, "lg_e"], 2)
                    nc.scalar.activation(lg[:, 24:32], lg[:, 16:24], ACT.Ln).then_inc(S[l, "lg_e"], 1)
                    for hd in range(RH):
                        act.wait_ge(S[l, "d_pre"], hd + 1)
                        nc.scalar.activation(dec[:, hd, :, :], dec[:, hd, :, :], ACT.Exp).then_inc(S[l, "d_e"], 1)

                    def ysq(hd):
                        act.wait_ge(S[l, "y_mm"], hd + 1)
                        for j in range(TT):
                            nc.scalar.activation(rA[:, j, :], ps[4 + j][:, :], ACT.Square,
                                                 accum_out=sq[:, 32 + j:33 + j]).then_inc(S[l, "y_sq"], 1)

                    for q in range(RET_GROUPS):
                        splitn(n0 + 2 * q + 2)
                        act.wait_ge(w_used, 2 * (n0 + 2 * q + 1) + 2)
                        for j in range(TT):
                            src = ps[2 * (q % 2) + j][:, :]
                            if q < 4:
                                if q >= 1:
                                    act.wait_ge(S[l, "r0" if j == 0 else "r1"], q)
                                nc.scalar.activation(rraw[:, j, :], src, ACT.Copy).then_inc(S[l, "qk_raw"], 1)
                            elif q % 2 == 0:
                                hd = (q - 4) // 2
                                nc.scalar.activation(vr[:, j, RV * hd:RV * hd + RV], src, ACT.Copy).then_inc(S[l, "v_in"], 1)
                            else:
                                hd = (q - 4) // 2
                                nc.scalar.activation(sg[:, j, RV * hd:RV * hd + RV], src, ACT.Silu).then_inc(S[l, "g_in"], 1)
                        splitn(n0 + 2 * q + 3)
                        if q < 4:
                            for b in range(2):
                                act.wait_ge(S[l, "qk_t"], 2 * q + b + 1)
                                nc.scalar.activation(rT[:, 4 * q + 2 * b:4 * q + 2 * b + 2, :],
                                                     ps[4 + b][:, :].rearrange("p (a t) -> p a t", a=2),
                                                     ACT.Copy).then_inc(S[l, "qk_in"], 1)
                        elif q % 2:
                            ysq((q - 4) // 2)
                    for u in range(RET_OUT_UNITS):
                        act.wait_ge(S[l, "y_t"], u + 1)
                        nc.scalar.activation(feat[:, 2 * u:2 * u + 2, :], ps[4 + u % 4][:, :].rearrange("p (a t) -> p a t", a=2),
                                             ACT.Copy).then_inc(S[l, "y_hi"], 1)
                        if 1 <= u < RET_OUT_UNITS - 1:
                            splitn(n0 + 2 * RET_GROUPS + u + 1)
                turn(s)

                s += 1
                n0 = FIRST_UNIT[s]
                q0 = n0 // 2

                def relu(st, b, q, par_, static):
                    act.wait_ge(w_used, 4 * q + 2 * par_ + 2)
                    if not static or st >= 2:
                        act.wait_ge(S[l, "a_lo"], st - 1)
                    nc.scalar.activation(rl[b], ps[4 + b][:, :], ACT.Relu).then_inc(S[l, "relu"], 1)
                    act.wait_ge(S[l, "relu"], st + 1)
                    nc.scalar.activation(feat[:, 4 * b:4 * b + 2, :], rl[b].rearrange("p (a t) -> p a t", a=2),
                                         ACT.Square).then_inc(S[l, "a_hi"], 1)

                relu(0, 0, q0, 0, True)
                splitn(n0 + 2)
                relu(1, 1, q0, 1, True)
                splitn(n0 + 3)
                with act.Fori(0, MLP_STEPS // 2 - 1) as it:
                    for b in range(2):
                        q = q0 + 1 + it * 2 + b
                        split(q + 1, 0, False)
                        relu(it * 2 + 2 + b, b, q, 1, False)
                        split(q + 1, 1, False)
                turn(s)

        @block.vector
        def _(dve):
            steps = [0]
            V = nc.vector

            def link(ins):
                steps[0] += 1
                ins.then_inc(chain, 1)
                dve.wait_ge(chain, steps[0])

            def split(q, par_):
                for hf in range(2):
                    dve.wait_ge(hi_done, 4 * q + 2 * par_ + hf + 1)
                    V.tensor_tensor(wlo[:, 2 * par_ + hf, :], raw[:, par_, hf * HALF:(hf + 1) * HALF],
                                    whi[:, 2 * par_ + hf, :].bitcast(F32), ALU.subtract).then_inc(lo_done, 1)

            def splitn(n):
                if n < N_UNITS:
                    split(n // 2, n % 2)

            def rsqrt(dst, v, scratch, done=None):
                link(V.tensor_scalar(dst.bitcast(I32), v.bitcast(I32), -0.5, 1597463007.0, ALU.mult, ALU.add))
                for it in range(3):
                    link(V.tensor_tensor(scratch, v, dst, ALU.mult))
                    link(V.tensor_tensor(scratch, scratch, dst, ALU.mult))
                    link(V.tensor_scalar(scratch, scratch, -0.5, 1.5, ALU.mult, ALU.add))
                    ins = V.tensor_tensor(dst, dst, scratch, ALU.mult)
                    if it == 2 and done is not None:
                        ins.then_inc(done, 1)
                        dve.wait_ge(done, 1)
                    else:
                        link(ins)

            def take_gain(u):
                dve.wait_ge(gain_in[u % 2], 16 * (u // 2 + 1))

            def normed(s, j):
                dve.wait_ge(x_root, s + j + 1)
                link(V.reciprocal(rs[:, j:j + 1], sq[:, 2 + j:3 + j]))
                if j == 0:
                    take_gain(2 * s)
                V.scalar_tensor_tensor(out=h[:, j, :], in0=x[:, j, :], scalar=rs[:, j:j + 1], in1=gain[:, 2 * s % 2, :],
                                       op0=ALU.mult, op1=ALU.mult).then_inc(h_done, 1)

            def gained(s, j):
                if j == 0:
                    take_gain(2 * s)
                dve.wait_ge(x_done, 2 * (s - 1) + j + 1)
                V.tensor_tensor(h[:, j, :], x[:, j, :], gain[:, 2 * s % 2, :], ALU.mult).then_inc(h_done, 1)

            def lows(s, j):
                for c in range(2):
                    dve.wait_ge(h_hi, 4 * s + 2 * j + c + 1)
                    tk = slice(j * P, (j + 1) * P)
                    V.tensor_tensor(feat[:, HT_LO + 4 * c:HT_LO + 4 * c + 4, tk],
                                    ps[4 + 2 * j + c][:, :].rearrange("p (k t) -> p k t", k=4),
                                    feat[:, HT_HI + 4 * c:HT_HI + 4 * c + 4, tk].bitcast(F32),
                                    ALU.subtract).then_inc(h_lo, 1)

            def post(s, j):
                u = 2 * s + 1
                dve.wait_ge(m_root, 2 * s + j + 1)
                link(V.reciprocal(rs[:, 4 + j:5 + j], sq[:, 6 + j:7 + j]))
                if j == 0:
                    take_gain(u)
                link(V.scalar_tensor_tensor(out=h[:, j, :], in0=pacc[:, 1024 * j:1024 * j + 1024], scalar=rs[:, 4 + j:5 + j],
                                            in1=gain[:, u % 2, :], op0=ALU.mult, op1=ALU.mult))
                V.tensor_tensor(x[:, j, :], x[:, j, :], h[:, j, :], ALU.add).then_inc(x_done, 1)
                if s % 2 == 0:
                    gained(s + 1, j)

            def turn(s):
                post(s, 0)
                if s + 1 < 2 * DEPTH:
                    splitn(FIRST_UNIT[s + 1])
                post(s, 1)
                if s + 1 < 2 * DEPTH:
                    if s % 2:
                        normed(s + 1, 0)
                        normed(s + 1, 1)
                    lows(s + 1, 0)
                    splitn(FIRST_UNIT[s + 1] + 1)
                    lows(s + 1, 1)
                    if s % 2 == 0:
                        dve.wait_ge(x_sq, 2 * s + 4)
                        link(V.tensor_scalar(rs[:, 2:4], sq[:, 0:2], 1.0 / D_MODEL, EPS, ALU.mult, ALU.add))
                        V.scalar_tensor_tensor(out=ecol[:, 2:4], in0=rs[:, 2:4], scalar=EPS, in1=rs[:, 2:4],
                                               op0=ALU.mult, op1=ALU.mult).then_inc(x_own, 1)

            for i in range(2):
                dve.wait_ge(set_a, i + 1)
                link(V.tensor_scalar(negA[:, i, :], negA[:, i, :], -1.0, None, ALU.mult))
                dve.wait_ge(set_w, i + 1)
                link(V.tensor_tensor(wdt_lo[:, i, :], view(tmp, 512 + 512 * i, 512), wdt_hi[:, i, :].bitcast(F32), ALU.subtract))
            splitn(0)
            splitn(1)
            for l in range(DEPTH):
                kind, s, n0 = l % 3, 2 * l, FIRST_UNIT[2 * l]
                i = l // 3
                if l == 0:
                    dve.wait_ge(set_e, 4)
                    for j in range(TT):
                        normed(0, j)
                    for j in range(TT):
                        lows(0, j)
                if kind == 0:
                    v, av, r = (dtw[:, k, :] for k in range(3))
                    den, z, z2, p_ = (dtw[:, k, :] for k in range(3, 7))

                    def dt_first():
                        dve.wait_ge(S[l, "dt_mm"], 3)
                        link(V.tensor_tensor(v.rearrange("p (j d) -> p j d", j=2), ps[2][:, 0:128].rearrange("p (j d) -> p j d", j=2),
                                             par[:, i, 0:64].unsqueeze(1).to_broadcast([P, 2, 64]), ALU.add))
                        V.scalar_tensor_tensor(out=av, in0=v, scalar=-1.0, in1=v, op0=ALU.mult, op1=ALU.max).then_inc(S[l, "dt_abs"], 1)
                        V.tensor_scalar(r, v, 0.0, None, ALU.max)

                    def dt_rest():
                        dve.wait_ge(S[l, "dt_u"], 1)
                        link(V.tensor_scalar(den, av, 2.0, None, ALU.add))
                        link(V.reciprocal(den, den))
                        link(V.tensor_tensor(z, av, den, ALU.mult))
                        link(V.tensor_tensor(z2, z, z, ALU.mult))
                        link(V.tensor_scalar(p_, z2, 1.0 / 15, None, ALU.mult))
                        for k in (13, 11, 9, 7, 5, 3):
                            link(V.scalar_tensor_tensor(out=p_, in0=p_, scalar=1.0 / k, in1=z2, op0=ALU.add, op1=ALU.mult))
                        link(V.scalar_tensor_tensor(out=p_, in0=p_, scalar=1.0, in1=z, op0=ALU.add, op1=ALU.mult))
                        V.scalar_tensor_tensor(out=dts[:, 0, :], in0=p_, scalar=2.0, in1=r, op0=ALU.mult,
                                               op1=ALU.add).then_inc(S[l, "dt_ok"], 1)
                        dve.wait_ge(S[l, "dt_ok"], 1)
                        V.tensor_tensor(dts[:, 1, :].rearrange("p (j d) -> p j d", j=2), dts[:, 0, :].rearrange("p (j d) -> p j d", j=2),
                                        negA[:, i, :].unsqueeze(1).to_broadcast([P, 2, 64]), ALU.mult).then_inc(S[l, "dt_ok"], 1)

                    for u in range(XBC_UNITS):
                        ct = 2 * u
                        if u == 2:
                            dt_first()
                        if u == 4:
                            dt_rest()
                        dve.wait_ge(S[l, "conv_in"], u + 1)
                        if u >= 2:
                            dve.wait_ge(S[l, "conv_y"], 2 * (u - 1))
                        if u == 0:
                            dve.wait_ge(S[l, "pad_ok"], 2)
                        o = cacc[u % 2][:, 0, :]
                        for t in range(SSM_CONV):
                            tap = cols[:, i, CT_N * t + ct:CT_N * t + ct + 1]
                            src = cpad[u % 2][:, 0, t:t + SEQ]
                            if t == 0:
                                ins = V.tensor_scalar(o, src, tap, None, ALU.mult)
                            else:
                                ins = V.scalar_tensor_tensor(out=o, in0=src, scalar=tap, in1=o, op0=ALU.mult, op1=ALU.add)
                            if t < SSM_CONV - 1:
                                link(ins)
                        ins.then_inc(S[l, "conv0"], 1)
                        splitn(n0 + u + 2)
                    for u in range(Z_UNITS):
                        splitn(n0 + XBC_UNITS + u + 2)

                    def masked(g):
                        dve.wait_ge(S[l, "cb_mm"], g + 1)
                        if g == 0:
                            dve.wait_ge(S[l, "conv_y"], 2 * XBC_UNITS)
                            dve.wait_ge(S[l, "x_tok"], 8)
                        else:
                            dve.wait_ge(S[l, "cd_ok"], 2 * g)
                        if g >= 2:
                            dve.wait_ge(S[l, "y_mm"], g - 1)
                        cb = ps[4][:, :].rearrange("p (a j t) -> p a j t", a=2, j=2)
                        for b, m in enumerate((upto, after)):
                            V.tensor_tensor(CBM[:, b, :, :], cb[:, 0, :, :], m.unsqueeze(1).to_broadcast([P, 2, P]),
                                            ALU.mult).then_inc(S[l, "cb_ok"], 1)
                        V.tensor_copy(CBX[g % 2], cb[:, 1, :, :]).then_inc(S[l, "cb_ok"], 1)

                    def exponents(g):
                        for j in range(TT):
                            if g >= 1:
                                dve.wait_ge(S[l, "seg_mm"], 2 * (g - 1) + j + 1)
                            for hd in range(HPG):
                                c = 64 * j + HPG * g + hd
                                ins = V.tensor_scalar(MF[0][:, j, P * hd:P * hd + P], upto, dts[:, 1, c:c + 1], None, ALU.mult)
                            ins.then_inc(S[l, "mff_ok"], 1)

                    def weights(g):
                        dve.wait_ge(S[l, "cb_ok"], 3 * g + 3)
                        for j in range(TT):
                            dve.wait_ge(S[l, "cd_ok"], 2 * g + j + 1)
                            for hd in range(HPG):
                                c = 64 * j + 32 + HPG * g + hd
                                o = CD[:, j, P * hd:P * hd + P]
                                ins = V.scalar_tensor_tensor(out=o, in0=CBM[:, 1, j, :], scalar=dts[:, 0, c:c + 1], in1=o,
                                                             op0=ALU.mult, op1=ALU.add)
                            link(ins)
                            dve.wait_ge(S[l, "seg_e"], 2 * g + j + 1)
                            if g >= 2 and j == 0:
                                dve.wait_ge(S[l, "y_mm"], g - 1)
                            V.tensor_tensor(WM[g % 2][:, j, :], EX[:, j, :], CD[:, j, :], ALU.mult).then_inc(S[l, "w_ok"], 1)

                    def joined(g):
                        dve.wait_ge(S[l, "y_mm"], g + 1)
                        if g >= 1:
                            dve.wait_ge(S[l, "y_g"], g)
                        for j in range(TT):
                            ins = V.tensor_tensor(YT[0][:, j, :].rearrange("p (h d) -> p h d", h=HPG),
                                                  ps[g % 2][:, 256 * j:256 * j + 256].rearrange("p (h d) -> p h d", h=HPG),
                                                  fac[:, j, HPG * g:HPG * g + HPG].unsqueeze(2).to_broadcast([P, HPG, SSM_HDIM]),
                                                  ALU.mult)
                        link(ins)
                        V.tensor_tensor(YT[1], ps[2 + g % 2][:, :].rearrange("p (j c) -> p j c", j=2), YT[0],
                                        ALU.add).then_inc(S[l, "y_v"], 1)

                    exponents(0)
                    masked(0)
                    exponents(1)
                    weights(0)
                    for g in range(SSM_GROUPS):
                        if g >= 1:
                            joined(g - 1)
                        if g + 1 < SSM_GROUPS:
                            masked(g + 1)
                        if g + 2 < SSM_GROUPS:
                            exponents(g + 2)
                        if g + 1 < SSM_GROUPS:
                            weights(g + 1)
                        if g >= 1:
                            for kk in range(2):
                                low_y(V, dve, l, i, g - 1, kk)
                    joined(SSM_GROUPS - 1)
                    for kk in range(2):
                        low_y(V, dve, l, i, SSM_GROUPS - 1, kk)
                    dve.wait_ge(S[l, "y_sq"], 2 * SSM_GROUPS)
                    link(V.tensor_reduce(rs[:, 10:12], sq[:, 16:32].rearrange("p (j g) -> p j g", j=2), AX.X, ALU.add))
                    link(V.tensor_scalar(rs[:, 12:14], rs[:, 10:12], 1.0 / SSM_INNER, EPS, ALU.mult, ALU.add))
                    V.tensor_scalar(ecol[:, 2:4], rs[:, 12:14], EPS, None, ALU.mult).then_inc(x_own, 1)
                    for u in range(SSM_OUT_UNITS - 2):
                        splitn(n0 + XBC_UNITS + Z_UNITS + u + 2)
                    turn(s)
                elif kind == 1:
                    dve.wait_ge(tab_in, 48)
                    for b in range(2):
                        V.tensor_tensor(tw[:, 2 * b, :, :], tabA[:, 0:256].rearrange("p (j d) -> p j d", j=2),
                                        gq[:, 128 * b:128 * b + 128].unsqueeze(1).to_broadcast([P, 2, AD]), ALU.mult)
                    for b in range(2):
                        for a in range(2):
                            for r_ in range(2):
                                o = 64 * a + 32 * r_
                                og = 128 * b + 64 * a + 32 * (1 - r_)
                                ins = V.tensor_tensor(tw[:, 2 * b + 1, :, o:o + 32],
                                                      tabA[:, 256:512].rearrange("p (j d) -> p j d", j=2)[:, :, o:o + 32],
                                                      gq[:, og:og + 32].unsqueeze(1).to_broadcast([P, 2, 32]), ALU.mult)
                    ins.then_inc(S[l, "tab_ok"], 1)
                    for u in range(2 * ATT_GROUPS):
                        splitn(n0 + u + 2)
                    dve.wait_ge(S[l, "qkv_in"], 6)
                    for j in range(TT):
                        V.tensor_tensor(ra[j], qkv[:, j, 0:1280], qkv[:, j, 0:1280], ALU.mult).then_inc(S[l, "tab_ok"], 1)
                    for j in range(TT):
                        dve.wait_ge(S[l, "tab_ok"], 2 + j)
                        ins = V.tensor_reduce(rs[:, 40 + 10 * j:50 + 10 * j], ra[j].rearrange("p (h d) -> p h d", d=AD), AX.X, ALU.add)
                    link(ins)
                    link(V.tensor_scalar(rs[:, 60:80], rs[:, 40:60], 1.0 / AD, EPS, ALU.mult, ALU.add))
                    rsqrt(rs[:, 20:40], rs[:, 60:80], rs[:, 80:100], S[l, "qn_r"])
                    rope_att(dve, V, link, 0, S[l, "r0"])

                    def smax(hd):
                        dve.wait_ge(S[l, "s_mm"], hd + 1)
                        m = sq[:, 56 + 2 * (hd % 2):58 + 2 * (hd % 2)]
                        link(V.tensor_reduce(m, ps[hd % 2][:, :].rearrange("p (j s) -> p j s", j=2), AX.X, ALU.max))
                        V.tensor_scalar(sq[:, 48 + 2 * (hd % 2):50 + 2 * (hd % 2)], m, -float(AD) ** -0.5, None,
                                        ALU.mult).then_inc(S[l, "s_max"], 1)

                    smax(0)
                    for hd in range(AQ):
                        if hd + 1 < AQ:
                            smax(hd + 1)
                        dve.wait_ge(S[l, "s_e"], 2 * hd + 2)
                        link(V.reciprocal(rs[:, 100:102], sq[:, 52 + 2 * (hd % 2):54 + 2 * (hd % 2)]))
                        for j in range(TT):
                            V.tensor_scalar(prob[hd % 2][:, j, :], prob[hd % 2][:, j, :], rs[:, 100 + j:101 + j], None,
                                            ALU.mult).then_inc(S[l, "p_ok"], 1)
                        dve.wait_ge(S[l, "o_hi"], hd + 1)
                        V.tensor_tensor(feat[:, 8 + hd, :], ps[4 + hd % 2][:, 0:SEQ], feat[:, hd, :].bitcast(F32),
                                        ALU.subtract).then_inc(S[l, "o_lo"], 1)
                        dve.wait_ge(S[l, "p_ok"], 2 * hd + 2)
                    for u in range(ATT_OUT_UNITS - 2):
                        splitn(n0 + 2 * ATT_GROUPS + u + 2)
                    turn(s)
                else:
                    dve.wait_ge(S[l, "lg_e"], 1)
                    V.tensor_scalar(lg[:, 16:24], lg[:, 8:16], -1.0, 1.0, ALU.mult, ALU.add).then_inc(S[l, "lg_e"], 1)
                    dve.wait_ge(S[l, "lg_e"], 3)
                    link(V.tensor_scalar(lg[:, 32:40], lg[:, 16:24], 1.0, None, ALU.is_equal))
                    V.tensor_tensor(lg[:, 40:48], lg[:, 24:32], lg[:, 32:40], ALU.add)
                    link(V.scalar_tensor_tensor(out=lg[:, 48:56], in0=lg[:, 16:24], scalar=-1.0, in1=lg[:, 32:40], op0=ALU.add, op1=ALU.add))
                    link(V.reciprocal(lg[:, 48:56], lg[:, 48:56]))
                    link(V.scalar_tensor_tensor(out=lg[:, 48:56], in0=lg[:, 48:56], scalar=-1.0, in1=lg[:, 8:16], op0=ALU.mult, op1=ALU.mult))
                    link(V.tensor_tensor(lg[:, 56:64], lg[:, 48:56], lg[:, 40:48], ALU.mult))
                    for hd in range(RH):
                        link(V.tensor_scalar(drow, tabR[:, T_AHEAD:T_AHEAD + 512].rearrange("p (j t) -> p j t", j=2),
                                             lg[:, 56 + hd:57 + hd], None, ALU.mult))
                        V.scalar_tensor_tensor(out=dec[:, hd, :, :], in0=tabR[:, T_BEHIND:T_BEHIND + 512].rearrange("p (j t) -> p j t", j=2),
                                               scalar=lg[:, 60 + hd:61 + hd], in1=drow, op0=ALU.mult,
                                               op1=ALU.add).then_inc(S[l, "d_pre"], 1)
                        dve.wait_ge(S[l, "d_pre"], hd + 1)

                    def scored(hd):
                        dve.wait_ge(S[l, "s_mm"], hd + 1)
                        dve.wait_ge(S[l, "d_e"], hd + 1)
                        if hd >= 2:
                            dve.wait_ge(S[l, "y_mm"], hd - 1)
                        V.scalar_tensor_tensor(out=wt[hd % 2], in0=ps[6 + hd % 2][:, :].rearrange("p (j t) -> p j t", j=2),
                                               scalar=float(RQK) ** -0.5, in1=dec[:, hd, :, :], op0=ALU.mult,
                                               op1=ALU.mult).then_inc(S[l, "s_w"], 1)

                    for q in range(RET_GROUPS):
                        splitn(n0 + 2 * q + 2)
                        if q < 4:
                            dve.wait_ge(S[l, "qk_raw"], 2 * q + 1)
                            if q >= 1:
                                dve.wait_ge(S[l, "qk_t"], 2 * q)
                            V.tensor_tensor(rA[:, 0, :].rearrange("p (h d) -> p h d", h=2), rraw[:, 0, :].rearrange("p (h d) -> p h d", h=2),
                                            tabR[:, T_COSR:T_COSR + 256].unsqueeze(1).to_broadcast([P, 2, 256]), ALU.mult)
                            s5 = rraw[:, 0, :].rearrange("p (h r d) -> p h r d", h=4, r=2)
                            o5 = rB[:, 0, :].rearrange("p (h r d) -> p h r d", h=4, r=2)
                            sn = tabR[:, T_SINR:T_SINR + 256].rearrange("p (a r d) -> p a r d", a=2, r=2)
                            for hd in range(2):
                                for r_ in range(2):
                                    ins = V.tensor_tensor(o5[:, 2 * hd:2 * hd + 2, r_, :], s5[:, 2 * hd:2 * hd + 2, 1 - r_, :],
                                                          sn[:, :, r_, :], ALU.mult)
                            link(ins)
                            V.tensor_tensor(rA[:, 0, :], rA[:, 0, :], rB[:, 0, :], ALU.add).then_inc(S[l, "r0"], 1)
                        elif q % 2 == 0:
                            scored((q - 4) // 2)
                        splitn(n0 + 2 * q + 3)
                        if q >= 4 and q % 2:
                            hd = (q - 4) // 2
                            dve.wait_ge(S[l, "y_sq"], 2 * hd + 2)
                            link(V.tensor_scalar(rs[:, 104:106], sq[:, 32:34], 1.0 / RV, EPS, ALU.mult, ALU.add))
                            rsqrt(rs[:, 106:108], rs[:, 104:106], rs[:, 108:110])
                            for j in range(TT):
                                V.scalar_tensor_tensor(out=vr[:, j, RV * hd:RV * hd + RV], in0=ps[4 + j][:, :], scalar=rs[:, 106 + j:107 + j],
                                                       in1=sg[:, j, RV * hd:RV * hd + RV], op0=ALU.mult, op1=ALU.mult).then_inc(S[l, "y_g"], 1)
                            dve.wait_ge(S[l, "y_g"], 2 * hd + 2)
                    for u in range(RET_OUT_UNITS):
                        dve.wait_ge(S[l, "y_hi"], u + 1)
                        V.tensor_tensor(feat[:, 16 + 2 * u:18 + 2 * u, :], ps[4 + u % 4][:, :].rearrange("p (a t) -> p a t", a=2),
                                        feat[:, 2 * u:2 * u + 2, :].bitcast(F32), ALU.subtract).then_inc(S[l, "y_lo"], 1)
                        if 1 <= u < RET_OUT_UNITS - 1:
                            splitn(n0 + 2 * RET_GROUPS + u + 1)
                    turn(s)

                s += 1
                n0 = FIRST_UNIT[s]
                q0 = n0 // 2

                def square(st, b, static):
                    dve.wait_ge(S[l, "relu"], st + 1)
                    if not static or st >= 1:
                        dve.wait_ge(S[l, "a_lo"], st)
                    V.tensor_tensor(aa, rl[b], rl[b], ALU.mult).then_inc(S[l, "sqr"], 1)
                    dve.wait_ge(S[l, "sqr"], st + 1)
                    dve.wait_ge(S[l, "a_hi"], st + 1)
                    V.tensor_tensor(feat[:, 4 * b + 2:4 * b + 4, :], aa.rearrange("p (a t) -> p a t", a=2),
                                    feat[:, 4 * b:4 * b + 2, :].bitcast(F32), ALU.subtract).then_inc(S[l, "a_lo"], 1)

                square(0, 0, True)
                splitn(n0 + 2)
                square(1, 1, True)
                splitn(n0 + 3)
                with dve.Fori(0, MLP_STEPS // 2 - 1) as it:
                    for b in range(2):
                        q = q0 + 1 + it * 2 + b
                        split(q + 1, 0)
                        square(it * 2 + 2 + b, b, False)
                        split(q + 1, 1)
                turn(s)

        @block.tensor
        def _(pe):
            mm = nc.tensor.matmul
            TP = nc.tensor.transpose

            def token_major(q, par_, lhs_hi, lhs_lo, banks, first, k0, nk, width):
                cn = width // 512
                for hf in range(2):
                    slot = 2 * par_ + hf
                    pe.wait_ge(lo_done, 4 * q + 2 * par_ + hf + 1)
                    for j in range(TT):
                        for k in range(nk):
                            kk = k0 + hf * nk + k
                            tk = slice(j * P, (j + 1) * P)
                            st = first and hf == 0 and k == 0
                            for c in range(cn):
                                cs = slice(k * width + 512 * c, k * width + 512 * c + 512)
                                o = ps[banks[j * cn + c]][:, :]
                                mm(o, lhs_hi(kk)[:, tk], whi[:, slot, cs], start=st, stop=False, skip_group_check=True)
                                ins = mm(o, lhs_hi(kk)[:, tk], wlo[:, slot, cs], start=False, stop=False, skip_group_check=True)
                            for c in range(cn):
                                cs = slice(k * width + 512 * c, k * width + 512 * c + 512)
                                ins = mm(ps[banks[j * cn + c]][:, :], lhs_lo(kk)[:, tk], whi[:, slot, cs],
                                         start=False, stop=True, skip_group_check=True)
                    ins.then_inc(w_used, 1)

            def feature_major(q, par_, bank):
                for hf in range(2):
                    slot = 2 * par_ + hf
                    pe.wait_ge(lo_done, 4 * q + 2 * par_ + hf + 1)
                    for f in range(2):
                        o = ps[bank][:, f * SEQ:(f + 1) * SEQ]
                        for k in range(4):
                            ws = slice(k * 256 + f * P, k * 256 + f * P + P)
                            kk = 4 * hf + k
                            mm(o, whi[:, slot, ws], feat[:, HT_HI + kk, :], start=(hf == 0 and f == 0 and k == 0), stop=False, skip_group_check=True)
                            mm(o, whi[:, slot, ws], feat[:, HT_LO + kk, :], start=False, stop=False, skip_group_check=True)
                            ins = mm(o, wlo[:, slot, ws], feat[:, HT_HI + kk, :], start=False, stop=True, skip_group_check=True)
                    ins.then_inc(w_used, 1)

            ht = (lambda k: feat[:, HT_HI + k, :]), (lambda k: feat[:, HT_LO + k, :])

            def turned(s, j):
                pe.wait_ge(h_done, 2 * s + j + 1)
                for c in range(2):
                    for k in range(4):
                        ins = TP(ps[4 + 2 * j + c][:, k * P:(k + 1) * P], h[:, j, (4 * c + k) * P:(4 * c + k + 1) * P], ident)
                    ins.then_inc(h_t, 1)

            def head_part(n, j):
                for hf in range(2):
                    m = 2 * n + hf
                    slot = m % 4
                    if j == 0:
                        pe.wait_ge(lo_done, m + 1)
                    tk = slice(j * P, (j + 1) * P)
                    for k in range(2):
                        cs, kk = slice(512 * k, 512 * k + 512), 4 * (n % 2) + 2 * hf + k
                        o = ps[j][:, :]
                        mm(o, feat[:, HT_HI + kk, tk], whi[:, slot, cs], start=(kk == 0), stop=False, skip_group_check=True)
                        mm(o, feat[:, HT_HI + kk, tk], wlo[:, slot, cs], start=False, stop=False, skip_group_check=True)
                        ins = mm(o, feat[:, HT_LO + kk, tk], whi[:, slot, cs], start=False, stop=True, skip_group_check=True)
                    if j == 1:
                        ins.then_inc(w_used, 1)

            def head(s, feature):
                n = FIRST_UNIT[s]
                turned(s, 0)
                if feature:
                    turned(s, 1)
                    pe.wait_ge(h_lo, 4 * s + 4)
                    feature_major(n // 2, 0, 4)
                    feature_major(n // 2, 1, 5)
                else:
                    pe.wait_ge(h_lo, 4 * s + 2)
                    head_part(n, 0)
                    turned(s, 1)
                    head_part(n + 1, 0)
                    pe.wait_ge(h_lo, 4 * s + 4)
                    head_part(n, 1)
                    head_part(n + 1, 1)

            def tail(n, lhs_hi, lhs_lo, k0):
                for j in range(TT):
                    tk = slice(j * P, (j + 1) * P)
                    for k in range(4):
                        if j == 0:
                            pe.wait_ge(lo_done, 2 * n + k + 1)
                        for c in range(2):
                            cs = slice(512 * c, 512 * c + 512)
                            mm(ps[2 * j + c][:, :], lhs_hi(k0 + k)[:, tk], whi[:, k, cs], start=False, stop=False, skip_group_check=True)
                            mm(ps[2 * j + c][:, :], lhs_hi(k0 + k)[:, tk], wlo[:, k, cs], start=False, stop=False, skip_group_check=True)
                        for c in range(2):
                            ins = mm(ps[2 * j + c][:, :], lhs_lo(k0 + k)[:, tk], whi[:, k, 512 * c:512 * c + 512],
                                     start=False, stop=True, skip_group_check=True)
                        if j == 1:
                            ins.then_inc(w_used, 1)
                    if j == 0:
                        ins.then_inc(acc0, 1)

            def project(s, n, units, lhs_hi, lhs_lo, ready, per):
                for u in range(units - 2):
                    pe.wait_ge(ready, per * (u + 1))
                    token_major((n + u) // 2, (n + u) % 2, lhs_hi, lhs_lo, (0, 1, 2, 3), u == 0, 2 * u, 1, D_MODEL)
                pe.wait_ge(ready, per * units)
                tail(n + units - 2, lhs_hi, lhs_lo, 2 * units - 4)

            pe.wait_ge(const_in, 16)
            pe.wait_ge(rows_in, 16 * 8)
            for i in range(2):
                TP(ps[0][:, 256 * i:256 * i + 96], view(tmp, 256 * i, P)[0:96, :], ident[0:96, 0:96])
                ins = TP(ps[0][:, 256 * i + 128:256 * i + 240], view(tmp, 256 * i + 128, P)[0:112, :], ident[0:112, 0:112])
            ins.then_inc(set_t, 1)

            for l in range(DEPTH):
                kind, s, n0 = l % 3, 2 * l, FIRST_UNIT[2 * l]
                i = l // 3
                head(s, kind == 0)
                if kind == 0:
                    pe.wait_ge(lo_done, 1)
                    o = ps[3][0:64, 0:SEQ]
                    for k in range(KD):
                        ks = slice(64 * k, 64 * k + 64)
                        mm(o, wdt_hi[:, i, ks], feat[:, HT_HI + k, :], start=(k == 0), stop=False)
                        mm(o, wdt_hi[:, i, ks], feat[:, HT_LO + k, :], start=False, stop=False)
                        ins = mm(o, wdt_lo[:, i, ks], feat[:, HT_HI + k, :], start=False, stop=(k == KD - 1))
                    ins.then_inc(S[l, "dt_mm"], 1)

                    def x_transposes(u):
                        pe.wait_ge(S[l, "conv_y"], 2 * u + 2)
                        if u >= 2:
                            pe.wait_ge(S[l, "x_tok"], u - 1)
                        for j in range(TT):
                            for cc in range(2):
                                ins = TP(ps[6 + u % 2][:, 256 * j + P * cc:256 * j + P * cc + P], xc[u % 4][:, cc, j * P:(j + 1) * P], ident)
                        ins.then_inc(S[l, "x_t"], 1)

                    for u in range(2, XBC_UNITS):
                        pe.wait_ge(S[l, "conv_in"], u - 1)
                        feature_major((n0 + u) // 2, (n0 + u) % 2, 4 + u % 2)
                        if u == 2:
                            pe.wait_ge(S[l, "dt_mm"], 2)
                            for j in range(TT):
                                ins = TP(ps[2][:, 64 * j:64 * j + 64], dt_feat[0:64, j * P:(j + 1) * P], ident[0:64, 0:64])
                            ins.then_inc(S[l, "dt_mm"], 1)
                        if u < 10:
                            x_transposes(u - 2)
                    dAv = dts[:, 1, :].rearrange("p (j d h) -> p j d h", j=2, d=2)
                    pe.wait_ge(S[l, "dt_ok"], 2)
                    pe.wait_ge(S[l, "x_tok"], 8)
                    for b, (m, j, fb) in enumerate(((fromon, 0, 1), (upto, 1, 0), (after, 0, 0), (before, 1, 1))):
                        ins = mm(ps[7][:, 32 * b:32 * b + 32], m, dAv[:, j, fb, :], start=True, stop=True)
                    ins.then_inc(S[l, "pre_mm"], 1)
                    for u in range(Z_UNITS):
                        n = n0 + XBC_UNITS + u
                        if u >= 4:
                            pe.wait_ge(S[l, "z_ok"], 2 * (u // 2 - 1))
                        token_major(n // 2, n % 2, *ht, (2 * (u // 2 % 2), 2 * (u // 2 % 2) + 1), u % 2 == 0, 4 * (u % 2), 2, 512)

                    def seg(g):
                        if g == 0:
                            pe.wait_ge(S[l, "conv_y"], 2 * XBC_UNITS)
                        else:
                            pe.wait_ge(S[l, "cb_ok"], 3 * g)
                        for a in range(2):
                            for j in range(TT):
                                src = j if a == 0 else 1 - j
                                ins = mm(ps[4][:, 256 * a + P * j:256 * a + P * j + P], BT[:, g, src * P:(src + 1) * P],
                                         CT[:, g, j * P:(j + 1) * P], start=True, stop=True)
                        ins.then_inc(S[l, "cb_mm"], 1)
                        for j in range(TT):
                            pe.wait_ge(S[l, "mff_ok"], 2 * g + j + 1)
                            pe.wait_ge(S[l, "mfb_ok"], 2 * g + j + 1)
                            if g >= 1:
                                pe.wait_ge(S[l, "seg_e"], 2 * (g - 1) + j + 1)
                            mm(ps[5 + j][:, :], after, MF[0][:, j, :], start=True, stop=False)
                            mm(ps[5 + j][:, :], before, MF[1][:, j, :], start=False, stop=True).then_inc(S[l, "seg_mm"], 1)

                    def y_transposes(g):
                        pe.wait_ge(S[l, "y_g"], g + 1)
                        if g >= 1:
                            pe.wait_ge(S[l, "y_lo"], 2 * g)
                        else:
                            pe.wait_ge(S[l, "pre_e"], 1)
                        for kk in range(2):
                            for j in range(TT):
                                ins = TP(ps[7][:, 256 * kk + P * j:256 * kk + P * j + P], YT[2][:, j, P * kk:P * kk + P], ident)
                        ins.then_inc(S[l, "y_t"], 1)

                    pe.wait_ge(S[l, "z_ok"], 8)
                    seg(0)
                    for g in range(SSM_GROUPS):
                        if g + 1 < SSM_GROUPS:
                            seg(g + 1)
                        pe.wait_ge(S[l, "xs_ok"], g + 1)
                        pe.wait_ge(S[l, "cb_ok"], 3 * g + 3)
                        if g >= 2:
                            pe.wait_ge(S[l, "y_v"], g - 1)
                        for j in range(TT):
                            mm(ps[g % 2][:, 256 * j:256 * j + 256], CBX[g % 2][:, j, :], XS[g % 2][:, 1 - j, :], start=True, stop=True)
                        pe.wait_ge(S[l, "w_ok"], 2 * g + 2)
                        for j in range(TT):
                            for hd in range(HPG):
                                c = 256 * g + SSM_HDIM * hd
                                ins = mm(ps[2 + g % 2][:, 256 * j + SSM_HDIM * hd:256 * j + SSM_HDIM * (hd + 1)],
                                         WM[g % 2][:, j, P * hd:P * hd + P], xtok[:, j, c:c + SSM_HDIM], start=True, stop=True)
                        ins.then_inc(S[l, "y_mm"], 1)
                        if g >= 1:
                            y_transposes(g - 1)
                    y_transposes(SSM_GROUPS - 1)
                    pe.wait_ge(S[l, "y_v"], SSM_GROUPS)
                    project(s, n0 + XBC_UNITS + Z_UNITS, SSM_OUT_UNITS, lambda k: feat[:, k, :], lambda k: feat[:, 16 + k, :],
                            S[l, "y_lo"], 2)
                elif kind == 1:
                    for u in range(2, 2 * ATT_GROUPS):
                        token_major((n0 + u) // 2, (n0 + u) % 2, *ht, (2 * (u // 2), 2 * (u // 2) + 1), u % 2 == 0, 4 * (u % 2), 2, 512)
                    pe.wait_ge(S[l, "r0"], 1)
                    pe.wait_ge(S[l, "r1"], 1)
                    for c in range(5):
                        if c >= 2:
                            pe.wait_ge(S[l, "qk_in"], c - 1)
                        for b in range(2):
                            for j in range(TT):
                                ins = TP(ps[6 + c % 2][:, 256 * b + P * j:256 * b + P * j + P], qkv[:, j, P * (2 * c + b):P * (2 * c + b + 1)], ident)
                        ins.then_inc(S[l, "qk_t"], 1)

                    def scores(hd):
                        if hd >= 2:
                            pe.wait_ge(S[l, "s_e"], 2 * (hd - 1))
                        for j in range(TT):
                            ins = mm(ps[hd % 2][:, j * SEQ:(j + 1) * SEQ], qkT[:, hd, j * P:(j + 1) * P], qkT[:, AQ + hd // 4, :],
                                     start=True, stop=True)
                        ins.then_inc(S[l, "s_mm"], 1)

                    pe.wait_ge(S[l, "qk_in"], 5)
                    scores(0)
                    for hd in range(AQ):
                        if hd + 1 < AQ:
                            scores(hd + 1)
                        pe.wait_ge(S[l, "p_ok"], 2 * hd + 2)
                        if hd >= 2:
                            pe.wait_ge(S[l, "p_in"], hd - 1)
                        for b in range(2):
                            for j in range(TT):
                                ins = TP(ps[2 + hd % 2][:, 256 * b + P * j:256 * b + P * j + P], prob[hd % 2][:, j, P * b:P * b + P], ident)
                        ins.then_inc(S[l, "p_t"], 1)
                        pe.wait_ge(S[l, "p_in"], hd + 1)
                        if hd >= 2:
                            pe.wait_ge(S[l, "o_lo"], hd - 1)
                        vo = AQ * AD + AKV * AD + AD * (hd // 4)
                        for b in range(2):
                            ins = mm(ps[4 + hd % 2][:, 0:SEQ], qkv[:, b, vo:vo + AD], probT[hd % 2][:, b, :], start=(b == 0), stop=(b == 1))
                        ins.then_inc(S[l, "o_mm"], 1)
                    project(s, n0 + 2 * ATT_GROUPS, ATT_OUT_UNITS, lambda k: feat[:, k, :], lambda k: feat[:, 8 + k, :], S[l, "o_lo"], 2)
                else:
                    def rope_transposes(q):
                        pe.wait_ge(S[l, "r0"], q + 1)
                        pe.wait_ge(S[l, "r1"], q + 1)
                        for b in range(2):
                            if q >= 1:
                                pe.wait_ge(S[l, "qk_in"], 2 * q - 1 + b)
                            for a in range(2):
                                for j in range(TT):
                                    c = P * (2 * b + a)
                                    ins = TP(ps[4 + b][:, 256 * a + P * j:256 * a + P * j + P], rA[:, j, c:c + P], ident)
                            ins.then_inc(S[l, "qk_t"], 1)

                    def scores(hd):
                        if hd >= 2:
                            pe.wait_ge(S[l, "s_w"], hd - 1)
                        for b in range(TT):
                            for k in range(2):
                                ins = mm(ps[6 + hd % 2][:, b * SEQ:(b + 1) * SEQ], rT[:, 8 + 2 * hd + k, b * P:(b + 1) * P], rT[:, 2 * hd + k, :],
                                         start=(k == 0), stop=(k == 1))
                        ins.then_inc(S[l, "s_mm"], 1)

                    def y_head(hd):
                        pe.wait_ge(S[l, "s_w"], hd + 1)
                        pe.wait_ge(S[l, "v_in"], 2 * hd + 2)
                        if hd == 0:
                            pe.wait_ge(S[l, "qk_in"], 8)
                        else:
                            pe.wait_ge(S[l, "y_g"], 2 * hd)
                        for j in range(TT):
                            for b in range(TT):
                                ins = mm(ps[4 + j][:, :], wt[hd % 2][:, b, j * P:(j + 1) * P], vr[:, b, RV * hd:RV * hd + RV],
                                         start=(b == 0), stop=(b == 1))
                        ins.then_inc(S[l, "y_mm"], 1)

                    for q in range(RET_GROUPS):
                        for hf in range(2):
                            n = n0 + 2 * q + hf
                            if q >= 2 and hf == 0:
                                if q < 6:
                                    pe.wait_ge(S[l, "qk_raw"], 2 * (q - 1))
                                elif q % 2 == 0:
                                    pe.wait_ge(S[l, "v_in"], 2 * ((q - 6) // 2 + 1))
                                else:
                                    pe.wait_ge(S[l, "g_in"], 2 * ((q - 6) // 2 + 1))
                            if q >= 1:
                                token_major(n // 2, n % 2, *ht, (2 * (q % 2), 2 * (q % 2) + 1), hf == 0, 4 * hf, 2, 512)
                            if hf == 0 and 1 <= q <= 4:
                                rope_transposes(q - 1)
                            if hf == 0 and q >= 5 and q % 2:
                                y_head((q - 5) // 2)
                            if hf == 1 and q >= 4 and q % 2 == 0:
                                if q == 4:
                                    pe.wait_ge(S[l, "qk_in"], 8)
                                scores((q - 4) // 2)

                    def y_transposes(u):
                        pe.wait_ge(S[l, "y_g"], 2 * (u // 2) + 2)
                        if u < 2:
                            pe.wait_ge(S[l, "y_g"], 8)
                        if u >= 4:
                            pe.wait_ge(S[l, "y_lo"], u - 3)
                        for a in range(2):
                            for j in range(TT):
                                c = P * (2 * u + a)
                                ins = TP(ps[4 + u % 4][:, 256 * a + P * j:256 * a + P * j + P], vr[:, j, c:c + P], ident)
                        ins.then_inc(S[l, "y_t"], 1)

                    for u in range(3):
                        y_transposes(u)
                    pe.wait_ge(S[l, "g_in"], 8)
                    for u in range(RET_OUT_UNITS - 2):
                        pe.wait_ge(S[l, "y_lo"], u + 1)
                        n = n0 + 2 * RET_GROUPS + u
                        token_major(n // 2, n % 2, lambda k: feat[:, k, :], lambda k: feat[:, 16 + k, :], (0, 1, 2, 3), u == 0, 2 * u, 1,
                                    D_MODEL)
                        if u + 3 < RET_OUT_UNITS:
                            y_transposes(u + 3)
                    pe.wait_ge(S[l, "y_lo"], RET_OUT_UNITS)
                    tail(n0 + 2 * RET_GROUPS + RET_OUT_UNITS - 2, lambda k: feat[:, k, :], lambda k: feat[:, 16 + k, :], 2 * RET_OUT_UNITS - 4)

                s += 1
                n0 = FIRST_UNIT[s]
                q0 = n0 // 2
                head(s, True)

                def up(st, b, q, par_, static):
                    if not static or st >= 2:
                        pe.wait_ge(S[l, "relu"], st - 1)
                    feature_major(q, par_, 4 + b)

                def down(st, b, q, par_, first):
                    pe.wait_ge(S[l, "a_lo"], st + 1)
                    token_major(q, par_, lambda k: feat[:, 4 * b + k, :], lambda k: feat[:, 4 * b + 2 + k, :], (0, 1, 2, 3), first, 0, 1,
                                D_MODEL)

                down(0, 0, q0 + 1, 0, True)
                up(2, 0, q0 + 1, 1, True)
                with pe.Fori(0, MLP_STEPS // 2 - 2) as it:
                    for b in range(2):
                        t = it * 2 + 1 + b
                        down(t, 1 - b, q0 + 1 + t, 0, False)
                        up(t + 2, 1 - b, q0 + 1 + t, 1, False)
                down(MLP_STEPS - 3, 1, q0 + MLP_STEPS - 2, 0, False)
                up(MLP_STEPS - 1, 1, q0 + MLP_STEPS - 2, 1, True)
                pe.wait_ge(S[l, "a_lo"], MLP_STEPS)
                tail(n0 + MLP_UNITS - 2, lambda k: feat[:, k + 2 * (k // 2), :], lambda k: feat[:, 2 + k + 2 * (k // 2), :], 0)


_INS = ["x", "norm_mix_pre", "norm_mix_post", "norm_ffn_pre", "norm_ffn_post", "mlp_w_in", "mlp_w_out",
        "ssm_w_in", "ssm_conv_w", "ssm_conv_b", "ssm_dt_bias", "ssm_a_log", "ssm_d", "ssm_norm", "ssm_w_out",
        "att_w_in", "att_q_norm", "att_k_norm", "att_w_out", "ret_w_in", "ret_log2_decay", "ret_w_out"]


def kernel(**inputs):
    import concourse.bacc as _bacc
    from concourse.bass_utils import run_bass_kernel_spmd as _run

    nc = _bacc.Bacc("TRN2", target_bir_lowering=False, num_devices=1)
    arrays, aps = {}, {}
    for name in _INS:
        a = np.ascontiguousarray(inputs[name])
        arrays[f"in_{name}"] = a
        aps[name] = nc.dram_tensor(f"in_{name}", a.shape, F32, kind="ExternalInput").ap()
    extra = []
    for name, a in zip(("consts", "tab_a", "tab_r"), shape_constants()):
        arrays[f"in_{name}"] = a
        extra.append(nc.dram_tensor(f"in_{name}", a.shape, F32, kind="ExternalInput").ap())
    out = nc.dram_tensor("out_x", (1, SEQ, D_MODEL), F32, kind="ExternalOutput").ap()
    build(nc, aps, *extra, out)
    r = _run(nc, [arrays], core_ids=[0])
    return r.results[0]["out_x"]
```

```python
from contextlib import ExitStack

import numpy as np

import concourse.bass as bass
from concourse import mybir

ALU = mybir.AluOpType
ACT = mybir.ActivationFunctionType
AX = mybir.AxisListType
F32 = mybir.dt.float32
F32R = mybir.dt.float32r
I32 = mybir.dt.int32

P = 128
D_MODEL, SEQ, DEPTH = 1024, 256, 4
TT = SEQ // P
KD = D_MODEL // P
EPS = 1e-6
D_FF = 4 * D_MODEL
SSM_INNER, SSM_HEADS, SSM_HDIM, SSM_GROUPS, SSM_STATE, SSM_CONV = 2048, 32, 64, 8, 128, 5
HPG = SSM_HEADS // SSM_GROUPS
CONV_DIM = SSM_INNER + 2 * SSM_GROUPS * SSM_STATE
CT_N = CONV_DIM // P
PAD = SSM_CONV // 2
AQ, AKV, AD = 8, 2, 128
ATT_COLS = (2, 0, 1)
ATT_HEADS = ((8, 2), (0, 4), (4, 4))
ATT_PAIRS = (8, 0, 2, 4, 6)
RH, RQK, RV = 4, 256, 512
GRID_W, ROPE_THETA = 64, 10000.0
SSM_LAYERS = [l for l in range(DEPTH) if l % 3 == 0]

UNIT = 2048
HALF = UNIT // 2
XBC_UNITS = CONV_DIM // 256
Z_UNITS = 2 * SSM_INNER // 512
SSM_OUT_UNITS = SSM_INNER // 256
ATT_GROUPS = (AQ + 2 * AKV) * AD // 512
ATT_OUT_UNITS = AQ * AD // 256
RET_GROUPS = 6 * D_MODEL // 512
RET_OUT_UNITS = 2 * D_MODEL // 256
MLP_STEPS = D_FF // 256
MLP_UNITS = 2 * MLP_STEPS
MIX_UNITS = {0: XBC_UNITS + Z_UNITS + SSM_OUT_UNITS, 1: 2 * ATT_GROUPS + ATT_OUT_UNITS,
             2: 2 * RET_GROUPS + RET_OUT_UNITS}
FIRST_UNIT = []
_n = 0
for _l in range(DEPTH):
    FIRST_UNIT += [_n, _n + MIX_UNITS[_l % 3]]
    _n += MIX_UNITS[_l % 3] + MLP_UNITS
N_UNITS = _n

C_ID, C_LE, C_GT, C_GE, C_LT = (P * i for i in range(5))
N_CONST = 5 * P
T_COSA, T_SINA = 0, 256
N_TABA = 512
T_COSR, T_SINR, T_AHEAD, T_BEHIND = 0, 512, 1024, 1536
N_TABR = 2048


def rope_tables(dim):
    rows = SEQ // GRID_W
    row = np.repeat(np.arange(rows, dtype=np.float32), GRID_W)
    col = np.tile(np.arange(GRID_W, dtype=np.float32), rows)
    half = dim // 2
    nf = half // 2
    inv = np.float32(ROPE_THETA) ** (-(np.arange(nf, dtype=np.float32) * np.float32(2)) / np.float32(half))
    ang = np.stack([row[:, None] * inv, col[:, None] * inv], axis=1).astype(np.float32)
    c, s = np.cos(ang), np.sin(ang)
    cos = np.stack([c, c], axis=2).reshape(TT, P, dim)
    sin = np.stack([-s, s], axis=2).reshape(TT, P, dim)
    return [a.transpose(1, 0, 2).reshape(P, TT * dim).astype(np.float32) for a in (cos, sin)]


def shape_constants():
    a = np.arange(P)
    k, t = a[:, None], a[None, :]
    base = np.concatenate([k == t, k <= t, k > t, k >= t, k < t], axis=1).astype(np.float32)
    tab_a = np.concatenate(rope_tables(AD), axis=1)
    s = (np.arange(TT)[None, :, None] * P + a[:, None, None])
    diff = (np.arange(SEQ)[None, None, :] - s).astype(np.float32)
    tab_r = np.concatenate(rope_tables(RQK) + [np.maximum(diff, 0).reshape(P, -1),
                                               np.maximum(-diff, 0).reshape(P, -1)], axis=1)
    return base, tab_a, tab_r.astype(np.float32)


def build(nc, w, consts, tab_a, tab_r, out):
    ctx = ExitStack()
    with ctx:
        def sb(name, shape, dt=F32):
            return ctx.enter_context(nc.sbuf_tensor(name, [P] + list(shape), dt))

        def sem(name):
            return ctx.enter_context(nc.semaphore(name))

        raw = sb("raw", [2, UNIT])
        whi = sb("whi", [4, HALF], F32R)
        wlo = sb("wlo", [4, HALF], F32R)
        feat = sb("feat", [32, SEQ], F32R)
        x = sb("x", [TT, D_MODEL])
        h = sb("h", [TT, D_MODEL])
        big = sb("big", [12288])
        tmp = sb("tmp", [9472])
        gain = sb("gain", [2, D_MODEL])
        cst = sb("cst", [N_CONST])
        cols = sb("cols", [2, 208])
        par = sb("par", [2, 160])
        negA = sb("negA", [2, 64])
        wdt_hi = sb("wdt_hi", [2, 512], F32R)
        wdt_lo = sb("wdt_lo", [2, 512], F32R)
        sq = sb("sq", [64])
        rs = sb("rs", [128])
        dts = sb("dts", [2, P])
        fac = sb("fac", [4, 32])
        srcf = sb("srcf", [2, 32])
        lg = sb("lg", [64])
        pacc = ctx.enter_context(nc.psum_tensor("pacc", [P, 4 * 512], F32))
        ps = [pacc[:, 512 * i:512 * i + 512] for i in range(4)]
        ps += [ctx.enter_context(nc.psum_tensor(f"ps{i}", [P, 512], F32)) for i in range(4, 8)]
        ecol = sb("ecol", [8])

        ident = cst[:, C_ID:C_ID + P]
        upto, after, fromon, before = (cst[:, c:c + P] for c in (C_LE, C_GT, C_GE, C_LT))
        HT_HI, HT_LO = 16, 24

        raw_in = [sem("raw_in0"), sem("raw_in1")]
        hi_done, lo_done, w_used = sem("hi_done"), sem("lo_done"), sem("w_used")
        x_in = [sem("x_in0"), sem("x_in1")]
        const_in, rows_in, par_in, wdt_in = sem("const_in"), sem("rows_in"), sem("par_in"), sem("wdt_in")
        gain_in = [sem("gain_in0"), sem("gain_in1")]
        tab_in = sem("tab_in")
        out_done = sem("out_done")
        set_t, set_e, set_a, set_w, set_lo = (sem(f"set_{c}") for c in ("t", "e", "a", "w", "lo"))
        x_sq, h_done, h_t, h_hi, h_lo = sem("x_sq"), sem("h_done"), sem("h_t"), sem("h_hi"), sem("h_lo")
        acc0, m_sq, x_done = sem("acc0"), sem("m_sq"), sem("x_done")
        x_root, m_root, x_own, eps_set = sem("x_root"), sem("m_root"), sem("x_own"), sem("eps_set")
        table = sem("table")
        chain = sem("chain")
        pchain = sem("pchain")
        S = {}
        for l in range(DEPTH):
            names = {0: "pad_ok dt_mm dt_abs dt_u dt_ok pre_mm pre_e conv_in conv0 conv1 conv_y x_t x_tok z_ok cb_mm cb_ok "
                        "mff_ok mfb_ok cd_ok seg_mm seg_e w_ok xs_ok y_mm y_v y_g y_sq y_t y_hi y_lo",
                     1: "qkv_in tab_ok qn_sq qn_root qn_r r0 r1 qk_t qk_in s_mm s_max s_e p_ok p_t p_in o_mm o_hi o_lo",
                     2: "lg_e d_pre d_e qk_raw r0 r1 qk_t qk_in v_in g_in s_mm s_w y_mm y_sq y_g y_t y_hi y_lo"}[l % 3]
            for nm in (names + " relu sqr a_hi a_lo").split():
                S[l, nm] = sem(f"l{l}_{nm}")

        def view(buf, at, *shape):
            n = int(np.prod(shape))
            v = buf[:, at:at + n]
            if len(shape) == 2:
                return v.rearrange("p (a b) -> p a b", b=shape[1])
            if len(shape) == 3:
                return v.rearrange("p (a b c) -> p a b c", b=shape[1], c=shape[2])
            return v

        junk = sb("junk", [D_MODEL], mybir.dt.bfloat16)
        dtw = h[:, 0, 0:7 * P].rearrange("p (a b) -> p a b", b=P)
        dt_feat = h[:, 1, 0:SEQ]
        xtok = view(big, 0, TT, SSM_INNER)
        BT, CT = view(big, 4096, SSM_GROUPS, SEQ), view(big, 6144, SSM_GROUPS, SEQ)
        sz = view(big, 8192, TT, SSM_INNER)
        CW = SEQ + 2 * PAD
        cpad = [view(tmp, 2 * CW * i, 2, CW) for i in range(2)]
        cacc = [view(tmp, 4 * CW + 512 * i, 2, SEQ) for i in range(2)]
        xc = [view(tmp, 4 * CW + 1024 + 512 * i, 2, SEQ) for i in range(4)]
        prod = view(tmp, 4 * CW + 3072, SSM_CONV, SEQ)
        MF = [view(tmp, 1024 * fb, TT, 512) for fb in range(2)]
        EX = view(tmp, 2048, TT, 512)
        CD = view(tmp, 3072, TT, 512)
        WM = [view(tmp, 4096, TT, 512), h[:, 0, :].rearrange("p (a b) -> p a b", b=512)]
        CBM = view(tmp, 5120, 2, TT, P)
        CBX = [view(tmp, 5632, TT, P), view(tmp, 8448, TT, P)]
        YT = [view(tmp, 5888 + 512 * i, TT, 256) for i in range(3)]
        XD = view(tmp, 7424, TT, 256)
        XS = [view(tmp, 7936, TT, 256), h[:, 1, 0:512].rearrange("p (a b) -> p a b", b=256)]
        qkv = view(big, 0, TT, 1536)
        qkT = view(big, 3072, 10, SEQ)
        prob = [view(big, 5632 + 512 * i, TT, SEQ) for i in range(2)]
        probT = [view(big, 6656 + 512 * i, TT, SEQ) for i in range(2)]
        tabA = view(tmp, 0, N_TABA)
        gq = view(tmp, 512, 256)
        tw = view(tmp, 768, 4, TT, AD)
        ra = [view(tmp, 1792 + 1280 * j, 1280) for j in range(2)]
        rb = [view(tmp, 4352 + 1280 * j, 1280) for j in range(2)]
        rT = view(big, 0, 16, SEQ)
        vr = view(big, 4096, TT, 4 * RV)
        sg = view(big, 8192, TT, 4 * RV)
        tabR = view(tmp, 0, N_TABR)
        dec = view(tmp, 2048, RH, TT, SEQ)
        rraw = view(tmp, 4096, TT, 512)
        rA, rB = view(tmp, 5120, TT, 512), view(tmp, 6144, TT, 512)
        wt = [view(tmp, 7168 + 512 * i, TT, SEQ) for i in range(2)]
        drow = view(tmp, 8192, TT, 256)
        rl = [view(tmp, 512 * i, 512) for i in range(2)]
        aa = view(tmp, 1024, 512)

        qn_sum, qn_root, qn = (rs[:, 20 * k + 20:20 * k + 40].rearrange("p (j h) -> p j h", j=TT) for k in range(3))

        def rope_att(ops, link, j, gi, done):
            h0, hn = ATT_HEADS[gi]
            b = 1 if gi == 0 else 0
            hv = qkv[:, j, AD * h0:AD * (h0 + hn)].rearrange("p (h d) -> p h d", d=AD)
            if gi == 0:
                link(ops.tensor_tensor(hv, hv, qn[:, j, h0:h0 + hn].unsqueeze(2).to_broadcast([P, hn, AD]), ALU.mult))
            ca, cb = (r[j][:, AD * h0:AD * (h0 + hn)].rearrange("p (h d) -> p h d", d=AD) for r in (ra, rb))
            ops.tensor_tensor(ca, hv, tw[:, 2 * b, j, :].unsqueeze(1).to_broadcast([P, hn, AD]), ALU.mult)
            src = hv.rearrange("p h (a r d) -> p h a r d", a=2, r=2)
            dst = cb.rearrange("p h (a r d) -> p h a r d", a=2, r=2)
            sn = tw[:, 2 * b + 1, j, :].rearrange("p (a r d) -> p a r d", a=2, r=2)
            for a in range(2):
                for r_ in range(2):
                    ins = ops.tensor_tensor(dst[:, :, a, r_, :], src[:, :, a, 1 - r_, :],
                                            sn[:, a, r_, :].unsqueeze(1).to_broadcast([P, hn, AD // 4]), ALU.mult)
            link(ins)
            ops.tensor_tensor(hv, ca, cb, ALU.add).then_inc(done, 1)

        def low_y(V, dve, l, i, g, kk):
            dve.wait_ge(S[l, "y_hi"], 2 * g + kk + 1)
            if kk == 0:
                dve.wait_ge(S[l, "y_hi"], 2 * g + 2)
            V.scalar_tensor_tensor(out=feat[:, 16 + 2 * g + kk, :], in0=ps[7][:, 256 * kk:256 * kk + 256],
                                   scalar=cols[:, i, 192 + 2 * g + kk:193 + 2 * g + kk],
                                   in1=feat[:, 2 * g + kk, :].bitcast(F32), op0=ALU.mult,
                                   op1=ALU.subtract).then_inc(S[l, "y_lo"], 1)

        block = ctx.enter_context(nc.Block())

        @block.sync
        def _(sp):
            def load(q, par_, src, static):
                if not static or q >= 1:
                    sp.wait_ge(lo_done, 4 * q + 2 * par_ - 2)
                dst = raw[:, par_, :]
                if len(src.shape) == 3:
                    dst = dst.rearrange("p (k n) -> p k n", k=src.shape[1])
                sp.dma_start(dst, src).then_inc(raw_in[par_], 16)

            def group_src(wm, c0, hf):
                return wm.rearrange("(k p) n -> p k n", p=P)[:, 4 * hf:4 * hf + 4, c0:c0 + 512]

            def rows_src(wm, u):
                return wm[256 * u:256 * u + 256, :].rearrange("(k p) n -> p k n", p=P)

            for j in range(TT):
                sp.dma_start(x[:, j, :], w["x"][0, j * P:(j + 1) * P, :]).then_inc(x_in[j], 16)
            sp.dma_start(cst[:, :], consts).then_inc(const_in, 16)
            for l in range(DEPTH):
                n = FIRST_UNIT[2 * l]
                kind, i = l % 3, l // 3
                srcs = []
                if kind == 0:
                    wi = w["ssm_w_in"][i]
                    for u in range(XBC_UNITS):
                        c0 = SSM_INNER + 256 * u
                        srcs.append(wi.rearrange("(k p) n -> p k n", p=P)[:, :, c0:c0 + 256])
                    srcs += [group_src(wi, 512 * (u // 2), u % 2) for u in range(Z_UNITS)]
                    srcs += [rows_src(w["ssm_w_out"][i], u) for u in range(SSM_OUT_UNITS)]
                elif kind == 1:
                    srcs += [group_src(w["att_w_in"][i], 512 * ATT_COLS[u // 2], u % 2) for u in range(2 * ATT_GROUPS)]
                    srcs += [rows_src(w["att_w_out"][i], u) for u in range(ATT_OUT_UNITS)]
                else:
                    for q in range(RET_GROUPS):
                        c0 = 512 * q if q < 4 else 512 * (4 + (q - 4) // 2 + 4 * (q % 2))
                        srcs += [group_src(w["ret_w_in"][i], c0, hf) for hf in range(2)]
                    srcs += [rows_src(w["ret_w_out"][i], u) for u in range(RET_OUT_UNITS)]
                for u, src in enumerate(srcs):
                    load((n + u) // 2, (n + u) % 2, src, True)
                    if l == 0 and u == 1:
                        for i_ in range(len(SSM_LAYERS)):
                            cw = w["ssm_conv_w"][i_].rearrange("t (c p) -> (t c) p", p=P)
                            r0, r1 = view(big, 8192 + 256 * i_, P), view(big, 8320 + 256 * i_, P)
                            sp.dma_start(r0[0:96, :], cw[0:96, :]).then_inc(rows_in, 16)
                            sp.dma_start(r1[0:64, :], cw[96:160, :]).then_inc(rows_in, 16)
                            sp.dma_start(r1[64:96, :], w["ssm_conv_b"][i_].rearrange("(c p) -> c p", p=P)).then_inc(rows_in, 16)
                            sp.dma_start(r1[96:112, :], w["ssm_norm"][i_].rearrange("(c p) -> c p", p=P)).then_inc(rows_in, 16)
                            sp.dma_start(view(big, 8704 + 512 * i_, KD, 64),
                                           w["ssm_w_in"][i_][:, SSM_INNER + CONV_DIM:].rearrange("(k p) n -> p k n", p=P)).then_inc(wdt_in, 16)
                q0 = FIRST_UNIT[2 * l + 1] // 2
                w1 = w["mlp_w_in"][l].rearrange("(k p) f -> p k f", p=P)
                w2 = w["mlp_w_out"][l].rearrange("(s k p) n -> p s k n", p=P, k=2)
                load(q0, 0, w1[:, :, 0:256], True)
                load(q0, 1, w1[:, :, 256:512], True)
                with sp.Fori(0, MLP_STEPS // 2 - 1) as it:
                    for b in range(2):
                        load(q0 + 1 + it * 2 + b, 0, w2[:, bass.ds(it * 2 + b, 1), :, :].squeeze(1), False)
                        load(q0 + 1 + it * 2 + b, 1, w1[:, :, bass.ds(it * 512 + 512 + 256 * b, 256)], False)
                load(q0 + MLP_STEPS - 1, 0, w2[:, MLP_STEPS - 2, :, :], True)
                load(q0 + MLP_STEPS - 1, 1, w2[:, MLP_STEPS - 1, :, :], True)
            for j in range(TT):
                sp.wait_ge(x_done, TT * (2 * DEPTH - 1) + j + 1)
                sp.dma_start(out[0, j * P:(j + 1) * P, :], x[:, j, :]).then_inc(out_done, 16)
            sp.wait_ge(out_done, 32)

        @block.gpsimd
        def _(pool):
            steps = [0]

            def link(ins):
                steps[0] += 1
                ins.then_inc(pchain, 1)
                pool.wait_ge(pchain, steps[0])

            gain_rows = []
            for l in range(DEPTH):
                gain_rows += [w["norm_mix_pre"][l], w["norm_mix_post"][l], w["norm_ffn_pre"][l], w["norm_ffn_post"][l]]
            sent = [0]

            def send_gain():
                u = sent[0]
                if u >= len(gain_rows):
                    return
                sent[0] += 1
                if u >= 2:
                    pool.wait_ge(h_done if u % 2 == 0 else x_done, 2 * ((u - 2) // 2) + 2)
                pool.dma_start(gain[:, u % 2, :], gain_rows[u].partition_broadcast(P)).then_inc(gain_in[u % 2], 16)

            nc.gpsimd.memset(ecol[:, 0:1], EPS).then_inc(eps_set, 1)
            send_gain()
            send_gain()
            for i in range(len(SSM_LAYERS)):
                pool.dma_start(par[:, i, 0:64], w["ssm_dt_bias"][i].rearrange("a h -> (a h)").partition_broadcast(P)).then_inc(par_in, 16)
                pool.dma_start(par[:, i, 64:128], w["ssm_a_log"][i].rearrange("a h -> (a h)").partition_broadcast(P)).then_inc(par_in, 16)
                pool.dma_start(par[:, i, 128:160], w["ssm_d"][i].partition_broadcast(P)).then_inc(par_in, 16)

            def turn(s):
                for m in range(2 * FIRST_UNIT[s + 1], 2 * FIRST_UNIT[s + 1] + 4):
                    pool.wait_ge(hi_done, m + 1)
                    hf = slice(m % 2 * HALF, (m % 2 + 1) * HALF)
                    nc.gpsimd.tensor_tensor(wlo[:, m % 4, :], raw[:, m // 2 % 2, hf], whi[:, m % 4, :].bitcast(F32),
                                            ALU.subtract).then_inc(lo_done, 1)

            def rope_ret(l, q):
                pool.wait_ge(S[l, "qk_raw"], 2 * q + 2)
                if q >= 1:
                    pool.wait_ge(S[l, "qk_t"], 2 * q)
                src = rraw[:, 1, :].rearrange("p (h d) -> p h d", h=2)
                cosb = tabR[:, T_COSR + 256:T_COSR + 512].unsqueeze(1).to_broadcast([P, 2, 256])
                nc.gpsimd.tensor_tensor(rA[:, 1, :].rearrange("p (h d) -> p h d", h=2), src, cosb, ALU.mult)
                s5 = rraw[:, 1, :].rearrange("p (h r d) -> p h r d", h=4, r=2)
                o5 = rB[:, 1, :].rearrange("p (h r d) -> p h r d", h=4, r=2)
                sn = tabR[:, T_SINR + 256:T_SINR + 512].rearrange("p (a r d) -> p a r d", a=2, r=2)
                for hd in range(2):
                    for r in range(2):
                        ins = nc.gpsimd.tensor_tensor(o5[:, 2 * hd:2 * hd + 2, r, :], s5[:, 2 * hd:2 * hd + 2, 1 - r, :],
                                                      sn[:, :, r, :], ALU.mult)
                link(ins)
                nc.gpsimd.tensor_tensor(rA[:, 1, :], rA[:, 1, :], rB[:, 1, :], ALU.add).then_inc(S[l, "r1"], 1)

            for l in range(DEPTH):
                kind, i = l % 3, l // 3
                s = 2 * l
                send_gain()
                if kind == 0:
                    pool.wait_ge(h_done, 2 * s + 2)
                    for b in range(2):
                        nc.gpsimd.memset(cpad[b][:, :, 0:PAD], 0.0)
                        nc.gpsimd.memset(cpad[b][:, :, PAD + SEQ:CW], 0.0).then_inc(S[l, "pad_ok"], 1)
                    pool.wait_ge(S[l, "pad_ok"], 2)
                    pool.wait_ge(set_e, 4)
                    for u in range(XBC_UNITS):
                        ct = 2 * u + 1
                        if u >= 1:
                            pool.wait_ge(S[l, "conv1"], u)
                        pool.wait_ge(S[l, "conv_in"], u + 1)
                        if u >= 2:
                            pool.wait_ge(S[l, "conv_y"], 2 * (u - 1))
                        src = cpad[u % 2][:, 1, 0:SEQ]
                        windows = bass.AP(tensor=src.tensor, offset=src.offset, ap=[src.ap[0], [1, SSM_CONV], [1, SEQ]])
                        taps = cols[:, i, ct:5 * CT_N:CT_N].unsqueeze(2).to_broadcast([P, SSM_CONV, SEQ])
                        link(nc.gpsimd.tensor_tensor(prod, windows, taps, ALU.mult))
                        link(nc.gpsimd.tensor_tensor(prod[:, 0:2, :], prod[:, 0:2, :], prod[:, 2:4, :], ALU.add))
                        link(nc.gpsimd.tensor_tensor(prod[:, 0, :], prod[:, 0, :], prod[:, 4, :], ALU.add))
                        nc.gpsimd.tensor_tensor(cacc[u % 2][:, 1, :], prod[:, 0, :], prod[:, 1, :],
                                                ALU.add).then_inc(S[l, "conv1"], 1)
                    pool.wait_ge(S[l, "dt_ok"], 2)
                    dA = dts[:, 1, :].rearrange("p (j d h) -> p j d h", j=2, d=2)
                    pool.wait_ge(S[l, "x_tok"], 8)
                    pool.wait_ge(S[l, "conv_y"], 2 * XBC_UNITS)
                    def exponents(g):
                        if g >= 1:
                            pool.wait_ge(S[l, "seg_mm"], 2 * g)
                        for j in range(TT):
                            nc.gpsimd.tensor_tensor(MF[1][:, j, :].rearrange("p (h t) -> p h t", h=HPG),
                                                    fromon.unsqueeze(1).to_broadcast([P, HPG, P]),
                                                    dA[:, j, 1, HPG * g:HPG * g + HPG].unsqueeze(2).to_broadcast([P, HPG, P]),
                                                    ALU.mult).then_inc(S[l, "mfb_ok"], 1)

                    def sources(g):
                        if g >= 2:
                            pool.wait_ge(S[l, "y_mm"], g - 1)
                        for j in range(TT):
                            ins = nc.gpsimd.tensor_tensor(XS[g % 2][:, j, :].rearrange("p (h d) -> p h d", h=HPG),
                                                          xtok[:, j, 256 * g:256 * g + 256].rearrange("p (h d) -> p h d", h=HPG),
                                                          srcf[:, j, HPG * g:HPG * g + HPG].unsqueeze(2).to_broadcast([P, HPG, SSM_HDIM]),
                                                          ALU.mult)
                        ins.then_inc(S[l, "xs_ok"], 1)

                    exponents(0)
                    pool.wait_ge(S[l, "pre_e"], 1)
                    nc.gpsimd.tensor_tensor(srcf[:, 0, :], fac[:, 2, :], dts[:, 0, 0:32], ALU.mult)
                    link(nc.gpsimd.tensor_tensor(srcf[:, 1, :], fac[:, 3, :], dts[:, 0, 96:128], ALU.mult))
                    def skipped(g):
                        if g >= 1:
                            pool.wait_ge(S[l, "y_g"], g)
                        dsk = par[:, i, 128 + HPG * g:128 + HPG * g + HPG].unsqueeze(2).to_broadcast([P, HPG, SSM_HDIM])
                        for j in range(TT):
                            ins = nc.gpsimd.tensor_tensor(XD[:, j, :].rearrange("p (h d) -> p h d", h=HPG),
                                                          xtok[:, j, 256 * g:256 * g + 256].rearrange("p (h d) -> p h d", h=HPG),
                                                          dsk, ALU.mult)
                        link(ins)

                    def gated(g):
                        pool.wait_ge(S[l, "y_v"], g + 1)
                        if g >= 1:
                            pool.wait_ge(S[l, "y_t"], g)
                            pool.wait_ge(S[l, "y_sq"], 2 * g)
                        link(nc.gpsimd.tensor_tensor(XD, YT[1], XD, ALU.add))
                        nc.gpsimd.tensor_tensor(YT[2], XD, sz[:, :, 256 * g:256 * g + 256], ALU.mult).then_inc(S[l, "y_g"], 1)

                    sources(0)
                    exponents(1)
                    for g in range(SSM_GROUPS):
                        if g >= 1:
                            gated(g - 1)
                        if g + 2 < SSM_GROUPS:
                            exponents(g + 2)
                        skipped(g)
                        if g + 1 < SSM_GROUPS:
                            sources(g + 1)
                    gated(SSM_GROUPS - 1)
                elif kind == 1:
                    pool.wait_ge(h_done, 2 * s + 2)
                    pool.dma_start(tabA, tab_a).then_inc(tab_in, 16)
                    pool.dma_start(gq[:, 0:128], w["att_q_norm"][i].partition_broadcast(P)).then_inc(tab_in, 16)
                    pool.dma_start(gq[:, 128:256], w["att_k_norm"][i].partition_broadcast(P)).then_inc(tab_in, 16)
                    pool.wait_ge(S[l, "tab_ok"], 1)
                    for gi in range(ATT_GROUPS):
                        pool.wait_ge(S[l, "qkv_in"], 2 * gi + 2)
                        if gi == 0:
                            pool.wait_ge(S[l, "qn_r"], 1)
                        rope_att(nc.gpsimd, link, 1, gi, S[l, "r1"])
                else:
                    pool.wait_ge(h_done, 2 * s + 2)
                    pool.dma_start(tabR, tab_r).then_inc(tab_in, 16)
                    pool.dma_start(lg[:, 0:8], w["ret_log2_decay"][i].rearrange("a h -> (a h)").partition_broadcast(P)).then_inc(tab_in, 16)
                    pool.wait_ge(tab_in, 80)
                    for q in range(4):
                        rope_ret(l, q)
                turn(s)
                send_gain()
                send_gain()
                if l < DEPTH - 1:
                    turn(s + 1)
                    send_gain()

        @block.scalar
        def _(act):
            def split(q, par_, static=True):
                act.wait_ge(raw_in[par_], 16 * (q + 1))
                for hf in range(2):
                    if not static or q >= 1:
                        act.wait_ge(w_used, 4 * q + 2 * par_ + hf - 3)
                    nc.scalar.activation(whi[:, 2 * par_ + hf, :], raw[:, par_, hf * HALF:(hf + 1) * HALF],
                                         ACT.Copy).then_inc(hi_done, 1)

            def splitn(n):
                if n < N_UNITS:
                    split(n // 2, n % 2)

            def split_half(m):
                act.wait_ge(raw_in[m // 2 % 2], 16 * (m // 4 + 1))
                act.wait_ge(w_used, m - 3)
                nc.scalar.activation(whi[:, m % 4, :], raw[:, m // 2 % 2, m % 2 * HALF:(m % 2 + 1) * HALF],
                                     ACT.Copy).then_inc(hi_done, 1)

            def squares(s, j):
                if s == 0:
                    act.wait_ge(x_in[j], 16)
                    act.wait_ge(eps_set, 1)
                else:
                    act.wait_ge(x_done, 2 * s - 2 + j + 1)
                nc.scalar.activation(junk[:, :], x[:, j, :], ACT.Square, accum_out=sq[:, j:j + 1]).then_inc(x_sq, 1)
                act.wait_ge(x_sq, 2 * s + j + 1)
                if s % 2 == 0:
                    nc.scalar.activation(sq[:, 2 + j:3 + j], sq[:, j:j + 1], ACT.Sqrt, bias=ecol[:, 0:1],
                                         scale=1.0 / D_MODEL).then_inc(x_root, 1)

            def leading(s, j):
                for c in range(2):
                    act.wait_ge(h_t, 4 * s + 2 * j + c + 1)
                    nc.scalar.activation(feat[:, HT_HI + 4 * c:HT_HI + 4 * c + 4, j * P:(j + 1) * P],
                                         ps[4 + 2 * j + c][:, :].rearrange("p (k t) -> p k t", k=4),
                                         ACT.Copy).then_inc(h_hi, 1)

            def post(s, j):
                if j == 0:
                    act.wait_ge(acc0, s + 1)
                else:
                    act.wait_ge(w_used, 2 * (FIRST_UNIT + [N_UNITS])[s + 1])
                nc.scalar.activation(junk[:, :], pacc[:, 1024 * j:1024 * j + 1024], ACT.Square,
                                     accum_out=sq[:, 4 + j:5 + j]).then_inc(m_sq, 1)
                act.wait_ge(m_sq, 2 * s + j + 1)
                if s % 2 or s // 2 % 3 == 0:
                    act.wait_ge(x_own, sum(1 for q in range(s + 1) if q % 2 or q // 2 % 3 == 0))
                    bias = ecol[:, 2 + j:3 + j]
                else:
                    bias = ecol[:, 0:1]
                nc.scalar.activation(sq[:, 6 + j:7 + j], sq[:, 4 + j:5 + j], ACT.Sqrt, bias=bias,
                                     scale=1.0 / D_MODEL).then_inc(m_root, 1)

            def turn(s):
                nc.scalar.activation(ecol[:, 4:5], ecol[:, 0:1], ACT.Sqrt).then_inc(table, 1)
                act.wait_ge(table, s + 1)
                post(s, 0)
                if s + 1 < 2 * DEPTH:
                    splitn(FIRST_UNIT[s + 1])
                    if s % 2:
                        squares(s + 1, 0)
                post(s, 1)
                if s + 1 < 2 * DEPTH:
                    leading(s + 1, 0)
                    if s % 2:
                        split_half(2 * FIRST_UNIT[s + 1] + 2)
                        squares(s + 1, 1)
                        split_half(2 * FIRST_UNIT[s + 1] + 3)
                    else:
                        splitn(FIRST_UNIT[s + 1] + 1)
                    leading(s + 1, 1)
                    if s % 2 == 0:
                        squares(s + 1, 0)
                        squares(s + 1, 1)

            squares(0, 0)
            squares(0, 1)
            splitn(0)
            leading(0, 0)
            leading(0, 1)
            splitn(1)
            act.wait_ge(par_in, 16 * 6)
            act.wait_ge(wdt_in, 16 * 2)
            for i in range(2):
                nc.scalar.activation(negA[:, i, :], par[:, i, 64:128], ACT.Exp).then_inc(set_a, 1)
                nc.scalar.activation(wdt_hi[:, i, :], view(big, 8704 + 512 * i, 512), ACT.Copy).then_inc(set_w, 1)
            act.wait_ge(set_t, 1)
            for i in range(2):
                nc.scalar.activation(cols[:, i, 0:96], ps[0][:, 256 * i:256 * i + 96], ACT.Copy).then_inc(set_e, 1)
                nc.scalar.activation(cols[:, i, 96:208], ps[0][:, 256 * i + 128:256 * i + 240], ACT.Copy).then_inc(set_e, 1)
            for l in range(DEPTH):
                kind, s, n0 = l % 3, 2 * l, FIRST_UNIT[2 * l]
                i = l // 3
                if kind == 0:
                    def conv_finish(u):
                        for cc in range(2):
                            ct = 2 * u + cc
                            act.wait_ge(S[l, "conv0" if cc == 0 else "conv1"], u + 1)
                            if ct < 16:
                                if u >= 4:
                                    act.wait_ge(S[l, "x_t"], u - 3)
                                dst = xc[u % 4][:, cc, :]
                            else:
                                dst = (BT if ct < 24 else CT)[:, ct % 8, :]
                            nc.scalar.activation(dst, cacc[u % 2][:, cc, :], ACT.Silu,
                                                 bias=cols[:, i, 160 + ct:161 + ct]).then_inc(S[l, "conv_y"], 1)

                    def y_leading(g):
                        act.wait_ge(S[l, "y_t"], g + 1)
                        for kk in range(2):
                            nc.scalar.activation(feat[:, 2 * g + kk, :], ps[7][:, 256 * kk:256 * kk + 256], ACT.Identity,
                                                 scale=cols[:, i, 192 + 2 * g + kk:193 + 2 * g + kk]).then_inc(S[l, "y_hi"], 1)

                    def x_evac(u):
                        act.wait_ge(S[l, "x_t"], u + 1)
                        nc.scalar.activation(xtok[:, :, 256 * u:256 * u + 256],
                                             ps[6 + u % 2][:, :].rearrange("p (j c) -> p j c", j=2),
                                             ACT.Copy).then_inc(S[l, "x_tok"], 1)

                    act.wait_ge(set_e, 4)
                    for u in range(XBC_UNITS):
                        if u == 5:
                            act.wait_ge(S[l, "dt_mm"], 1)
                            nc.scalar.activation(dt_feat[0:64, :], ps[3][0:64, 0:SEQ], ACT.Copy).then_inc(S[l, "dt_mm"], 1)
                        act.wait_ge(w_used, 2 * (n0 + u) + 2)
                        if u >= 2:
                            act.wait_ge(S[l, "conv0"], u - 1)
                            act.wait_ge(S[l, "conv1"], u - 1)
                        nc.scalar.activation(cpad[u % 2][:, :, PAD:PAD + SEQ],
                                             ps[4 + u % 2][:, :].rearrange("p (c t) -> p c t", c=2),
                                             ACT.Copy).then_inc(S[l, "conv_in"], 1)
                        if u == 7:
                            act.wait_ge(S[l, "dt_abs"], 1)
                            nc.scalar.activation(dtw[:, 1, :], dtw[:, 1, :], ACT.Exp, scale=-1.0).then_inc(S[l, "dt_u"], 1)
                        splitn(n0 + u + 2)
                        if u >= 1:
                            conv_finish(u - 1)
                        if 3 <= u < 11:
                            x_evac(u - 3)
                    conv_finish(XBC_UNITS - 1)
                    for u in range(Z_UNITS):
                        if u % 2:
                            act.wait_ge(w_used, 2 * (n0 + XBC_UNITS + u) + 2)
                            for j in range(TT):
                                nc.scalar.activation(sz[:, j, 256 * (u - 1):256 * (u + 1)],
                                                     ps[2 * (u // 2 % 2) + j][:, :], ACT.Silu).then_inc(S[l, "z_ok"], 1)
                        splitn(n0 + XBC_UNITS + u + 2)

                    act.wait_ge(S[l, "pre_mm"], 1)
                    nc.scalar.activation(fac[:, :, :].rearrange("p a h -> p (a h)"), ps[7][:, 0:128], ACT.Exp).then_inc(S[l, "pre_e"], 1)

                    def exps(g):
                        for j in range(TT):
                            act.wait_ge(S[l, "seg_mm"], 2 * g + j + 1)
                            if g >= 1:
                                act.wait_ge(S[l, "w_ok"], 2 * (g - 1) + j + 1)
                            nc.scalar.activation(EX[:, j, :], ps[5 + j][:, :], ACT.Exp).then_inc(S[l, "seg_e"], 1)

                    def forward(g):
                        act.wait_ge(S[l, "cb_ok"], 3 * g + 1)
                        for j in range(TT):
                            if g >= 1:
                                act.wait_ge(S[l, "w_ok"], 2 * (g - 1) + j + 1)
                            for hd in range(HPG):
                                c = 64 * j + HPG * g + hd
                                ins = nc.scalar.activation(CD[:, j, P * hd:P * hd + P], CBM[:, 0, j, :], ACT.Identity, scale=dts[:, 0, c:c + 1])
                            ins.then_inc(S[l, "cd_ok"], 1)

                    def y_squares(g):
                        act.wait_ge(S[l, "y_g"], g + 1)
                        for j in range(TT):
                            nc.scalar.activation(junk[:, 256 * j:256 * j + 256], YT[2][:, j, :], ACT.Square,
                                                 accum_out=sq[:, 16 + 8 * j + g:17 + 8 * j + g]).then_inc(S[l, "y_sq"], 1)
                        act.wait_ge(S[l, "y_sq"], 2 * g + 2)

                    exps(0)
                    forward(0)
                    for g in range(SSM_GROUPS):
                        if g + 1 < SSM_GROUPS:
                            forward(g + 1)
                            exps(g + 1)
                        if g >= 1:
                            y_squares(g - 1)
                            y_leading(g - 1)
                    y_squares(SSM_GROUPS - 1)
                    y_leading(SSM_GROUPS - 1)
                    for u in range(SSM_OUT_UNITS - 2):
                        splitn(n0 + XBC_UNITS + Z_UNITS + u + 2)
                elif kind == 1:
                    def pair_evac(c):
                        act.wait_ge(S[l, "qk_t"], c + 1)
                        hd = ATT_PAIRS[c]
                        nc.scalar.activation(qkT[:, hd:hd + 2, :], ps[6 + c % 2][:, :].rearrange("p (a t) -> p a t", a=2),
                                             ACT.Copy).then_inc(S[l, "qk_in"], 1)

                    for u in range(2 * ATT_GROUPS):
                        if u < 2 * ATT_GROUPS - 1:
                            splitn(n0 + u + 2)
                        if u % 2 == 0:
                            continue
                        gi = u // 2
                        h0, hn = ATT_HEADS[gi]
                        c = AD * 4 * ATT_COLS[gi]
                        act.wait_ge(w_used, 2 * (n0 + u) + 2)
                        for j in range(TT):
                            nc.scalar.activation(qkv[:, j, c:c + 512], ps[2 * gi + j][:, :], ACT.Copy).then_inc(S[l, "qkv_in"], 1)
                        if gi == ATT_GROUPS - 1:
                            pair_evac(0)
                            pair_evac(1)
                        for j in range(TT):
                            for k in range(hn):
                                nc.scalar.activation(junk[:, AD * (hn * j + k):AD * (hn * j + k + 1)], ps[2 * gi + j][:, AD * k:AD * k + AD],
                                                     ACT.Square, accum_out=qn_sum[:, j, h0 + k:h0 + k + 1]).then_inc(S[l, "qn_sq"], 1)
                        act.wait_ge(S[l, "qn_sq"], 2 * (2 + 4 * gi))
                        nc.scalar.activation(qn_root[:, :, h0:h0 + hn], qn_sum[:, :, h0:h0 + hn], ACT.Sqrt, bias=ecol[:, 0:1],
                                             scale=1.0 / AD).then_inc(S[l, "qn_root"], 1)

                    def exp_head(hd):
                        act.wait_ge(S[l, "s_max"], hd + 1)
                        if hd >= 2:
                            act.wait_ge(S[l, "p_t"], hd - 1)
                        for j in range(TT):
                            nc.scalar.activation(prob[hd % 2][:, j, :], ps[hd % 2][:, j * SEQ:(j + 1) * SEQ], ACT.Exp,
                                                 bias=sq[:, 48 + 2 * (hd % 2) + j:49 + 2 * (hd % 2) + j], scale=qn[:, j, hd:hd + 1],
                                                 accum_out=sq[:, 52 + 2 * (hd % 2) + j:53 + 2 * (hd % 2) + j]).then_inc(S[l, "s_e"], 1)

                    exp_head(0)
                    pair_evac(2)
                    exp_head(1)
                    pair_evac(3)
                    pair_evac(4)
                    for t in range(AQ + 2):
                        if t < AQ:
                            act.wait_ge(S[l, "p_t"], t + 1)
                            if t >= 2:
                                act.wait_ge(S[l, "o_mm"], t - 1)
                            nc.scalar.activation(probT[t % 2], ps[2 + t % 2][:, :].rearrange("p (a t) -> p a t", a=2),
                                                 ACT.Copy).then_inc(S[l, "p_in"], 1)
                        if t + 2 < AQ:
                            exp_head(t + 2)
                        if t >= 2:
                            hd = t - 2
                            act.wait_ge(S[l, "o_mm"], hd + 1)
                            nc.scalar.activation(feat[:, hd, :], ps[4 + hd % 2][:, 0:SEQ], ACT.Copy).then_inc(S[l, "o_hi"], 1)
                        if t == AQ:
                            splitn(n0 + 2 * ATT_GROUPS + 1)
                    for u in range(ATT_OUT_UNITS - 2):
                        splitn(n0 + 2 * ATT_GROUPS + u + 2)
                else:
                    def powers():
                        act.wait_ge(tab_in, 80)
                        nc.scalar.activation(lg[:, 8:16], lg[:, 0:8], ACT.Exp, scale=float(np.log(2.0))).then_inc(S[l, "lg_e"], 1)

                    def logs():
                        act.wait_ge(S[l, "lg_e"], 2)
                        nc.scalar.activation(lg[:, 24:32], lg[:, 16:24], ACT.Ln).then_inc(S[l, "lg_e"], 1)

                    def decay(hd):
                        act.wait_ge(S[l, "d_pre"], hd + 1)
                        nc.scalar.activation(dec[:, hd, :, :], dec[:, hd, :, :], ACT.Exp).then_inc(S[l, "d_e"], 1)

                    def ysq(hd):
                        act.wait_ge(S[l, "y_mm"], hd + 1)
                        for j in range(TT):
                            nc.scalar.activation(rA[:, j, :], ps[4 + j][:, :], ACT.Square,
                                                 accum_out=sq[:, 32 + j:33 + j]).then_inc(S[l, "y_sq"], 1)

                    for q in range(RET_GROUPS):
                        splitn(n0 + 2 * q + 2)
                        if q >= 4 and q % 2:
                            ysq((q - 4) // 2)
                        act.wait_ge(w_used, 2 * (n0 + 2 * q + 1) + 2)
                        for j in range(TT):
                            src = ps[2 * (q % 2) + j][:, :]
                            if q < 4:
                                if q >= 1:
                                    act.wait_ge(S[l, "r0" if j == 0 else "r1"], q)
                                nc.scalar.activation(rraw[:, j, :], src, ACT.Copy).then_inc(S[l, "qk_raw"], 1)
                            elif q % 2 == 0:
                                hd = (q - 4) // 2
                                nc.scalar.activation(vr[:, j, RV * hd:RV * hd + RV], src, ACT.Copy).then_inc(S[l, "v_in"], 1)
                            else:
                                hd = (q - 4) // 2
                                nc.scalar.activation(sg[:, j, RV * hd:RV * hd + RV], src, ACT.Silu).then_inc(S[l, "g_in"], 1)
                        if q < RET_GROUPS - 1:
                            splitn(n0 + 2 * q + 3)
                        if q < 4:
                            for b in range(2):
                                act.wait_ge(S[l, "qk_t"], 2 * q + b + 1)
                                nc.scalar.activation(rT[:, 4 * q + 2 * b:4 * q + 2 * b + 2, :],
                                                     ps[4 + b][:, :].rearrange("p (a t) -> p a t", a=2),
                                                     ACT.Copy).then_inc(S[l, "qk_in"], 1)
                            if q == 0:
                                powers()
                            elif q == 1:
                                logs()
                            else:
                                decay(2 * q - 4)
                                decay(2 * q - 3)
                    for u in range(RET_OUT_UNITS):
                        act.wait_ge(S[l, "y_t"], u + 1)
                        nc.scalar.activation(feat[:, 2 * u:2 * u + 2, :], ps[4 + (u + 2) % 4][:, :].rearrange("p (a t) -> p a t", a=2),
                                             ACT.Copy).then_inc(S[l, "y_hi"], 1)
                        if u < RET_OUT_UNITS - 1:
                            splitn(n0 + 2 * RET_GROUPS + u + 1)
                turn(s)

                s += 1
                n0 = FIRST_UNIT[s]
                q0 = n0 // 2

                def relu(st, b, q, par_, static):
                    act.wait_ge(w_used, 4 * q + 2 * par_ + 2)
                    if not static or st >= 2:
                        act.wait_ge(S[l, "a_lo"], st - 1)
                    nc.scalar.activation(rl[b], ps[4 + b][:, :], ACT.Relu).then_inc(S[l, "relu"], 1)
                    act.wait_ge(S[l, "relu"], st + 1)
                    nc.scalar.activation(feat[:, 4 * b:4 * b + 2, :], rl[b].rearrange("p (a t) -> p a t", a=2),
                                         ACT.Square).then_inc(S[l, "a_hi"], 1)

                relu(0, 0, q0, 0, True)
                splitn(n0 + 2)
                relu(1, 1, q0, 1, True)
                splitn(n0 + 3)
                with act.Fori(0, MLP_STEPS // 2 - 1) as it:
                    for b in range(2):
                        q = q0 + 1 + it * 2 + b
                        split(q + 1, 0, False)
                        relu(it * 2 + 2 + b, b, q, 1, False)
                        split(q + 1, 1, False)
                turn(s)

        @block.vector
        def _(dve):
            steps = [0]
            V = nc.vector

            def link(ins):
                steps[0] += 1
                ins.then_inc(chain, 1)
                dve.wait_ge(chain, steps[0])

            def split(q, par_):
                for hf in range(2):
                    dve.wait_ge(hi_done, 4 * q + 2 * par_ + hf + 1)
                    V.tensor_tensor(wlo[:, 2 * par_ + hf, :], raw[:, par_, hf * HALF:(hf + 1) * HALF],
                                    whi[:, 2 * par_ + hf, :].bitcast(F32), ALU.subtract).then_inc(lo_done, 1)

            def splitn(n):
                if n < N_UNITS:
                    split(n // 2, n % 2)

            def rsqrt(dst, v, scratch, done=None):
                link(V.tensor_scalar(dst.bitcast(I32), v.bitcast(I32), -0.5, 1597463007.0, ALU.mult, ALU.add))
                for it in range(3):
                    link(V.tensor_tensor(scratch, v, dst, ALU.mult))
                    link(V.tensor_tensor(scratch, scratch, dst, ALU.mult))
                    link(V.tensor_scalar(scratch, scratch, -0.5, 1.5, ALU.mult, ALU.add))
                    ins = V.tensor_tensor(dst, dst, scratch, ALU.mult)
                    if it == 2 and done is not None:
                        ins.then_inc(done, 1)
                        dve.wait_ge(done, 1)
                    else:
                        link(ins)

            def take_gain(u):
                dve.wait_ge(gain_in[u % 2], 16 * (u // 2 + 1))

            def normed(s, j):
                dve.wait_ge(x_root, s + j + 1)
                link(V.reciprocal(rs[:, j:j + 1], sq[:, 2 + j:3 + j]))
                if j == 0:
                    take_gain(2 * s)
                V.scalar_tensor_tensor(out=h[:, j, :], in0=x[:, j, :], scalar=rs[:, j:j + 1], in1=gain[:, 2 * s % 2, :],
                                       op0=ALU.mult, op1=ALU.mult).then_inc(h_done, 1)

            def gained(s, j):
                if j == 0:
                    take_gain(2 * s)
                dve.wait_ge(x_done, 2 * (s - 1) + j + 1)
                V.tensor_tensor(h[:, j, :], x[:, j, :], gain[:, 2 * s % 2, :], ALU.mult).then_inc(h_done, 1)

            def lows(s, j):
                for c in range(2):
                    dve.wait_ge(h_hi, 4 * s + 2 * j + c + 1)
                    tk = slice(j * P, (j + 1) * P)
                    V.tensor_tensor(feat[:, HT_LO + 4 * c:HT_LO + 4 * c + 4, tk],
                                    ps[4 + 2 * j + c][:, :].rearrange("p (k t) -> p k t", k=4),
                                    feat[:, HT_HI + 4 * c:HT_HI + 4 * c + 4, tk].bitcast(F32),
                                    ALU.subtract).then_inc(h_lo, 1)

            def post(s, j, lows_between=False):
                u = 2 * s + 1
                dve.wait_ge(m_root, 2 * s + j + 1)
                link(V.reciprocal(rs[:, 4 + j:5 + j], sq[:, 6 + j:7 + j]))
                if j == 0:
                    take_gain(u)
                link(V.scalar_tensor_tensor(out=h[:, j, :], in0=pacc[:, 1024 * j:1024 * j + 1024], scalar=rs[:, 4 + j:5 + j],
                                            in1=gain[:, u % 2, :], op0=ALU.mult, op1=ALU.mult))
                if lows_between:
                    lows(s + 1, 0)
                V.tensor_tensor(x[:, j, :], x[:, j, :], h[:, j, :], ALU.add).then_inc(x_done, 1)
                if s % 2 == 0:
                    gained(s + 1, j)

            def turn(s):
                post(s, 0)
                if s + 1 < 2 * DEPTH and s % 2:
                    normed(s + 1, 0)
                post(s, 1, s + 1 < 2 * DEPTH and s % 2 == 1)
                if s + 1 < 2 * DEPTH:
                    if s % 2:
                        normed(s + 1, 1)
                    else:
                        lows(s + 1, 0)
                    lows(s + 1, 1)
                    if s % 2 == 0:
                        dve.wait_ge(x_sq, 2 * s + 4)
                        link(V.tensor_scalar(rs[:, 2:4], sq[:, 0:2], 1.0 / D_MODEL, EPS, ALU.mult, ALU.add))
                        V.scalar_tensor_tensor(out=ecol[:, 2:4], in0=rs[:, 2:4], scalar=EPS, in1=rs[:, 2:4],
                                               op0=ALU.mult, op1=ALU.mult).then_inc(x_own, 1)
                    dve.wait_ge(lo_done, 2 * FIRST_UNIT[s + 1] + 4)

            for j in range(TT):
                normed(0, j)
            splitn(0)
            for j in range(TT):
                lows(0, j)
            splitn(1)
            for i in range(2):
                dve.wait_ge(set_a, i + 1)
                link(V.tensor_scalar(negA[:, i, :], negA[:, i, :], -1.0, None, ALU.mult))
                dve.wait_ge(set_w, i + 1)
                V.tensor_tensor(wdt_lo[:, i, :], view(big, 8704 + 512 * i, 512), wdt_hi[:, i, :].bitcast(F32),
                                ALU.subtract).then_inc(set_lo, 1)
            for l in range(DEPTH):
                kind, s, n0 = l % 3, 2 * l, FIRST_UNIT[2 * l]
                i = l // 3
                if kind == 0:
                    v, av, r = (dtw[:, k, :] for k in range(3))
                    den, z, z2, p_ = (dtw[:, k, :] for k in range(3, 7))

                    def dt_first():
                        dve.wait_ge(S[l, "dt_mm"], 3)
                        link(V.tensor_tensor(v.rearrange("p (j d) -> p j d", j=2), ps[2][:, 0:128].rearrange("p (j d) -> p j d", j=2),
                                             par[:, i, 0:64].unsqueeze(1).to_broadcast([P, 2, 64]), ALU.add))
                        V.scalar_tensor_tensor(out=av, in0=v, scalar=-1.0, in1=v, op0=ALU.mult, op1=ALU.max).then_inc(S[l, "dt_abs"], 1)
                        V.tensor_scalar(r, v, 0.0, None, ALU.max)

                    def dt_rest():
                        dve.wait_ge(S[l, "dt_u"], 1)
                        link(V.tensor_scalar(den, av, 2.0, None, ALU.add))
                        link(V.reciprocal(den, den))
                        link(V.tensor_tensor(z, av, den, ALU.mult))
                        link(V.tensor_tensor(z2, z, z, ALU.mult))
                        link(V.tensor_scalar(p_, z2, 1.0 / 15, None, ALU.mult))
                        for k in (13, 11, 9, 7, 5, 3):
                            link(V.scalar_tensor_tensor(out=p_, in0=p_, scalar=1.0 / k, in1=z2, op0=ALU.add, op1=ALU.mult))
                        link(V.scalar_tensor_tensor(out=p_, in0=p_, scalar=1.0, in1=z, op0=ALU.add, op1=ALU.mult))
                        V.scalar_tensor_tensor(out=dts[:, 0, :], in0=p_, scalar=2.0, in1=r, op0=ALU.mult,
                                               op1=ALU.add).then_inc(S[l, "dt_ok"], 1)
                        dve.wait_ge(S[l, "dt_ok"], 1)
                        V.tensor_tensor(dts[:, 1, :].rearrange("p (j d) -> p j d", j=2), dts[:, 0, :].rearrange("p (j d) -> p j d", j=2),
                                        negA[:, i, :].unsqueeze(1).to_broadcast([P, 2, 64]), ALU.mult).then_inc(S[l, "dt_ok"], 1)

                    dve.wait_ge(set_e, 4)
                    for u in range(XBC_UNITS):
                        ct = 2 * u
                        if u == 6:
                            dt_first()
                        if u == 8:
                            dt_rest()
                        dve.wait_ge(S[l, "conv_in"], u + 1)
                        if u >= 2:
                            dve.wait_ge(S[l, "conv_y"], 2 * (u - 1))
                        if u == 0:
                            dve.wait_ge(S[l, "pad_ok"], 2)
                        o = cacc[u % 2][:, 0, :]
                        for t in range(SSM_CONV):
                            tap = cols[:, i, CT_N * t + ct:CT_N * t + ct + 1]
                            src = cpad[u % 2][:, 0, t:t + SEQ]
                            if t == 0:
                                ins = V.tensor_scalar(o, src, tap, None, ALU.mult)
                            else:
                                ins = V.scalar_tensor_tensor(out=o, in0=src, scalar=tap, in1=o, op0=ALU.mult, op1=ALU.add)
                            if t < SSM_CONV - 1:
                                link(ins)
                        ins.then_inc(S[l, "conv0"], 1)
                        splitn(n0 + u + 2)
                    def masked(g):
                        dve.wait_ge(S[l, "cb_mm"], g + 1)
                        if g == 0:
                            dve.wait_ge(S[l, "conv_y"], 2 * XBC_UNITS)
                            dve.wait_ge(S[l, "x_tok"], 8)
                        else:
                            dve.wait_ge(S[l, "cd_ok"], 2 * g)
                        if g >= 2:
                            dve.wait_ge(S[l, "y_mm"], g - 1)
                        cb = ps[4][:, :].rearrange("p (a j t) -> p a j t", a=2, j=2)
                        for b, m in enumerate((upto, after)):
                            V.tensor_tensor(CBM[:, b, :, :], cb[:, 0, :, :], m.unsqueeze(1).to_broadcast([P, 2, P]),
                                            ALU.mult).then_inc(S[l, "cb_ok"], 1)
                        V.tensor_copy(CBX[g % 2], cb[:, 1, :, :]).then_inc(S[l, "cb_ok"], 1)

                    def exponents(g):
                        for j in range(TT):
                            if g >= 1:
                                dve.wait_ge(S[l, "seg_mm"], 2 * (g - 1) + j + 1)
                            for hd in range(HPG):
                                c = 64 * j + HPG * g + hd
                                ins = V.tensor_scalar(MF[0][:, j, P * hd:P * hd + P], upto, dts[:, 1, c:c + 1], None, ALU.mult)
                            ins.then_inc(S[l, "mff_ok"], 1)

                    def weights(g):
                        dve.wait_ge(S[l, "cb_ok"], 3 * g + 3)
                        for j in range(TT):
                            dve.wait_ge(S[l, "cd_ok"], 2 * g + j + 1)
                            for hd in range(HPG):
                                c = 64 * j + 32 + HPG * g + hd
                                o = CD[:, j, P * hd:P * hd + P]
                                ins = V.scalar_tensor_tensor(out=o, in0=CBM[:, 1, j, :], scalar=dts[:, 0, c:c + 1], in1=o,
                                                             op0=ALU.mult, op1=ALU.add)
                            link(ins)
                            dve.wait_ge(S[l, "seg_e"], 2 * g + j + 1)
                            if g >= 2 and j == 0:
                                dve.wait_ge(S[l, "y_mm"], g - 1)
                            V.tensor_tensor(WM[g % 2][:, j, :], EX[:, j, :], CD[:, j, :], ALU.mult).then_inc(S[l, "w_ok"], 1)

                    def joined(g):
                        dve.wait_ge(S[l, "y_mm"], g + 1)
                        if g >= 1:
                            dve.wait_ge(S[l, "y_g"], g)
                        for j in range(TT):
                            ins = V.tensor_tensor(YT[0][:, j, :].rearrange("p (h d) -> p h d", h=HPG),
                                                  ps[g % 2][:, 256 * j:256 * j + 256].rearrange("p (h d) -> p h d", h=HPG),
                                                  fac[:, j, HPG * g:HPG * g + HPG].unsqueeze(2).to_broadcast([P, HPG, SSM_HDIM]),
                                                  ALU.mult)
                        link(ins)
                        V.tensor_tensor(YT[1], ps[2 + g % 2][:, :].rearrange("p (j c) -> p j c", j=2), YT[0],
                                        ALU.add).then_inc(S[l, "y_v"], 1)

                    for u in range(Z_UNITS):
                        splitn(n0 + XBC_UNITS + u + 2)
                        if u == 1:
                            dve.wait_ge(S[l, "conv_y"], 2 * XBC_UNITS)
                            dve.wait_ge(S[l, "x_tok"], 8)
                            exponents(0)
                    masked(0)
                    exponents(1)
                    weights(0)
                    for g in range(SSM_GROUPS):
                        if g >= 1:
                            joined(g - 1)
                        if g + 1 < SSM_GROUPS:
                            masked(g + 1)
                        if g + 2 < SSM_GROUPS:
                            exponents(g + 2)
                        if g + 1 < SSM_GROUPS:
                            weights(g + 1)
                        if 1 <= g < SSM_GROUPS - 1:
                            for kk in range(2):
                                low_y(V, dve, l, i, g - 1, kk)
                    joined(SSM_GROUPS - 1)
                    for kk in range(2):
                        low_y(V, dve, l, i, SSM_GROUPS - 2, kk)
                    for kk in range(2):
                        low_y(V, dve, l, i, SSM_GROUPS - 1, kk)
                    dve.wait_ge(S[l, "y_sq"], 2 * SSM_GROUPS)
                    link(V.tensor_reduce(rs[:, 10:12], sq[:, 16:32].rearrange("p (j g) -> p j g", j=2), AX.X, ALU.add))
                    link(V.tensor_scalar(rs[:, 12:14], rs[:, 10:12], 1.0 / SSM_INNER, EPS, ALU.mult, ALU.add))
                    V.tensor_scalar(ecol[:, 2:4], rs[:, 12:14], EPS, None, ALU.mult).then_inc(x_own, 1)
                    for u in range(SSM_OUT_UNITS - 2):
                        splitn(n0 + XBC_UNITS + Z_UNITS + u + 2)
                    turn(s)
                elif kind == 1:
                    splitn(n0 + 2)
                    splitn(n0 + 3)
                    dve.wait_ge(tab_in, 48)
                    for b in range(2):
                        V.tensor_tensor(tw[:, 2 * b, :, :], tabA[:, 0:256].rearrange("p (j d) -> p j d", j=2),
                                        gq[:, 128 * b:128 * b + 128].unsqueeze(1).to_broadcast([P, 2, AD]), ALU.mult)
                    for b in range(2):
                        for a in range(2):
                            for r_ in range(2):
                                o = 64 * a + 32 * r_
                                og = 128 * b + 64 * a + 32 * (1 - r_)
                                ins = V.tensor_tensor(tw[:, 2 * b + 1, :, o:o + 32],
                                                      tabA[:, 256:512].rearrange("p (j d) -> p j d", j=2)[:, :, o:o + 32],
                                                      gq[:, og:og + 32].unsqueeze(1).to_broadcast([P, 2, 32]), ALU.mult)
                    ins.then_inc(S[l, "tab_ok"], 1)
                    def factors(gi):
                        h0, hn = ATT_HEADS[gi]
                        q = qn[:, :, h0:h0 + hn]
                        dve.wait_ge(S[l, "qn_root"], gi + 1)
                        ins = V.reciprocal(q, qn_root[:, :, h0:h0 + hn])
                        if gi > 0:
                            link(ins)
                            ins = V.tensor_scalar(q, q, float(AD) ** -0.5, None, ALU.mult)
                        ins.then_inc(S[l, "qn_r"], 1)
                        if gi == 0:
                            dve.wait_ge(S[l, "qn_r"], 1)

                    for gi in range(ATT_GROUPS):
                        if gi > 0:
                            splitn(n0 + 2 * gi + 2)
                        if gi == 1:
                            splitn(n0 + 2 * gi + 3)
                        if gi == 0:
                            factors(0)
                        dve.wait_ge(S[l, "qkv_in"], 2 * gi + 1)
                        rope_att(V, link, 0, gi, S[l, "r0"])
                        if gi == 1:
                            factors(gi)

                    def smax(hd):
                        dve.wait_ge(S[l, "s_mm"], hd + 1)
                        if hd == 0:
                            dve.wait_ge(S[l, "qn_r"], 2)
                        if hd == 4:
                            dve.wait_ge(S[l, "qn_r"], 3)
                        m = sq[:, 56 + 2 * (hd % 2):58 + 2 * (hd % 2)]
                        link(V.tensor_reduce(m, ps[hd % 2][:, :].rearrange("p (j s) -> p j s", j=2), AX.X, ALU.max))
                        V.scalar_tensor_tensor(out=sq[:, 48 + 2 * (hd % 2):50 + 2 * (hd % 2)], in0=m, scalar=-1.0, in1=qn[:, :, hd],
                                               op0=ALU.mult, op1=ALU.mult).then_inc(S[l, "s_max"], 1)

                    def divided(hd):
                        dve.wait_ge(S[l, "s_e"], 2 * hd + 2)
                        if hd >= 1:
                            dve.wait_ge(S[l, "p_ok"], 2 * hd)
                        link(V.reciprocal(rs[:, 100:102], sq[:, 52 + 2 * (hd % 2):54 + 2 * (hd % 2)]))
                        for j in range(TT):
                            V.tensor_scalar(prob[hd % 2][:, j, :], prob[hd % 2][:, j, :], rs[:, 100 + j:101 + j], None,
                                            ALU.mult).then_inc(S[l, "p_ok"], 1)

                    smax(0)
                    smax(1)
                    divided(0)
                    factors(2)
                    for t in range(AQ + 2):
                        if t + 1 < AQ:
                            divided(t + 1)
                        if t + 2 < AQ:
                            smax(t + 2)
                        if t >= 2:
                            hd = t - 2
                            dve.wait_ge(S[l, "o_hi"], hd + 1)
                            V.tensor_tensor(feat[:, 8 + hd, :], ps[4 + hd % 2][:, 0:SEQ], feat[:, hd, :].bitcast(F32),
                                            ALU.subtract).then_inc(S[l, "o_lo"], 1)
                        if t == AQ:
                            splitn(n0 + 2 * ATT_GROUPS + 1)
                    for u in range(ATT_OUT_UNITS - 2):
                        splitn(n0 + 2 * ATT_GROUPS + u + 2)
                    turn(s)
                else:
                    def one_minus():
                        dve.wait_ge(S[l, "lg_e"], 1)
                        V.tensor_scalar(lg[:, 16:24], lg[:, 8:16], -1.0, 1.0, ALU.mult, ALU.add).then_inc(S[l, "lg_e"], 1)

                    def log_gamma():
                        dve.wait_ge(S[l, "lg_e"], 3)
                        link(V.tensor_scalar(lg[:, 32:40], lg[:, 16:24], 1.0, None, ALU.is_equal))
                        V.tensor_tensor(lg[:, 40:48], lg[:, 24:32], lg[:, 32:40], ALU.add)
                        link(V.scalar_tensor_tensor(out=lg[:, 48:56], in0=lg[:, 16:24], scalar=-1.0, in1=lg[:, 32:40], op0=ALU.add, op1=ALU.add))
                        link(V.reciprocal(lg[:, 48:56], lg[:, 48:56]))
                        link(V.scalar_tensor_tensor(out=lg[:, 48:56], in0=lg[:, 48:56], scalar=-1.0, in1=lg[:, 8:16], op0=ALU.mult, op1=ALU.mult))
                        link(V.tensor_tensor(lg[:, 56:64], lg[:, 48:56], lg[:, 40:48], ALU.mult))

                    def decay(hd):
                        link(V.tensor_scalar(drow, tabR[:, T_AHEAD:T_AHEAD + 512].rearrange("p (j t) -> p j t", j=2),
                                             lg[:, 56 + hd:57 + hd], None, ALU.mult))
                        V.scalar_tensor_tensor(out=dec[:, hd, :, :], in0=tabR[:, T_BEHIND:T_BEHIND + 512].rearrange("p (j t) -> p j t", j=2),
                                               scalar=lg[:, 60 + hd:61 + hd], in1=drow, op0=ALU.mult,
                                               op1=ALU.add).then_inc(S[l, "d_pre"], 1)
                        dve.wait_ge(S[l, "d_pre"], hd + 1)

                    def scored(hd):
                        dve.wait_ge(S[l, "s_mm"], hd + 1)
                        dve.wait_ge(S[l, "d_e"], hd + 1)
                        if hd >= 2:
                            dve.wait_ge(S[l, "y_mm"], hd - 1)
                        V.scalar_tensor_tensor(out=wt[hd % 2], in0=ps[6 + hd % 2][:, :].rearrange("p (j t) -> p j t", j=2),
                                               scalar=float(RQK) ** -0.5, in1=dec[:, hd, :, :], op0=ALU.mult,
                                               op1=ALU.mult).then_inc(S[l, "s_w"], 1)

                    for q in range(RET_GROUPS):
                        splitn(n0 + 2 * q + 2)
                        if q < 4:
                            dve.wait_ge(tab_in, 80)
                            dve.wait_ge(S[l, "qk_raw"], 2 * q + 1)
                            if q >= 1:
                                dve.wait_ge(S[l, "qk_t"], 2 * q)
                            V.tensor_tensor(rA[:, 0, :].rearrange("p (h d) -> p h d", h=2), rraw[:, 0, :].rearrange("p (h d) -> p h d", h=2),
                                            tabR[:, T_COSR:T_COSR + 256].unsqueeze(1).to_broadcast([P, 2, 256]), ALU.mult)
                            s5 = rraw[:, 0, :].rearrange("p (h r d) -> p h r d", h=4, r=2)
                            o5 = rB[:, 0, :].rearrange("p (h r d) -> p h r d", h=4, r=2)
                            sn = tabR[:, T_SINR:T_SINR + 256].rearrange("p (a r d) -> p a r d", a=2, r=2)
                            for hd in range(2):
                                for r_ in range(2):
                                    ins = V.tensor_tensor(o5[:, 2 * hd:2 * hd + 2, r_, :], s5[:, 2 * hd:2 * hd + 2, 1 - r_, :],
                                                          sn[:, :, r_, :], ALU.mult)
                            link(ins)
                            V.tensor_tensor(rA[:, 0, :], rA[:, 0, :], rB[:, 0, :], ALU.add).then_inc(S[l, "r0"], 1)
                        elif q % 2 == 0:
                            scored((q - 4) // 2)
                        if q >= 4 and q % 2:
                            hd = (q - 4) // 2
                            dve.wait_ge(S[l, "y_sq"], 2 * hd + 2)
                            link(V.tensor_scalar(rs[:, 104:106], sq[:, 32:34], 1.0 / RV, EPS, ALU.mult, ALU.add))
                            rsqrt(rs[:, 106:108], rs[:, 104:106], rs[:, 108:110])
                            dve.wait_ge(S[l, "g_in"], 2 * hd + 2)
                            for j in range(TT):
                                V.scalar_tensor_tensor(out=vr[:, j, RV * hd:RV * hd + RV], in0=ps[4 + j][:, :], scalar=rs[:, 106 + j:107 + j],
                                                       in1=sg[:, j, RV * hd:RV * hd + RV], op0=ALU.mult, op1=ALU.mult).then_inc(S[l, "y_g"], 1)
                            dve.wait_ge(S[l, "y_g"], 2 * hd + 2)
                        if q < RET_GROUPS - 1:
                            splitn(n0 + 2 * q + 3)
                        if q == 0:
                            one_minus()
                        elif q == 2:
                            log_gamma()
                        if 2 <= q < 4:
                            decay(2 * q - 4)
                            decay(2 * q - 3)
                    for u in range(RET_OUT_UNITS):
                        dve.wait_ge(S[l, "y_hi"], u + 1)
                        V.tensor_tensor(feat[:, 16 + 2 * u:18 + 2 * u, :], ps[4 + (u + 2) % 4][:, :].rearrange("p (a t) -> p a t", a=2),
                                        feat[:, 2 * u:2 * u + 2, :].bitcast(F32), ALU.subtract).then_inc(S[l, "y_lo"], 1)
                        if u < RET_OUT_UNITS - 1:
                            splitn(n0 + 2 * RET_GROUPS + u + 1)
                    turn(s)

                s += 1
                n0 = FIRST_UNIT[s]
                q0 = n0 // 2

                def square(st, b, static):
                    dve.wait_ge(S[l, "relu"], st + 1)
                    if not static or st >= 1:
                        dve.wait_ge(S[l, "a_lo"], st)
                    V.tensor_tensor(aa, rl[b], rl[b], ALU.mult).then_inc(S[l, "sqr"], 1)
                    dve.wait_ge(S[l, "sqr"], st + 1)
                    dve.wait_ge(S[l, "a_hi"], st + 1)
                    V.tensor_tensor(feat[:, 4 * b + 2:4 * b + 4, :], aa.rearrange("p (a t) -> p a t", a=2),
                                    feat[:, 4 * b:4 * b + 2, :].bitcast(F32), ALU.subtract).then_inc(S[l, "a_lo"], 1)

                square(0, 0, True)
                splitn(n0 + 2)
                square(1, 1, True)
                splitn(n0 + 3)
                with dve.Fori(0, MLP_STEPS // 2 - 1) as it:
                    for b in range(2):
                        q = q0 + 1 + it * 2 + b
                        split(q + 1, 0)
                        square(it * 2 + 2 + b, b, False)
                        split(q + 1, 1)
                turn(s)

        @block.tensor
        def _(pe):
            mm = nc.tensor.matmul
            TP = nc.tensor.transpose

            def token_major(q, par_, lhs_hi, lhs_lo, banks, first, k0, nk, width):
                cn = width // 512
                for hf in range(2):
                    slot = 2 * par_ + hf
                    pe.wait_ge(lo_done, 4 * q + 2 * par_ + hf + 1)
                    for j in range(TT):
                        for k in range(nk):
                            kk = k0 + hf * nk + k
                            tk = slice(j * P, (j + 1) * P)
                            st = first and hf == 0 and k == 0
                            for c in range(cn):
                                cs = slice(k * width + 512 * c, k * width + 512 * c + 512)
                                o = ps[banks[j * cn + c]][:, :]
                                mm(o, lhs_hi(kk)[:, tk], whi[:, slot, cs], start=st, stop=False, skip_group_check=True)
                                ins = mm(o, lhs_hi(kk)[:, tk], wlo[:, slot, cs], start=False, stop=False, skip_group_check=True)
                            for c in range(cn):
                                cs = slice(k * width + 512 * c, k * width + 512 * c + 512)
                                ins = mm(ps[banks[j * cn + c]][:, :], lhs_lo(kk)[:, tk], whi[:, slot, cs],
                                         start=False, stop=True, skip_group_check=True)
                    ins.then_inc(w_used, 1)

            def feature_major(q, par_, bank):
                for hf in range(2):
                    slot = 2 * par_ + hf
                    pe.wait_ge(lo_done, 4 * q + 2 * par_ + hf + 1)
                    for f in range(2):
                        o = ps[bank][:, f * SEQ:(f + 1) * SEQ]
                        for k in range(4):
                            ws = slice(k * 256 + f * P, k * 256 + f * P + P)
                            kk = 4 * hf + k
                            mm(o, whi[:, slot, ws], feat[:, HT_HI + kk, :], start=(hf == 0 and f == 0 and k == 0), stop=False, skip_group_check=True)
                            mm(o, whi[:, slot, ws], feat[:, HT_LO + kk, :], start=False, stop=False, skip_group_check=True)
                            ins = mm(o, wlo[:, slot, ws], feat[:, HT_HI + kk, :], start=False, stop=True, skip_group_check=True)
                    ins.then_inc(w_used, 1)

            ht = (lambda k: feat[:, HT_HI + k, :]), (lambda k: feat[:, HT_LO + k, :])

            def turned(s, j):
                pe.wait_ge(h_done, 2 * s + j + 1)
                for c in range(2):
                    for k in range(4):
                        ins = TP(ps[4 + 2 * j + c][:, k * P:(k + 1) * P], h[:, j, (4 * c + k) * P:(4 * c + k + 1) * P], ident)
                    ins.then_inc(h_t, 1)

            def awake(bank, n):
                for _ in range(n):
                    mm(ps[bank][:, :], ident, cst[:, 0:512], start=True, stop=True, skip_group_check=True)

            def head_part(n, j):
                for hf in range(2):
                    m = 2 * n + hf
                    slot = m % 4
                    if j == 0:
                        pe.wait_ge(lo_done, m + 1)
                    tk = slice(j * P, (j + 1) * P)
                    for k in range(2):
                        cs, kk = slice(512 * k, 512 * k + 512), 4 * (n % 2) + 2 * hf + k
                        o = ps[j][:, :]
                        mm(o, feat[:, HT_HI + kk, tk], whi[:, slot, cs], start=(kk == 0), stop=False, skip_group_check=True)
                        mm(o, feat[:, HT_HI + kk, tk], wlo[:, slot, cs], start=False, stop=False, skip_group_check=True)
                        ins = mm(o, feat[:, HT_LO + kk, tk], whi[:, slot, cs], start=False, stop=True, skip_group_check=True)
                    if j == 1:
                        ins.then_inc(w_used, 1)

            def columns():
                pe.wait_ge(rows_in, 16 * 8)
                for i in range(2):
                    TP(ps[0][:, 256 * i:256 * i + 96], view(big, 8192 + 256 * i, P)[0:96, :], ident[0:96, 0:96])
                    ins = TP(ps[0][:, 256 * i + 128:256 * i + 240], view(big, 8320 + 256 * i, P)[0:112, :], ident[0:112, 0:112])
                ins.then_inc(set_t, 1)

            def head(s, feature):
                n = FIRST_UNIT[s]
                if s > 0 and s % 2 == 0:
                    awake(7, 1)
                turned(s, 0)
                if feature:
                    if s > 0:
                        awake(0, 4)
                    turned(s, 1)
                    if s == 0:
                        awake(1, 5)
                    pe.wait_ge(h_lo, 4 * s + 4)
                    feature_major(n // 2, 0, 4)
                    if s == 0:
                        columns()
                    feature_major(n // 2, 1, 5)
                else:
                    pe.wait_ge(h_lo, 4 * s + 2)
                    head_part(n, 0)
                    turned(s, 1)
                    head_part(n + 1, 0)
                    pe.wait_ge(h_lo, 4 * s + 4)
                    head_part(n, 1)
                    head_part(n + 1, 1)

            def tail(n, lhs_hi, lhs_lo, k0, ready, count):
                for j in range(TT):
                    tk = slice(j * P, (j + 1) * P)
                    for k in range(4):
                        if j == 0 and k == 2:
                            pe.wait_ge(ready, count)
                        if j == 0:
                            pe.wait_ge(lo_done, 2 * n + k + 1)
                        for c in range(2):
                            cs = slice(512 * c, 512 * c + 512)
                            mm(ps[2 * j + c][:, :], lhs_hi(k0 + k)[:, tk], whi[:, k, cs], start=False, stop=False, skip_group_check=True)
                            mm(ps[2 * j + c][:, :], lhs_hi(k0 + k)[:, tk], wlo[:, k, cs], start=False, stop=False, skip_group_check=True)
                        for c in range(2):
                            ins = mm(ps[2 * j + c][:, :], lhs_lo(k0 + k)[:, tk], whi[:, k, 512 * c:512 * c + 512],
                                     start=False, stop=True, skip_group_check=True)
                        if j == 1:
                            ins.then_inc(w_used, 1)
                    if j == 0:
                        ins.then_inc(acc0, 1)

            def project(s, n, units, lhs_hi, lhs_lo, ready, per, behind_first=None):
                for u in range(units - 2):
                    pe.wait_ge(ready, per * (u + 1))
                    token_major((n + u) // 2, (n + u) % 2, lhs_hi, lhs_lo, (0, 1, 2, 3), u == 0, 2 * u, 1, D_MODEL)
                    if u == 0 and behind_first:
                        behind_first()
                pe.wait_ge(ready, per * (units - 1))
                tail(n + units - 2, lhs_hi, lhs_lo, 2 * units - 4, ready, per * units)

            pe.wait_ge(const_in, 16)
            head(0, True)

            for l in range(DEPTH):
                kind, s, n0 = l % 3, 2 * l, FIRST_UNIT[2 * l]
                i = l // 3
                if s > 0:
                    head(s, kind == 0)
                if kind == 0:
                    def x_transposes(u):
                        pe.wait_ge(S[l, "conv_y"], 2 * u + 2)
                        if u >= 2:
                            pe.wait_ge(S[l, "x_tok"], u - 1)
                        for j in range(TT):
                            for cc in range(2):
                                ins = TP(ps[6 + u % 2][:, 256 * j + P * cc:256 * j + P * cc + P], xc[u % 4][:, cc, j * P:(j + 1) * P], ident)
                        ins.then_inc(S[l, "x_t"], 1)

                    for u in range(2, XBC_UNITS):
                        pe.wait_ge(S[l, "conv_in"], u - 1)
                        feature_major((n0 + u) // 2, (n0 + u) % 2, 4 + u % 2)
                        if u == 4:
                            pe.wait_ge(set_lo, 2)
                            o = ps[3][0:64, 0:SEQ]
                            for k in range(KD):
                                ks = slice(64 * k, 64 * k + 64)
                                mm(o, wdt_hi[:, i, ks], feat[:, HT_HI + k, :], start=(k == 0), stop=False)
                                mm(o, wdt_hi[:, i, ks], feat[:, HT_LO + k, :], start=False, stop=False)
                                ins = mm(o, wdt_lo[:, i, ks], feat[:, HT_HI + k, :], start=False, stop=(k == KD - 1))
                            ins.then_inc(S[l, "dt_mm"], 1)
                        if u == 6:
                            pe.wait_ge(S[l, "dt_mm"], 2)
                            for j in range(TT):
                                ins = TP(ps[2][:, 64 * j:64 * j + 64], dt_feat[0:64, j * P:(j + 1) * P], ident[0:64, 0:64])
                            ins.then_inc(S[l, "dt_mm"], 1)
                        if u < 10:
                            x_transposes(u - 2)
                    dAv = dts[:, 1, :].rearrange("p (j d h) -> p j d h", j=2, d=2)
                    pe.wait_ge(S[l, "dt_ok"], 2)
                    pe.wait_ge(S[l, "x_tok"], 8)
                    for b, (m, j, fb) in enumerate(((fromon, 0, 1), (upto, 1, 0), (after, 0, 0), (before, 1, 1))):
                        ins = mm(ps[7][:, 32 * b:32 * b + 32], m, dAv[:, j, fb, :], start=True, stop=True)
                    ins.then_inc(S[l, "pre_mm"], 1)
                    for u in range(Z_UNITS):
                        n = n0 + XBC_UNITS + u
                        if u >= 4:
                            pe.wait_ge(S[l, "z_ok"], 2 * (u // 2 - 1))
                        token_major(n // 2, n % 2, *ht, (2 * (u // 2 % 2), 2 * (u // 2 % 2) + 1), u % 2 == 0, 4 * (u % 2), 2, 512)

                    def seg(g):
                        if g == 0:
                            pe.wait_ge(S[l, "conv_y"], 2 * XBC_UNITS)
                        else:
                            pe.wait_ge(S[l, "cb_ok"], 3 * g)
                        for a in range(2):
                            for j in range(TT):
                                src = j if a == 0 else 1 - j
                                ins = mm(ps[4][:, 256 * a + P * j:256 * a + P * j + P], BT[:, g, src * P:(src + 1) * P],
                                         CT[:, g, j * P:(j + 1) * P], start=True, stop=True)
                        ins.then_inc(S[l, "cb_mm"], 1)
                        for j in range(TT):
                            pe.wait_ge(S[l, "mff_ok"], 2 * g + j + 1)
                            pe.wait_ge(S[l, "mfb_ok"], 2 * g + j + 1)
                            if g >= 1:
                                pe.wait_ge(S[l, "seg_e"], 2 * (g - 1) + j + 1)
                            mm(ps[5 + j][:, :], after, MF[0][:, j, :], start=True, stop=False)
                            mm(ps[5 + j][:, :], before, MF[1][:, j, :], start=False, stop=True).then_inc(S[l, "seg_mm"], 1)

                    def y_transposes(g):
                        pe.wait_ge(S[l, "y_g"], g + 1)
                        if g >= 1:
                            pe.wait_ge(S[l, "y_lo"], 2 * g)
                        else:
                            pe.wait_ge(S[l, "pre_e"], 1)
                        for kk in range(2):
                            for j in range(TT):
                                ins = TP(ps[7][:, 256 * kk + P * j:256 * kk + P * j + P], YT[2][:, j, P * kk:P * kk + P], ident)
                        ins.then_inc(S[l, "y_t"], 1)

                    seg(0)
                    for g in range(SSM_GROUPS):
                        if g + 1 < SSM_GROUPS:
                            seg(g + 1)
                        pe.wait_ge(S[l, "xs_ok"], g + 1)
                        pe.wait_ge(S[l, "cb_ok"], 3 * g + 3)
                        if g >= 2:
                            pe.wait_ge(S[l, "y_v"], g - 1)
                        if g == 0:
                            pe.wait_ge(S[l, "z_ok"], 8)
                        for j in range(TT):
                            mm(ps[g % 2][:, 256 * j:256 * j + 256], CBX[g % 2][:, j, :], XS[g % 2][:, 1 - j, :], start=True, stop=True)
                        pe.wait_ge(S[l, "w_ok"], 2 * g + 2)
                        for j in range(TT):
                            for hd in range(HPG):
                                c = 256 * g + SSM_HDIM * hd
                                ins = mm(ps[2 + g % 2][:, 256 * j + SSM_HDIM * hd:256 * j + SSM_HDIM * (hd + 1)],
                                         WM[g % 2][:, j, P * hd:P * hd + P], xtok[:, j, c:c + SSM_HDIM], start=True, stop=True)
                        ins.then_inc(S[l, "y_mm"], 1)
                        if g >= 1:
                            y_transposes(g - 1)
                    pe.wait_ge(S[l, "y_v"], SSM_GROUPS)
                    project(s, n0 + XBC_UNITS + Z_UNITS, SSM_OUT_UNITS, lambda k: feat[:, k, :], lambda k: feat[:, 16 + k, :],
                            S[l, "y_lo"], 2, lambda: y_transposes(SSM_GROUPS - 1))
                elif kind == 1:
                    for u in range(2, 2 * ATT_GROUPS):
                        token_major((n0 + u) // 2, (n0 + u) % 2, *ht, (2 * (u // 2), 2 * (u // 2) + 1), u % 2 == 0, 4 * (u % 2), 2, 512)
                    def pair_transposes(c):
                        hd = ATT_PAIRS[c]
                        if c >= 2:
                            pe.wait_ge(S[l, "qk_in"], c - 1)
                        pe.wait_ge(S[l, "r0"], (c + 1) // 2 + 1)
                        pe.wait_ge(S[l, "r1"], (c + 1) // 2 + 1)
                        for b in range(2):
                            for j in range(TT):
                                ins = TP(ps[6 + c % 2][:, 256 * b + P * j:256 * b + P * j + P], qkv[:, j, P * (hd + b):P * (hd + b + 1)], ident)
                        ins.then_inc(S[l, "qk_t"], 1)

                    def scores(hd):
                        pe.wait_ge(S[l, "qk_in"], 2 + hd // 2)
                        if hd == 0:
                            pe.wait_ge(S[l, "qn_root"], 2)
                        if hd >= 2:
                            pe.wait_ge(S[l, "s_e"], 2 * (hd - 1))
                        for j in range(TT):
                            ins = mm(ps[hd % 2][:, j * SEQ:(j + 1) * SEQ], qkT[:, hd, j * P:(j + 1) * P], qkT[:, AQ + hd // 4, :],
                                     start=True, stop=True)
                        ins.then_inc(S[l, "s_mm"], 1)

                    pair_transposes(0)
                    pair_transposes(1)
                    scores(0)
                    scores(1)
                    for c in range(2, 5):
                        pair_transposes(c)
                    for t in range(AQ + 1):
                        if t < AQ:
                            pe.wait_ge(S[l, "p_ok"], 2 * t + 2)
                            if t >= 2:
                                pe.wait_ge(S[l, "p_in"], t - 1)
                            for b in range(2):
                                for j in range(TT):
                                    ins = TP(ps[2 + t % 2][:, 256 * b + P * j:256 * b + P * j + P], prob[t % 2][:, j, P * b:P * b + P], ident)
                            ins.then_inc(S[l, "p_t"], 1)
                        if t + 2 < AQ:
                            scores(t + 2)
                        if t >= 1:
                            hd = t - 1
                            pe.wait_ge(S[l, "p_in"], hd + 1)
                            if hd == 0:
                                pe.wait_ge(S[l, "qn_root"], 3)
                            if hd >= 2:
                                pe.wait_ge(S[l, "o_lo"], hd - 1)
                            vo = AQ * AD + AKV * AD + AD * (hd // 4)
                            for b in range(2):
                                ins = mm(ps[4 + hd % 2][:, 0:SEQ], qkv[:, b, vo:vo + AD], probT[hd % 2][:, b, :], start=(b == 0), stop=(b == 1))
                            ins.then_inc(S[l, "o_mm"], 1)
                    project(s, n0 + 2 * ATT_GROUPS, ATT_OUT_UNITS, lambda k: feat[:, k, :], lambda k: feat[:, 8 + k, :], S[l, "o_lo"], 2)
                else:
                    def rope_transposes(q):
                        pe.wait_ge(S[l, "r0"], q + 1)
                        pe.wait_ge(S[l, "r1"], q + 1)
                        for b in range(2):
                            if q >= 1:
                                pe.wait_ge(S[l, "qk_in"], 2 * q - 1 + b)
                            for a in range(2):
                                for j in range(TT):
                                    c = P * (2 * b + a)
                                    ins = TP(ps[4 + b][:, 256 * a + P * j:256 * a + P * j + P], rA[:, j, c:c + P], ident)
                            ins.then_inc(S[l, "qk_t"], 1)

                    def scores(hd):
                        if hd >= 2:
                            pe.wait_ge(S[l, "s_w"], hd - 1)
                        for b in range(TT):
                            for k in range(2):
                                ins = mm(ps[6 + hd % 2][:, b * SEQ:(b + 1) * SEQ], rT[:, 8 + 2 * hd + k, b * P:(b + 1) * P], rT[:, 2 * hd + k, :],
                                         start=(k == 0), stop=(k == 1))
                        ins.then_inc(S[l, "s_mm"], 1)

                    def y_head(hd):
                        pe.wait_ge(S[l, "s_w"], hd + 1)
                        pe.wait_ge(S[l, "v_in"], 2 * hd + 2)
                        if hd == 0:
                            pe.wait_ge(S[l, "qk_in"], 8)
                        else:
                            pe.wait_ge(S[l, "y_g"], 2 * hd)
                        for j in range(TT):
                            for b in range(TT):
                                ins = mm(ps[4 + j][:, :], wt[hd % 2][:, b, j * P:(j + 1) * P], vr[:, b, RV * hd:RV * hd + RV],
                                         start=(b == 0), stop=(b == 1))
                        ins.then_inc(S[l, "y_mm"], 1)

                    for q in range(RET_GROUPS):
                        for hf in range(2):
                            n = n0 + 2 * q + hf
                            if q >= 2 and hf == 0:
                                if q < 6:
                                    pe.wait_ge(S[l, "qk_raw"], 2 * (q - 1))
                                elif q % 2 == 0:
                                    pe.wait_ge(S[l, "v_in"], 2 * ((q - 6) // 2 + 1))
                                else:
                                    pe.wait_ge(S[l, "g_in"], 2 * ((q - 6) // 2 + 1))
                            if q >= 1:
                                token_major(n // 2, n % 2, *ht, (2 * (q % 2), 2 * (q % 2) + 1), hf == 0, 4 * hf, 2, 512)
                            if hf == 0 and 1 <= q <= 4:
                                rope_transposes(q - 1)
                            if hf == 0 and q >= 5 and q % 2:
                                y_head((q - 5) // 2)
                            if hf == 1 and q >= 4 and q % 2 == 0:
                                if q == 4:
                                    pe.wait_ge(S[l, "qk_in"], 8)
                                scores((q - 4) // 2)

                    def y_transposes(u):
                        pe.wait_ge(S[l, "y_g"], 2 * (u // 2) + 2)
                        if u in (2, 3):
                            pe.wait_ge(S[l, "y_g"], 8)
                        if u >= 4:
                            pe.wait_ge(S[l, "y_lo"], u - 3)
                        for a in range(2):
                            for j in range(TT):
                                c = P * (2 * u + a)
                                ins = TP(ps[4 + (u + 2) % 4][:, 256 * a + P * j:256 * a + P * j + P], vr[:, j, c:c + P], ident)
                        ins.then_inc(S[l, "y_t"], 1)

                    for u in range(2):
                        y_transposes(u)
                    pe.wait_ge(S[l, "g_in"], 8)
                    for u in range(RET_OUT_UNITS - 2):
                        pe.wait_ge(S[l, "y_lo"], u + 1)
                        n = n0 + 2 * RET_GROUPS + u
                        token_major(n // 2, n % 2, lambda k: feat[:, k, :], lambda k: feat[:, 16 + k, :], (0, 1, 2, 3), u == 0, 2 * u, 1,
                                    D_MODEL)
                        y_transposes(u + 2)
                    pe.wait_ge(S[l, "y_lo"], RET_OUT_UNITS - 1)
                    tail(n0 + 2 * RET_GROUPS + RET_OUT_UNITS - 2, lambda k: feat[:, k, :], lambda k: feat[:, 16 + k, :], 2 * RET_OUT_UNITS - 4,
                         S[l, "y_lo"], RET_OUT_UNITS)

                s += 1
                n0 = FIRST_UNIT[s]
                q0 = n0 // 2
                head(s, True)

                def up(st, b, q, par_, static):
                    if not static or st >= 2:
                        pe.wait_ge(S[l, "relu"], st - 1)
                    feature_major(q, par_, 4 + b)

                def down(st, b, q, par_, first):
                    pe.wait_ge(S[l, "a_lo"], st + 1)
                    token_major(q, par_, lambda k: feat[:, 4 * b + k, :], lambda k: feat[:, 4 * b + 2 + k, :], (0, 1, 2, 3), first, 0, 1,
                                D_MODEL)

                down(0, 0, q0 + 1, 0, True)
                up(2, 0, q0 + 1, 1, True)
                with pe.Fori(0, MLP_STEPS // 2 - 2) as it:
                    for b in range(2):
                        t = it * 2 + 1 + b
                        down(t, 1 - b, q0 + 1 + t, 0, False)
                        up(t + 2, 1 - b, q0 + 1 + t, 1, False)
                down(MLP_STEPS - 3, 1, q0 + MLP_STEPS - 2, 0, False)
                up(MLP_STEPS - 1, 1, q0 + MLP_STEPS - 2, 1, True)
                pe.wait_ge(S[l, "a_lo"], MLP_STEPS - 1)
                tail(n0 + MLP_UNITS - 2, lambda k: feat[:, k + 2 * (k // 2), :], lambda k: feat[:, 2 + k + 2 * (k // 2), :], 0,
                     S[l, "a_lo"], MLP_STEPS)


_INS = ["x", "norm_mix_pre", "norm_mix_post", "norm_ffn_pre", "norm_ffn_post", "mlp_w_in", "mlp_w_out",
        "ssm_w_in", "ssm_conv_w", "ssm_conv_b", "ssm_dt_bias", "ssm_a_log", "ssm_d", "ssm_norm", "ssm_w_out",
        "att_w_in", "att_q_norm", "att_k_norm", "att_w_out", "ret_w_in", "ret_log2_decay", "ret_w_out"]


def kernel(**inputs):
    import concourse.bacc as _bacc
    from concourse.bass_utils import run_bass_kernel_spmd as _run

    nc = _bacc.Bacc("TRN2", target_bir_lowering=False, num_devices=1)
    arrays, aps = {}, {}
    for name in _INS:
        a = np.ascontiguousarray(inputs[name])
        arrays[f"in_{name}"] = a
        aps[name] = nc.dram_tensor(f"in_{name}", a.shape, F32, kind="ExternalInput").ap()
    extra = []
    for name, a in zip(("consts", "tab_a", "tab_r"), shape_constants()):
        arrays[f"in_{name}"] = a
        extra.append(nc.dram_tensor(f"in_{name}", a.shape, F32, kind="ExternalInput").ap())
    out = nc.dram_tensor("out_x", (1, SEQ, D_MODEL), F32, kind="ExternalOutput").ap()
    build(nc, aps, *extra, out)
    r = _run(nc, [arrays], core_ids=[0])
    return r.results[0]["out_x"]
```
